# Optimizing a Trainium2 kernel written in Bass

```python
import math, functools
import jax, jax.numpy as jnp
from jax import lax
import numpy as np

D_MODEL = 1024
BATCH = 1
SEQ = 512
DEPTH = 2
DEC_BATCH = 8
DEC_SEQ = 4
PAST_LEN = 256
PAGE_SIZE = 128

N_A = DEPTH // 2
N_B = DEPTH - N_A
MEM_LEN = 256
MEM_HEADS = 4
MEM_W = D_MODEL // 4
MEM_HD = MEM_W // MEM_HEADS
C_A = D_MODEL - MEM_W
CONV_A_WIDTH = 31
DIFF_HD = 64
DIFF_VD = 2 * DIFF_HD
DIFF_HEADS = (D_MODEL - MEM_W) // DIFF_VD
DIFF_QW = DIFF_HEADS * 2 * DIFF_HD
DIFF_KVW = DIFF_HEADS * DIFF_VD
FFN_CONV_WIDTH = 3
D_FF = ((8 * D_MODEL // 3 + 255) // 256) * 256
Q_BLOCK = 128
EPS = 1e-6
LN_EPS = 1e-5
NEG_INF = -1e30

kernel_name = 'yoco_conformer_diffattn_memxattn_step'

def _rms(x, g):
    xf = x.astype(jnp.float32)
    y = xf * lax.rsqrt(jnp.mean(xf * xf, axis=-1, keepdims=True) + EPS)
    return (y * g.astype(jnp.float32)).astype(x.dtype)

def _layernorm(x, g, b):
    xf = x.astype(jnp.float32)
    xc = xf - jnp.mean(xf, axis=-1, keepdims=True)
    var = jnp.mean(xc * xc, axis=-1, keepdims=True)
    y = xc * lax.rsqrt(var + LN_EPS) * g.astype(jnp.float32) + b.astype(jnp.float32)
    return y.astype(x.dtype)

def _causal_dwconv(x, prev, w, b):
    ext = jnp.concatenate([prev.astype(x.dtype), x], axis=1)
    y = lax.conv_general_dilated(ext, w[:, None, :].astype(x.dtype), (1,), 'VALID',
                                 dimension_numbers=('NWC', 'WIO', 'NWC'),
                                 feature_group_count=x.shape[-1])
    return y + b, ext[:, ext.shape[1] - (w.shape[0] - 1):]

def _mem_kv(mem, g, w, k_g):
    b, m, _ = mem.shape
    k, v = jnp.split(_rms(mem, g) @ w, 2, axis=-1)
    k = _rms(k.reshape(b, m, MEM_HEADS, MEM_HD), k_g)
    return k, v.reshape(b, m, MEM_HEADS, MEM_HD)

def _mem_attend(q, k, v):
    s = jnp.einsum('bthd,bmhd->bhtm', q, k).astype(jnp.float32) * (MEM_HD ** -0.5)
    p = jax.nn.softmax(s, axis=-1).astype(v.dtype)
    o = jnp.einsum('bhtm,bmhd->bthd', p, v)
    return o.reshape(q.shape[0], q.shape[1], MEM_W)

def _shared_kv(x, g, w, k_g):
    b, t, _ = x.shape
    k, v = jnp.split(_rms(x, g) @ w, [DIFF_QW], axis=-1)
    k = _rms(k.reshape(b, t, DIFF_HEADS, 2, DIFF_HD), k_g).reshape(b, t, DIFF_HEADS, DIFF_VD)
    return k, v.reshape(b, t, DIFF_HEADS, DIFF_VD)

def _lambda(lams, lam_init):
    lf = lams.astype(jnp.float32)
    return jnp.exp(jnp.sum(lf[0] * lf[1])) - jnp.exp(jnp.sum(lf[2] * lf[3])) + lam_init

def _diff_core(q, k, v, mask, lam):
    s = jnp.einsum('bqhcd,bkhcd->bhcqk', q, k).astype(jnp.float32) * (DIFF_HD ** -0.5)
    p = jax.nn.softmax(jnp.where(mask, s, NEG_INF), axis=-1)
    a = (p[:, :, 0] - lam * p[:, :, 1]).astype(v.dtype)
    return jnp.einsum('bhqk,bkhe->bqhe', a, v)

def _prompt_attend(q, k, v, lam):
    b, s = q.shape[:2]
    nb = s // Q_BLOCK
    kk = k.reshape(b, s, DIFF_HEADS, 2, DIFF_HD)
    qb = jnp.moveaxis(q.reshape(b, nb, Q_BLOCK, DIFF_HEADS, 2, DIFF_HD), 1, 0)
    kpos = jnp.arange(s)

    def block(args):
        q_i, i = args
        qpos = i * Q_BLOCK + jnp.arange(Q_BLOCK)
        return _diff_core(q_i, kk, v, kpos[None, :] <= qpos[:, None], lam)

    o = lax.map(block, (qb, jnp.arange(nb)))
    return jnp.moveaxis(o, 0, 1).reshape(b, s, DIFF_HEADS, DIFF_VD)

def _sample_attend(q, k, v, lam, past_k, past_v):
    b, t = q.shape[:2]
    p_len = past_k.shape[1]
    k_all = jnp.concatenate([past_k.astype(k.dtype), k], axis=1).reshape(b, p_len + t, DIFF_HEADS, 2, DIFF_HD)
    v_all = jnp.concatenate([past_v.astype(v.dtype), v], axis=1)
    qpos = p_len + jnp.arange(t)
    kpos = jnp.arange(p_len + t)
    return _diff_core(q, k_all, v_all, kpos[None, :] <= qpos[:, None], lam)

def _trunk(x, mem_k, mem_v, conv_a_prev, ffn_prev, attend, P):
    b, t, _ = x.shape
    new_conv_a, new_ffn = [], []
    k = v = None
    for l in range(DEPTH):
        h = _rms(x, P['norm_mix'][l])
        if l < N_A:
            a, g, mq = jnp.split(h @ P['w_in_a'][l], [C_A, 2 * C_A], axis=-1)
            c, st = _causal_dwconv(a * jax.nn.sigmoid(g), conv_a_prev[l], P['conv_a_w'][l], P['conv_a_b'][l])
            new_conv_a.append(st)
            c = jax.nn.silu(_layernorm(c, P['ln_a_g'][l], P['ln_a_b'][l]))
            w_out = P['w_out_a'][l]
        else:
            j = l - N_A
            if j == 0:
                k, v = _shared_kv(x, P['norm_kv'], P['w_kv'], P['k_norm'])
            qf, mq = jnp.split(h @ P['w_in_b'][j], [DIFF_QW], axis=-1)
            q = _rms(qf.reshape(b, t, DIFF_HEADS, 2, DIFF_HD), P['q_norm'][j])
            lam_init = 0.8 - 0.6 * math.exp(-0.3 * l)
            o = attend(q, k, v, _lambda(P['lambdas'][j], lam_init))
            c = (_rms(o, P['subln_g'][j]) * (1.0 - lam_init)).reshape(b, t, DIFF_KVW)
            w_out = P['w_out_b'][j]
        mq = _rms(mq.reshape(b, t, MEM_HEADS, MEM_HD), P['mem_q_norm'][l])
        m = _mem_attend(mq, mem_k[l], mem_v[l])
        x = x + jnp.concatenate([c, m], axis=-1) @ w_out
        h = _rms(x, P['norm_ffn'][l])
        gate, val = jnp.split(h @ P['w_up'][l], 2, axis=-1)
        gate, st = _causal_dwconv(gate, ffn_prev[l], P['ffn_conv_w'][l], P['ffn_conv_b'][l])
        new_ffn.append(st)
        x = x + (jax.nn.gelu(gate) * val) @ P['w_down'][l]
    return x, jnp.stack(new_conv_a), jnp.stack(new_ffn), k, v

def setup_inputs(seed: int = 0) -> dict:
    key = jax.random.key(seed)
    ks = iter(jax.random.split(key, 48))

    def nrm(shape, scale=1.0):
        return jax.random.normal(next(ks), shape, jnp.float32) * scale

    def gain(shape):
        return 1.0 + nrm(shape, 0.02)

    n_pages = PAST_LEN // PAGE_SIZE
    n_used = DEC_BATCH * n_pages
    n_phys = n_used + (n_used + 3) // 4
    page_table = jax.random.permutation(next(ks), n_phys)[:n_used].reshape(DEC_BATCH, n_pages).astype(jnp.int32)
    return {
        'x_prompt': nrm((BATCH, SEQ, D_MODEL)),
        'x_sample': nrm((DEC_BATCH, DEC_SEQ, D_MODEL)),
        'mem_prompt': nrm((BATCH, MEM_LEN, D_MODEL)),
        'cache_mem_k': nrm((DEPTH, DEC_BATCH, MEM_LEN, MEM_HEADS, MEM_HD)),
        'cache_mem_v': nrm((DEPTH, DEC_BATCH, MEM_LEN, MEM_HEADS, MEM_HD)),
        'state_conv_a': nrm((N_A, DEC_BATCH, CONV_A_WIDTH - 1, C_A), 0.5),
        'state_ffn_conv': nrm((DEPTH, DEC_BATCH, FFN_CONV_WIDTH - 1, D_FF)),
        'cache_k': nrm((n_phys, PAGE_SIZE, DIFF_HEADS, DIFF_VD)),
        'cache_v': nrm((n_phys, PAGE_SIZE, DIFF_HEADS, DIFF_VD)),
        'page_table': page_table,
        'norm_mix': gain((DEPTH, D_MODEL)),
        'norm_ffn': gain((DEPTH, D_MODEL)),
        'norm_mem': gain((DEPTH, D_MODEL)),
        'w_mem_kv': nrm((DEPTH, D_MODEL, 2 * MEM_W), D_MODEL ** -0.5),
        'mem_q_norm': gain((DEPTH, MEM_HD)),
        'mem_k_norm': gain((DEPTH, MEM_HD)),
        'w_in_a': nrm((N_A, D_MODEL, 2 * C_A + MEM_W), D_MODEL ** -0.5),
        'conv_a_w': nrm((N_A, CONV_A_WIDTH, C_A), CONV_A_WIDTH ** -0.5),
        'conv_a_b': nrm((N_A, C_A), 0.01),
        'ln_a_g': gain((N_A, C_A)),
        'ln_a_b': nrm((N_A, C_A), 0.01),
        'w_out_a': nrm((N_A, C_A + MEM_W, D_MODEL), (C_A + MEM_W) ** -0.5),
        'norm_kv': gain((D_MODEL,)),
        'w_kv': nrm((D_MODEL, DIFF_QW + DIFF_KVW), D_MODEL ** -0.5),
        'k_norm': gain((2, DIFF_HD)),
        'w_in_b': nrm((N_B, D_MODEL, DIFF_QW + MEM_W), D_MODEL ** -0.5),
        'q_norm': gain((N_B, 2, DIFF_HD)),
        'lambdas': nrm((N_B, 4, DIFF_HD), 0.1),
        'subln_g': gain((N_B, DIFF_VD)),
        'w_out_b': nrm((N_B, DIFF_KVW + MEM_W, D_MODEL), (DIFF_KVW + MEM_W) ** -0.5),
        'w_up': nrm((DEPTH, D_MODEL, 2 * D_FF), D_MODEL ** -0.5),
        'ffn_conv_w': nrm((DEPTH, FFN_CONV_WIDTH, D_FF), FFN_CONV_WIDTH ** -0.5),
        'ffn_conv_b': nrm((DEPTH, D_FF), 0.01),
        'w_down': nrm((DEPTH, D_FF, D_MODEL), D_FF ** -0.5),
    }

def reference(x_prompt, x_sample, mem_prompt, cache_mem_k, cache_mem_v, state_conv_a, state_ffn_conv,
              cache_k, cache_v, page_table, norm_mix, norm_ffn, norm_mem, w_mem_kv, mem_q_norm, mem_k_norm,
              w_in_a, conv_a_w, conv_a_b, ln_a_g, ln_a_b, w_out_a, norm_kv, w_kv, k_norm, w_in_b, q_norm,
              lambdas, subln_g, w_out_b, w_up, ffn_conv_w, ffn_conv_b, w_down):
    P = {'norm_mix': norm_mix, 'norm_ffn': norm_ffn, 'mem_q_norm': mem_q_norm,
         'w_in_a': w_in_a, 'conv_a_w': conv_a_w, 'conv_a_b': conv_a_b, 'ln_a_g': ln_a_g, 'ln_a_b': ln_a_b,
         'w_out_a': w_out_a, 'norm_kv': norm_kv, 'w_kv': w_kv, 'k_norm': k_norm, 'w_in_b': w_in_b,
         'q_norm': q_norm, 'lambdas': lambdas, 'subln_g': subln_g, 'w_out_b': w_out_b, 'w_up': w_up,
         'ffn_conv_w': ffn_conv_w, 'ffn_conv_b': ffn_conv_b, 'w_down': w_down}

    mk, mv = [], []
    for l in range(DEPTH):
        k_l, v_l = _mem_kv(mem_prompt, norm_mem[l], w_mem_kv[l], mem_k_norm[l])
        mk.append(k_l)
        mv.append(v_l)
    p_mem_k = jnp.stack(mk)
    p_mem_v = jnp.stack(mv)
    b_p = x_prompt.shape[0]
    zeros_a = jnp.zeros((N_A, b_p, CONV_A_WIDTH - 1, C_A), x_prompt.dtype)
    zeros_f = jnp.zeros((DEPTH, b_p, FFN_CONV_WIDTH - 1, D_FF), x_prompt.dtype)
    y_prompt, p_conv_a, p_ffn_conv, p_k, p_v = _trunk(x_prompt, p_mem_k, p_mem_v, zeros_a, zeros_f,
                                                       _prompt_attend, P)

    n_seq, n_pages = page_table.shape
    past_k = cache_k[page_table].reshape(n_seq, n_pages * PAGE_SIZE, DIFF_HEADS, DIFF_VD)
    past_v = cache_v[page_table].reshape(n_seq, n_pages * PAGE_SIZE, DIFF_HEADS, DIFF_VD)
    attend = functools.partial(_sample_attend, past_k=past_k, past_v=past_v)
    y_sample, s_conv_a, s_ffn_conv, s_k, s_v = _trunk(x_sample, cache_mem_k, cache_mem_v, state_conv_a,
                                                       state_ffn_conv, attend, P)
    return (y_prompt, y_sample, p_mem_k, p_mem_v, p_conv_a, p_ffn_conv, p_k, p_v,
            s_conv_a, s_ffn_conv, s_k, s_v)


_drawn_inputs = setup_inputs


def setup_inputs(seed=0):
    import zlib

    import numpy as np

    out = dict(_drawn_inputs(seed))
    spreads = {}
    factors = {'norm_mix': 2.703,
     'norm_mem': 2.883,
     'mem_q_norm': 8.0,
     'mem_k_norm': 2.804,
     'conv_a_b': 3.052,
     'ln_a_g': 3.478,
     'ln_a_b': 6.971,
     'norm_kv': 2.804,
     'k_norm': 2.893,
     'q_norm': 6.732,
     'subln_g': 6.517,
     'ffn_conv_b': 7.707}
    for name, (base, spread) in spreads.items():
        noise = np.random.default_rng([zlib.crc32(name.encode()), seed]).standard_normal(out[name].shape)
        drawn = base * np.exp(spread * noise) if base else spread * noise
        out[name] = __import__('jax').numpy.asarray(drawn.astype(out[name].dtype))
    for name, factor in factors.items():
        out[name] = (out[name] * factor).astype(out[name].dtype)
    return out
```

```python
import math
from contextlib import ExitStack

import concourse.bass as bass
from concourse import mybir

F32 = mybir.dt.float32
F32R = mybir.dt.float32r
I32 = mybir.dt.int32
ALU = mybir.AluOpType
ACT = mybir.ActivationFunctionType
AX = mybir.AxisListType

P = 128
D = 1024
KD = D // P
NPR = 512
DB, DS = 8, 4
NSA = DB * DS
T = NPR + NSA
HT = T // 2
QB = NPR // P
MEM = 256
MB = MEM // P
MH, MHD = 4, 64
MW = MH * MHD
MC = MW // P
CA = D - MW
CC = CA // P
TAPS = 31
CEXT = TAPS - 1 + NPR
SEXT = TAPS - 1 + DS
H = 6
VD = 128
PAST = 256
PAGES = PAST // P
NKEY = PAST + NSA
FF = 2816
FC = FF // P
FTAPS = 3
GEXT = FTAPS - 1 + NPR
GS = FTAPS - 1 + DS
GROUPS = ((0, 8), (8, 8), (16, 6))
EPS, LN_EPS = 1e-6, 1e-5
LAM_INIT = 0.8 - 0.6 * math.exp(-0.3)
ISQ = MHD ** -0.5

S_IN = 0
S_MEM = S_IN + 2 * CC + MC
S_OUT = (S_MEM + 8, S_MEM + 8 + 8 + 68 + 20)
S_FFN = (S_OUT[0] + 8, S_OUT[1] + 8)
S_B = S_FFN[0] + 68
STEPS = S_FFN[1] + 68
UP = tuple(tuple(f + o for o in (0, 24, 48)) for f in S_FFN)
DOWN = tuple(tuple(f + o for o in (16, 40, 60)) for f in S_FFN)

C_ID, C_BLK, C_MASK, C_NEW, C_FOLD = 0, P, 2 * P, 3 * P, 4 * P
C_ALL = C_FOLD + 48


def build(nc, a):
    ctx = ExitStack()
    with ctx:
        def sem(name):
            return ctx.enter_context(nc.semaphore(name))

        cursor = [nc.sbuf_base + 31 & ~31]

        def place(name, shape, dt=F32, at=None):
            size = 4
            for n in shape[1:]:
                size *= n
            size = size + 31 & ~31
            if at is None:
                at = cursor[0]
                cursor[0] += size
            assert at + size <= nc.sbuf_usable_end, (name, at + size)
            h = nc.alloc_sbuf_tensor_at(name, shape, dt, offset=at)
            return h, at + size

        xT, _ = place("x_resid", [P, KD, T])
        regA = cursor[0]
        xa_hi, e = place("xa_hi", [P, KD, T], F32R)
        xa_lo, e = place("xa_lo", [P, KD, T], F32R)
        regB = cursor[0]
        xb_hi, _ = place("xb_hi", [P, KD, T], F32R)
        xb_lo, endB = place("xb_lo", [P, KD, T], F32R)
        wraw, _ = place("w_raw", [P, 4, KD * P])
        whi, _ = place("w_hi", [P, 2, KD * P], F32R)
        wlo, _ = place("w_lo", [P, 2, KD * P], F32R)
        pT, _ = place("params", [P, 512])
        cst, _ = place("consts", [P, C_ALL])
        ones, _ = place("ones", [P, P])
        stT, _ = place("ffn_state", [P, 2 * FC, 2 * DB])
        gcol, _ = place("gate_tail", [P, 2 * DB + 2, FC])
        unew, _ = place("glu_new", [P, CC, NSA], at=cursor[0] - (4 * (2 * DB + 2) * FC + 31 & ~31))
        rstd, _ = place("rstd", [P, T])
        rstdM, _ = place("rstd_mem", [P, MEM])
        apad, _ = place("fold_padded", [P, 2, PAGES, H, NSA], at=cursor[0])
        sqt, _ = place("squares", [P, 2, T])
        orow, _ = place("diff_o_rows", [NSA, CA], at=cursor[0])
        qf, _ = place("tile_raw", [P, 2, T])
        t1, _ = place("turned", [P, T])
        rr, _ = place("root_row", [P, T])
        small, _ = place("small", [P, 3, H * T // 32])
        lamt, _ = place("lam", [P, 8])
        stat, _ = place("softmax_stats", [P, 2, 8])
        ptab, _ = place("page_table_sb", [1, 16], I32)
        w0 = cursor[0]
        gext, _ = place("gate_ext", [P, 2, GEXT + DB * GS])
        gcv, _ = place("gate_conv", [P, T])
        gel, _ = place("gelu", [P, T])
        val, _ = place("value", [P, T])
        prod, endW = place("product", [P, T])
        et, e = place("exps", [P, 2, 512], at=w0)
        anew, _ = place("fold_new", [NSA, H, NSA], at=e + 4 * 384)
        exps, _ = place("sample_exps", [P, NKEY], at=e)
        prb, e = place("probs", [P, 512], at=e)
        pTt, e = place("probs_t", [P, 4, P], at=e)
        kTb, e = place("mem_k_cache_t", [P, 2, MC, MEM], at=e)
        assert e <= endW
        memk, _ = place("mem_k", [P, 2, MC, MEM])
        memv, _ = place("mem_v", [P, 2, MB, MW])
        regC = cursor[0]
        uext, e = place("glu_ext", [P, CC, CEXT + DB * SEXT], at=regC)
        atile, _ = place("glu_a", [P, T], at=w0)
        gtile, _ = place("glu_g", [P, T], at=w0 + 4 * T)
        stile, _ = place("glu_s", [P, T], at=w0 + 8 * T)
        convt, eC = place("conv_out", [P, CC, T], at=e)
        rows, e1 = place("param_rows", [P, 4, P], at=e)
        frow, e1 = place("ffn_state_rows", [2 * 2 * DB, FF], at=e1)
        sprod, _ = place("sample_tap_products", [P, DB, DS, TAPS], at=w0 + 12 * T)
        crow, e2 = place("conv_state_rows", [4 * (TAPS - 1), 2, CA], at=w0 + 12 * T)
        assert e2 <= endW
        e1 = max(e1, eC)
        memT, _ = place("mem_t", [P, KD, MEM], at=e1)
        mT, e2 = place("mem_mix", [P, MC, T], at=e1)
        mq, e2 = place("mem_q", [P, MC, T], at=e2)
        qT, e = place("diff_q", [P, 2, T], at=regC)
        mT2, _ = place("mem_mix_b", [P, MC, T], at=regC)
        qnew, e = place("diff_q_new", [P, H, NSA], at=e)
        kT, e = place("diff_k", [P, H, T], at=e)
        od, e = place("diff_o", [P, H, T], at=e)
        vnat, e = place("diff_v", [P, 2, QB, VD], at=e)
        vnew, e = place("diff_v_new", [NSA, H, VD], at=e)
        mq2, e = place("mem_q_b", [P, MC, T], at=e)
        cs, e = place("fold_scaled", [P, 48], at=e)
        mcache, e = place("mem_cache", [P, DB, MB * MW], at=regA)
        qm, e = place("mem_q_padded", [P, MC, DB * 144], at=e)
        ctail, _ = place("conv_tail", [NSA, 2, CA], at=e)
        qpad, e = place("diff_q_padded", [P, 2, 136 * H], at=e)
        mkn, e = place("mem_k_rows", [P, MB, MW], at=e)
        assert e <= regB
        knat, e = place("k_rows_out", [P, QB, CA], at=regA)
        knsam, e = place("k_rows_sample_out", [NSA, CA], at=e)
        assert e <= regA + 4 * DB * MB * MW
        xnat, e = place("x_rows", [P, 5, D], at=regB)
        mnat, e = place("mem_rows", [P, MB, D], at=e)
        assert e <= endB
        lamin, _ = place("lambdas_in", [P, 4, MHD], at=e)
        mg_hi, mg_lo = [], []
        at = regB
        for l in range(2):
            for part, lst in (("hi", mg_hi), ("lo", mg_lo)):
                h_, at = place(f"mem_g{l}_{part}", [P, KD, MEM], F32R, at=at)
                lst.append(h_)
        kpg, e = place("k_pages", [P, 2, PAGES, CA], at=regB)
        vpg, e = place("v_pages", [P, 2, PAGES, CA], at=e)
        kTs, e = place("k_pages_t", [P, H, NKEY], at=e)
        assert e <= endB
        fout, e = place("ffn_state_out", [P, 5, P], at=regC)
        ynat, e = place("y_rows_out", [P, 2, QB, P], at=e)
        ysam, _ = place("y_sample_out", [NSA, D], at=e)

        acc = [ctx.enter_context(nc.psum_tensor(f"acc{i}", [P, 2, 512], F32)) for i in range(2)]
        psX = ctx.enter_context(nc.psum_tensor("psX", [P, 2, 512], F32))
        psT = ctx.enter_context(nc.psum_tensor("psT", [P, 2, 512], F32))

        ld_const, ld_rows, ld_x, ld_state, ld_mem = (sem(n) for n in (
            "ld_const", "ld_rows", "ld_x", "ld_state", "ld_mem"))
        w_loaded = [sem(f"w_loaded{i}") for i in range(4)]
        w_hi_ready, w_lo_ready = sem("w_hi_ready"), sem("w_lo_ready")
        mm_done = sem("mm_done")
        acc_free = sem("acc_free")
        setup_filled, setup_drained = sem("setup_filled"), sem("setup_drained")
        zeroed = sem("zeroed")
        sq_ready, sq_used = sem("sq_ready"), sem("sq_used")
        turned, var_ready, sd_ready = sem("turned"), sem("var_ready"), sem("sd_ready")
        xg_hi, xg_lo, xb_h, xb_l = sem("xg_hi"), sem("xg_lo"), sem("xb_h"), sem("xb_l")
        mg_h, mg_l = sem("mg_h"), sem("mg_l")
        tile_ev, tile_pe, qk_done = sem("tile_ev"), sem("tile_pe"), sem("qk_done")
        sig_ready, conv_step = sem("sig_ready"), sem("conv_step")
        ln_mean, ln_m, ln_c, ln_n, ln_y, ln_hi = (sem(n) for n in (
            "ln_mean", "ln_m", "ln_c", "ln_n", "ln_y", "ln_hi"))
        cm_hi, cm_lo = sem("cm_hi"), sem("cm_lo")
        ma_S, ma_nb, ma_exp, ma_p, ma_T, ma_aT, ma_pv, ma_o = (sem("ma_" + n) for n in (
            "scores", "max", "exp", "probs", "turned", "copied", "pv", "out"))
        mc_k, mc_v, qm_zero, qm_ready = sem("mc_k"), sem("mc_v"), sem("qm_zero"), sem("qm_ready")
        ms_T, ms_kc, ms_S = sem("ms_turned"), sem("ms_copied"), sem("ms_scores")
        mx_nb, mx_exp, mx_p, mx_T, mx_aT, mx_pv, mx_o = (sem("mx_" + n) for n in (
            "max", "exp", "probs", "turned", "copied", "pv", "out"))
        at_S, at_nb, at_exp, at_p, at_T, at_aT, at_pv, at_O = (sem("at_" + n) for n in (
            "scores", "max", "exp", "probs", "turned", "copied", "pv", "out"))
        kp_ld = [sem(f"kp_ld{i}") for i in range(2)]
        vp_ld = [sem(f"vp_ld{i}") for i in range(2)]
        ld_pt = sem("ld_pt")
        qp_zero, qp_ready, kn_ready = sem("qp_zero"), sem("qp_ready"), sem("kn_ready")
        ds_T, ds_kc, ds_S, ds_nb, ds_exp, ds_p, ds_A, ds_a, ds_pv, ds_row, ds_rc, ds_rT, ds_o = (sem("ds_" + n) for n in (
            "turned", "copied", "scores", "max", "exp", "probs", "folded", "fold_copied", "pv", "rows", "rows_copied",
            "rows_turned", "out"))
        kn_T, kn_c = sem("kn_turned"), sem("kn_copied")
        mk_T, mk_c = sem("mk_turned"), sem("mk_copied")
        ct_T, ct_c = sem("ct_turned"), sem("ct_copied")
        conv_ready, gelu_ready, u_ready, uhi_ready, ulo_ready = (sem(n) for n in (
            "gate_conv_ready", "gelu_ready", "u_ready", "uhi_ready", "ulo_ready"))
        ft_T, ft_c = sem("ft_turned"), sem("ft_copied")
        y_T, y_c = sem("y_turned"), sem("y_copied")
        ld_lam, lam_sum, lam_exp = sem("ld_lam"), sem("lam_sum"), sem("lam_exp")
        dve_self, act_self = sem("dve_self"), sem("act_self")
        st_mk, st_mv, st_misc, st_kn, st_ft, st_cs = (sem(n) for n in (
            "st_mk", "st_mv", "st_misc", "st_kn", "st_ft", "st_cs"))
        st_y = [sem(f"st_y{i}") for i in range(2)]
        st_v = [sem(f"st_v{i}") for i in range(2)]

        ident = cst[:, C_ID:C_ID + P]
        blk = cst[:, C_BLK:C_BLK + P]

        col, put, nrow = {}, [], [0]

        def param(name, src, n):
            col[name] = nrow[0]
            done = 0
            while done < n:
                r = nrow[0] + done
                k = min(n - done, P - r % P)
                put.append((r, k, src, done))
                done += k
            nrow[0] += n

        param("norm_mix", a["norm_mix"].rearrange("l (c p) -> (l c) p", p=P), 16)
        param("norm_ffn", a["norm_ffn"].rearrange("l (c p) -> (l c) p", p=P), 16)
        param("norm_mem", a["norm_mem"].rearrange("l (c p) -> (l c) p", p=P), 16)
        param("norm_kv", a["norm_kv"].rearrange("(c p) -> c p", p=P), 8)
        param("conv_a_b", a["conv_a_b"].rearrange("l (c p) -> (l c) p", p=P), CC)
        param("ln_a_g", a["ln_a_g"].rearrange("l (c p) -> (l c) p", p=P), CC)
        param("ln_a_b", a["ln_a_b"].rearrange("l (c p) -> (l c) p", p=P), CC)
        param("conv_a_w", a["conv_a_w"].rearrange("l t (c p) -> (l t c) p", p=P), TAPS * CC)
        param("ffn_conv_w", a["ffn_conv_w"].rearrange("l t (c p) -> (l t c) p", p=P), 2 * FTAPS * FC)
        param("ffn_conv_b", a["ffn_conv_b"].rearrange("l (c p) -> (l c) p", p=P), 2 * FC)
        param("k_norm", a["k_norm"].rearrange("(o c) d -> o (c d)", o=1), 1)
        param("q_norm", a["q_norm"].rearrange("o c d -> o (c d)"), 1)
        param("subln", a["subln_g"], 1)
        param("mem_q", None, 2)
        param("mem_k", None, 2)
        NROW = nrow[0]

        def pcol(name, i=0, rows_=slice(0, P)):
            return pT[rows_, col[name] + i:col[name] + i + 1]

        def pcol_at(name, i):
            return pT[:, bass.ds(i + col[name], 1)]

        SQ = dict(n0=0, mem=8, tA=16, ln=22, n1=28, n2=36, tB=44, sub=58, n3=64)
        RT = dict(n0=0, mem=1, ln=2, n1=3, n2=4, sub=5, n3=11)

        tiles = {}
        for s in [S_MEM - 2, S_MEM - 1] + list(range(S_MEM, S_MEM + 8)) + list(range(S_B, S_B + 20)):
            if s < S_MEM:
                kind = "q"
            elif s < S_MEM + 8:
                kind = "k" if (s - S_MEM) % 4 < 2 else "v"
            else:
                kind = "kvq"[(s - S_B) % 3] if s < S_B + 18 else "q"
            nq = sum(1 for v in tiles.values() if v[0] != "v")
            tiles[s] = (kind, len(tiles), nq if kind != "v" else None)

        def sq_index(s):
            nq = tiles[s][2]
            return SQ["tA"] + nq if s < S_B else SQ["tB"] + nq - 6

        def cols_of(s):
            return MEM if S_MEM <= s < S_MEM + 8 else T

        def psum2(t, n):
            return t[:, :, 0:HT] if n == T else t[:, 0, 0:n]

        def ma_bank(m, h):
            return (psX[:, m % 2, 0:MEM], acc[m % 2][:, 0, 0:MEM])[h]

        ms_keys, ms_scores = acc[0][:, 1, :], acc[1][:, 1, 0:MEM]

        def flat2(ap, n):
            return ap.rearrange("p (c n) -> p c n", c=2) if n == T else ap

        block = ctx.enter_context(nc.Block())

        def beat(b):
            out = []
            for what, lag in (("S", 18), ("T", 22), ("O", 23)):
                n, r = divmod(b - lag, 3)
                if r == 0 and 0 <= n < H * QB:
                    out.append((what, n))
            return out

        LAST_BEAT = 18 + 3 * (H * QB - 1) + 5

        @block.sync
        def _(sp):
            sp.dma_start(cst[:, :], a["consts"]).then_inc(ld_const, 16)
            x_rows = a["x_prompt"].rearrange("o (i p) n -> (o p) i n", p=P)
            sp.dma_start(xnat[:, 0:QB, :], x_rows).then_inc(ld_x, 16)
            sp.dma_start(xnat[0:NSA, QB, :], a["x_sample"].rearrange("b t n -> (b t) n")).then_inc(ld_x, 16)

            def load(s, src, kb=KD):
                if not isinstance(s, int) or s >= 4:
                    sp.wait_ge(w_lo_ready, s - 3)
                slot = s % 4 if isinstance(s, int) else slot_of[0]
                sp.dma_start(wraw[:, slot, 0:kb * P].rearrange("p (k n) -> p k n", n=P), src).then_inc(w_loaded[slot], 16)

            slot_of = [0]

            def block_cols(w, m, k0=0, kb=KD):
                return w[k0 * P:(k0 + kb) * P, m * P:(m + 1) * P].rearrange("(k p) n -> p k n", p=P)

            win, wmem = a["w_in_a"][0], a["w_mem_kv"]
            for s in range(S_IN, S_MEM):
                m = s // 2 + CC * (s % 2) if s < 2 * CC else s
                load(s, block_cols(win, m))
                if s == 1:
                    sp.dma_start(crow[0:120, :, :], a["state_conv_a"][0].rearrange("(g b) t n -> (b t) g n", g=2)
                                 ).then_inc(ld_state, 16)
                    sp.dma_start(frow[:, :], a["state_ffn_conv"].rearrange("l b r n -> (l b r) n")).then_inc(ld_state, 16)
                    sp.dma_start(lamin[:, :, :].rearrange("p c n -> p (c n)"),
                                 a["lambdas"].rearrange("o c n -> o (c n)").partition_broadcast(P)).then_inc(ld_lam, 16)
                    sp.dma_start(mnat[:, :, :], a["mem_prompt"].rearrange("o (i p) n -> (o p) i n", p=P)
                                 ).then_inc(ld_mem, 16)
            for s in range(S_MEM, S_OUT[0]):
                l, m = divmod(s - S_MEM, 4)
                load(s, block_cols(wmem[l], m))
            for l in range(2):
                wo = a["w_out_a"][0] if l == 0 else a["w_out_b"][0]
                for m in range(KD):
                    load(S_OUT[l] + m, block_cols(wo, m))
                for g, (g0, n) in enumerate(GROUPS):
                    with sp.Fori(0, n // 2) as i:
                        for c in range(4):
                            s = UP[l][g] + c
                            slot_of[0] = s % 4
                            first = g0 + c // 2 + FC * (c % 2)
                            src = a["w_up"][l][:, bass.ds(i * (2 * P) + first * P, P)].rearrange("(k p) n -> p k n", p=P)
                            load(i * 4 + s, src)
                    with sp.Fori(0, 2) as i:
                        for c in range(4):
                            s = DOWN[l][g] + c
                            slot_of[0] = s % 4
                            src = a["w_down"][l][g0 * P:(g0 + n) * P, bass.ds(i * (4 * P) + c * P, P)
                                                 ].rearrange("(k p) n -> p k n", p=P)
                            load(i * 4 + s, src, kb=n)
                if l == 0:
                    for h in range(H):
                        load(S_B + 3 * h, block_cols(a["w_kv"], h))
                        load(S_B + 3 * h + 1, block_cols(a["w_kv"], H + h))
                        load(S_B + 3 * h + 2, block_cols(a["w_in_b"][0], h))
                    for c in range(MC):
                        load(S_B + 18 + c, block_cols(a["w_in_b"][0], H + c))

        @block.tensor
        def _(pe):
            def mm_step(s, slot, hi, lo, kb=KD, cols=T, ready=None, hooks=None):
                pe.wait_ge(w_lo_ready, s + 1)
                if not isinstance(s, int) or s >= 2:
                    pe.wait_ge(acc_free, s - 1)
                n, parts = (HT, 2) if cols == T else (cols, 1)
                for k in range(kb):
                    if ready:
                        ready(k)
                    wh, wl = whi[:, slot, k * P:(k + 1) * P], wlo[:, slot, k * P:(k + 1) * P]
                    for q, (w, x) in enumerate(((wh, hi), (wh, lo), (wl, hi))):
                        for c in range(parts):
                            last = nc.tensor.matmul(acc[slot][:, c, 0:n], w, x[:, k, c * n:(c + 1) * n],
                                                    start=(k == 0 and q == 0), stop=(k == kb - 1 and q == 2))
                    if k == kb - 1:
                        last.then_inc(mm_done, 1)
                    if hooks:
                        hooks(k)

            def square_sum(k, out, w, cols=T, first=True, final=True):
                pe.wait_ge(sq_ready, k + 1)
                n, parts = (HT, 2) if cols == T else (cols, 1)
                for c in range(parts):
                    last = nc.tensor.matmul(out[:, c, 0:n], w, sqt[:, k % 2, c * n:(c + 1) * n],
                                            start=first, stop=final)
                last.then_inc(sq_used, 1)

            def tile_hook(s):
                kind, t, nq = tiles[s]
                if kind != "v":
                    square_sum(sq_index(s), acc[s % 2], blk, cols_of(s))
                    return
                pe.wait_ge(tile_ev, t + 1)
                src = qf[:, t % 2, :]
                if s < S_B:
                    for i in range(MB):
                        last = nc.tensor.transpose(acc[s % 2][:, 0, i * P:(i + 1) * P], src[:, i * P:(i + 1) * P], ident)
                else:
                    for i in range(QB):
                        nc.tensor.transpose(acc[s % 2][:, 0, i * P:(i + 1) * P], src[:, i * P:(i + 1) * P], ident)
                    last = nc.tensor.transpose(acc[s % 2][0:NSA, 1, 0:P], src[:, NPR:T], ident)
                last.then_inc(tile_pe, 1)

            pe.wait_ge(ld_const, 16)
            pe.wait_ge(zeroed, 1)

            def setup_bank(q):
                if q >= 2:
                    pe.wait_ge(setup_drained, q - 1)
                return psT[:, q % 2, :]

            pe.wait_ge(ld_rows, 16 * (sum(1 for x in put if x[2] is not None) + 4))
            b = setup_bank(0)
            for i in range(4):
                n = min(P, NROW - i * P)
                last = nc.tensor.transpose(b[:, i * P:i * P + n], rows[0:n, i, :], ident[0:n, 0:n])
            last.then_inc(setup_filled, 1)
            pe.wait_ge(ld_x, 32)
            b = setup_bank(1)
            for c in range(KD):
                last = nc.tensor.transpose(b[:, c * NSA:(c + 1) * NSA], xnat[0:NSA, QB, c * P:(c + 1) * P],
                                           ident[0:NSA, 0:NSA])
            last.then_inc(setup_filled, 1)
            for c in range(KD):
                b = setup_bank(2 + c)
                for i in range(QB):
                    last = nc.tensor.transpose(b[:, i * P:(i + 1) * P], xnat[:, i, c * P:(c + 1) * P], ident)
                last.then_inc(setup_filled, 1)
                if c:
                    square_sum(SQ["n0"] + c - 1, psX, ones[:, :], first=(c == 1), final=False)
            square_sum(SQ["n0"] + 7, psX, ones[:, :], first=False)

            def xa_ready(n):
                return lambda k: pe.wait_ge(xg_lo, 8 * n + k + 1)

            mm_step(0, 0, xa_hi, xa_lo, ready=xa_ready(0))
            mm_step(1, 1, xa_hi, xa_lo)
            pe.wait_ge(ld_mem, 16)
            for j in range(4):
                b = setup_bank(10 + j)
                for cc in range(2):
                    for m in range(MB):
                        last = nc.tensor.transpose(b[:, (cc * MB + m) * P:(cc * MB + m + 1) * P],
                                                   mnat[:, m, (2 * j + cc) * P:(2 * j + cc + 1) * P], ident)
                last.then_inc(setup_filled, 1)
            pe.wait_ge(ld_state, 32)
            for j in range(CC):
                b = setup_bank(14 + j)
                for g in range(2):
                    last = nc.tensor.transpose(b[:, g * 120:(g + 1) * 120], crow[0:120, g, j * P:(j + 1) * P],
                                               ident[0:120, 0:120])
                last.then_inc(setup_filled, 1)
            for g in range(2):
                b = setup_bank(20 + g)
                for j in range(11):
                    c = g * 11 + j
                    last = nc.tensor.transpose(b[:, j * 32:(j + 1) * 32], frow[:, c * P:(c + 1) * P], ident[0:32, 0:32])
                last.then_inc(setup_filled, 1)
            pe.wait_ge(turned, RT["n0"] + 1)
            for c in range(KD):
                square_sum(SQ["mem"] + c, psX, ones[:, :], MEM, first=(c == 0), final=(c == KD - 1))

            def conv_tail():
                pe.wait_ge(setup_drained, 22)
                for g in range(2):
                    for j in range(CC):
                        dst = ((psX, psT)[g][:, 0, j * P:(j + 1) * P] if j < 4 else
                               psX[:, 1, (2 * g + j - 4) * P:(2 * g + j - 3) * P])
                        dst, src = (dst[0:30, :], uext[:, j, NPR:CEXT]) if g == 0 else (dst[0:NSA, :], unew[:, j, :])
                        last = nc.tensor.transpose(dst, src, ident)
                last.then_inc(ct_T, 1)

            def memory_keys_out(l):
                pe.wait_ge(qk_done, 2 + 2 * (l + 1))
                for c in range(MC):
                    for m in range(MB):
                        last = nc.tensor.transpose(psT[:, l, m * MW + c * P:m * MW + (c + 1) * P],
                                                   memk[:, l, c, m * P:(m + 1) * P], ident)
                last.then_inc(mk_T, 1)

            def beside(s, k):
                if k == 3 and s - 1 in tiles:
                    tile_hook(s - 1)
                if (s, k) == (S_MEM + 3, 5):
                    conv_tail()
                if (s, k) == (S_MEM + 6, 5):
                    pe.wait_ge(ct_c, 3)
                    memory_keys_out(0)

            for s in range(2, S_MEM):
                mm_step(s, s % 2, xa_hi, xa_lo, hooks=lambda k, s=s: beside(s, k))
            for s in range(S_MEM, S_OUT[0]):
                l = (s - S_MEM) // 4
                mm_step(s, s % 2, mg_hi[l], mg_lo[l], cols=MEM,
                        ready=(lambda k, l=l: pe.wait_ge(mg_l, 8 * l + k + 1)) if (s - S_MEM) % 4 == 0 else None,
                        hooks=lambda k, s=s: beside(s, k))
            tile_hook(S_OUT[0] - 1)

            memory_keys_out(1)

            def mem_attention(l, q):
                base = 8 * l
                pe.wait_ge(acc_free, S_OUT[l])

                def scores(m):
                    c, tb = divmod(m, QB)
                    if m >= 2:
                        pe.wait_ge(ma_exp, base + m - 1)
                    for h in range(2):
                        r = slice(h * MHD, (h + 1) * MHD)
                        last = nc.tensor.matmul(ma_bank(m, h), q[r, c, tb * P:(tb + 1) * P],
                                                memk[r, l, c, :], start=True, stop=True)
                    last.then_inc(ma_S, 1)

                def turn(m):
                    pe.wait_ge(ma_p, base + m + 1)
                    if m:
                        pe.wait_ge(ma_aT, base + m)
                    for x in range(4):
                        last = nc.tensor.transpose(psT[:, 0, x * P:(x + 1) * P], et[:, m % 2, x * P:(x + 1) * P], ident)
                    last.then_inc(ma_T, 1)

                def pv(m):
                    c = m // QB
                    pe.wait_ge(ma_aT, base + m + 1)
                    if m:
                        pe.wait_ge(ma_o, base + m)
                    for mb in range(MB):
                        last = nc.tensor.matmul(psT[:, 1, 0:2 * P], memv[:, l, mb, c * P:(c + 1) * P],
                                                pTt[:, mb:4:2, :], start=(mb == 0), stop=(mb == MB - 1))
                    last.then_inc(ma_pv, 1)

                def turn_cached(b_):
                    if b_ == 0:
                        pe.wait_ge(mc_k, 16 * DB * (l + 1))
                    else:
                        pe.wait_ge(ms_kc, base + b_)
                    for c in range(MC):
                        for m in range(MB):
                            last = nc.tensor.transpose(ms_keys[:, c * MEM + m * P:c * MEM + (m + 1) * P],
                                                       mcache[:, b_, m * MW + c * P:m * MW + (c + 1) * P], ident)
                    last.then_inc(ms_T, 1)

                def scores_cached(b_):
                    if b_ == 0:
                        pe.wait_ge(qm_ready, l + 1)
                    pe.wait_ge(ms_kc, base + b_ + 1)
                    for c in range(MC):
                        last = nc.tensor.matmul(ms_scores, qm[:, c, b_ * P:(b_ + 1) * P], kTb[:, b_ % 2, c, :],
                                                start=(b_ == 0 and c == 0), stop=(b_ == DB - 1 and c == MC - 1))
                    last.then_inc(ms_S, 1)

                scores(0)
                for m in range(8):
                    if m < 7:
                        scores(m + 1)
                    turn_cached(m)
                    if m:
                        pv(m - 1)
                        scores_cached(m - 1)
                    turn(m)
                pv(7)
                scores_cached(DB - 1)
                pe.wait_ge(ma_o, base + 8)

            def mem_sample(l):
                pe.wait_ge(mx_p, l + 1)
                for m in range(MB):
                    last = nc.tensor.transpose(psT[:, 0, m * P:(m + 1) * P], et[:, 0, m * P:(m + 1) * P], ident)
                last.then_inc(mx_T, 1)
                pe.wait_ge(mx_aT, l + 1)
                pe.wait_ge(mc_v, 16 * DB * (l + 1))
                for b_ in range(DB):
                    for c in range(MC):
                        for m in range(MB):
                            x = (b_ * MC + c) * 16
                            last = nc.tensor.matmul(psX[:, 1, x:x + 16], mcache[:, b_, m * MW + c * P:m * MW + (c + 1) * P],
                                                    pTt[:, m, b_ * 16:(b_ + 1) * 16], start=(m == 0), stop=(m == MB - 1))
                last.then_inc(mx_pv, 1)

            pe.wait_ge(mk_c, 2)
            mem_attention(0, mq)
            mem_sample(0)

            pe.wait_ge(mx_o, 1)
            for j in range(CC):
                pe.wait_ge(conv_step, 2 * TAPS * (j // 2 + 1) - 1 + j % 2)
                for c in range(2):
                    last = nc.tensor.matmul(psX[:, c, 0:HT], ones[:, :], convt[:, j, c * HT:(c + 1) * HT],
                                            start=(j == 0), stop=(j == CC - 1))
            last.then_inc(ln_mean, 1)
            pe.wait_ge(ln_m, 1)
            for j in range(CC):
                square_sum(SQ["ln"] + j, psX, ones[:, :], first=(j == 0), final=(j == CC - 1))
            def out_section(l, n):
                order = [CC, CC + 1] + list(range(CC))
                for m in range(KD):
                    s = S_OUT[l] + m
                    pe.wait_ge(w_lo_ready, s + 1)
                    pe.wait_ge(acc_free, s - 1)
                    for i, k in enumerate(order):
                        if m == 0:
                            pe.wait_ge(cm_lo, 8 * l + i + 1)
                        wh, wl = whi[:, s % 2, k * P:(k + 1) * P], wlo[:, s % 2, k * P:(k + 1) * P]
                        for q, (w, x) in enumerate(((wh, xb_hi), (wh, xb_lo), (wl, xb_hi))):
                            for c in range(2):
                                last = nc.tensor.matmul(acc[s % 2][:, c, 0:HT], w, x[:, k, c * HT:(c + 1) * HT],
                                                        start=(i == 0 and q == 0), stop=(i == KD - 1 and q == 2))
                    last.then_inc(mm_done, 1)
                    if m:
                        square_sum(SQ[n] + m - 1, psX, ones[:, :], first=(m == 1), final=False)
                square_sum(SQ[n] + KD - 1, psX, ones[:, :], first=False)

            def ffn(l, norm):
                for g, (g0, n) in enumerate(GROUPS):
                    s0 = UP[l][g]
                    for c in range(4):
                        mm_step(s0 + c, (s0 + c) % 2, xa_hi, xa_lo,
                                ready=xa_ready(norm) if g == 0 and c == 0 else None)
                    with pe.Fori(1, n // 2) as i:
                        for c in range(4):
                            mm_step(i * 4 + (s0 + c), (s0 + c) % 2, xa_hi, xa_lo)
                    s0 = DOWN[l][g]
                    if g < 2:
                        for c in range(4):
                            mm_step(s0 + c, (s0 + c) % 2, xb_hi, xb_lo, kb=n,
                                    ready=(lambda k: pe.wait_ge(ulo_ready, l * FC + g0 + k + 1)) if c == 0 else None)
                        with pe.Fori(1, 2) as i:
                            for c in range(4):
                                mm_step(i * 4 + (s0 + c), (s0 + c) % 2, xb_hi, xb_lo, kb=n)
                        continue
                    for m in range(KD):
                        mm_step(s0 + m, (s0 + m) % 2, xb_hi, xb_lo, kb=n,
                                ready=(lambda k: pe.wait_ge(ulo_ready, l * FC + g0 + k + 1)) if m == 0 else None,
                                hooks=lambda k, m=m: after_chunk(l, m - 1) if k == 3 and m else None)
                    after_chunk(l, KD - 1)

            def after_chunk(l, m):
                if l == 0:
                    square_sum(SQ["n2"] + m, psX, ones[:, :], first=(m == 0), final=(m == KD - 1))
                    return
                pe.wait_ge(acc_free, DOWN[1][2] + m + 1)
                if m >= 2:
                    pe.wait_ge(y_c, m - 1)
                for i in range(QB):
                    nc.tensor.transpose(psT[:, m % 2, i * P:(i + 1) * P], xT[:, m, i * P:(i + 1) * P], ident)
                last = nc.tensor.transpose(psX[0:NSA, m // 4, (m % 4) * P:(m % 4 + 1) * P], xT[:, m, NPR:T], ident)
                last.then_inc(y_T, 1)

            def ffn_tail(l):
                if l:
                    pe.wait_ge(y_c, KD)
                for r in range(5):
                    n = 4 * FC if r < 4 else 2 * FC
                    last = nc.tensor.transpose(psT[0:n, r // 4, (r % 4) * P:(r % 4 + 1) * P],
                                               gcol[:, 4 * r:4 * r + n // FC, :], ident)
                last.then_inc(ft_T, 1)

            pe.wait_ge(turned, RT["ln"] + 1)
            out_section(0, "n1")
            ffn(0, 1)
            ffn_tail(0)

            def attend(what, n):
                h, i = divmod(n, QB)
                L = (i + 1) * P
                if what == "S":
                    if i == 0:
                        pe.wait_ge(qk_done, 6 + 2 * h + 2)
                    if n:
                        pe.wait_ge(at_exp, n)
                    else:
                        pe.wait_ge(turned, RT["n2"] + 1)
                    for c in range(2):
                        r = slice(c * MHD, (c + 1) * MHD)
                        last = nc.tensor.matmul(psX[:, c, 0:L], qT[r, h % 2, i * P:(i + 1) * P], kT[r, h, 0:L],
                                                start=True, stop=True)
                    last.then_inc(at_S, 1)
                elif what == "T":
                    pe.wait_ge(at_p, n + 1)
                    if n:
                        pe.wait_ge(at_aT, n)
                    for j in range(i + 1):
                        last = nc.tensor.transpose(psT[:, 0, j * P:(j + 1) * P], prb[:, j * P:(j + 1) * P], ident)
                    last.then_inc(at_T, 1)
                else:
                    pe.wait_ge(at_aT, n + 1)
                    if n:
                        pe.wait_ge(at_O, n)
                    if i == 0:
                        pe.wait_ge(acc_free, S_B + 3 * h + 2)
                    for j in range(i + 1):
                        last = nc.tensor.matmul(psT[:, 1, 0:P], vnat[:, h % 2, j, :], pTt[:, j, :],
                                                start=(j == 0), stop=(j == i))
                    last.then_inc(at_pv, 1)

            pe.wait_ge(ft_c, 1)
            for s in range(S_B, S_B + 20):
                def hooks(k, s=s):
                    if k % 2 == 0:
                        for what, n in beat(4 * (s - S_B) + k // 2):
                            attend(what, n)
                    if k == 3 and s > S_B:
                        tile_hook(s - 1)
                q_step = (s - S_B) % 3 == 2 or s >= S_B + 18
                hi, lo = (xb_hi, xb_lo) if q_step else (xa_hi, xa_lo)
                ready = xa_ready(2) if s == S_B else (lambda k: pe.wait_ge(xb_l, k + 1)) if s == S_B + 2 else None
                mm_step(s, s % 2, hi, lo, ready=ready, hooks=hooks)
            tile_hook(S_B + 19)
            for b_ in range(80, LAST_BEAT + 1):
                for what, n in beat(b_):
                    attend(what, n)

            pe.wait_ge(at_O, H * QB)
            for h in range(H):
                if h >= 2:
                    pe.wait_ge(kn_c, h - 1)
                for i in range(QB):
                    nc.tensor.transpose(psT[:, h % 2, i * P:(i + 1) * P], kT[:, h, i * P:(i + 1) * P], ident)
                last = nc.tensor.transpose(psX[0:NSA, h // 4, (h % 4) * P:(h % 4 + 1) * P], kT[:, h, NPR:T], ident)
                last.then_inc(kn_T, 1)

            def o_rows(h):
                return acc[0][0:NSA, h // 4, (h % 4) * VD:(h % 4 + 1) * VD]

            pe.wait_ge(acc_free, S_OUT[1])
            pe.wait_ge(kn_c, H + 1)
            pe.wait_ge(kn_ready, 1)
            for g in range(DB // 2):
                for b2 in range(2):
                    b_ = 2 * g + b2
                    pe.wait_ge(kp_ld[b2], 32 * (g + 1))
                    for q in range(3):
                        u = 3 * b_ + q
                        if u >= 2:
                            pe.wait_ge(ds_kc, u - 1)
                        for hh in range(2):
                            for pg in range(PAGES):
                                last = nc.tensor.transpose(psT[:, u % 2, (hh * PAGES + pg) * P:(hh * PAGES + pg + 1) * P],
                                                           kpg[:, b2, pg, (2 * q + hh) * VD:(2 * q + hh + 1) * VD], ident)
                        last.then_inc(ds_T, 1)
                    pe.wait_ge(ds_kc, 3 * b_ + 3)
                    if b2 == 0:
                        pe.wait_ge(qp_ready, g + 1)
                        if g:
                            pe.wait_ge(ds_exp, g)
                    for h in range(H):
                        last = nc.tensor.matmul(psX[:, 0, 0:NKEY], qpad[:, b2, h * P:(h + 1) * P], kTs[:, h, :],
                                                start=(b2 == 0 and h == 0), stop=(b2 == 1 and h == H - 1))
                    last.then_inc(ds_S, 1)
                pe.wait_ge(ds_p, g + 1)
                for kb in range(PAGES):
                    nc.tensor.matmul(psX[:, 1, kb * 48:(kb + 1) * 48], exps[:, kb * P:(kb + 1) * P], cs[:, :],
                                     start=True, stop=True)
                last = nc.tensor.matmul(psX[0:NSA, 1, 96:144], exps[:, PAST:NKEY], cs[:, :], start=True, stop=True)
                last.then_inc(ds_A, 1)
                pe.wait_ge(ds_a, g + 1)
                for b2 in range(2):
                    pe.wait_ge(vp_ld[b2], 32 * (g + 1))
                    for h in range(H):
                        for pg in range(PAGES):
                            last = nc.tensor.matmul(o_rows(h), apad[:, b2, pg, h, :], vpg[:, b2, pg, h * VD:(h + 1) * VD],
                                                    start=(g + b2 + pg == 0 and h % 4 == 0), stop=False)
                last.then_inc(ds_pv, 1)
            for h in range(H):
                last = nc.tensor.matmul(o_rows(h), anew[:, h, :], vnew[:, h, :], start=False, stop=h in (3, H - 1))
            last.then_inc(ds_row, 1)
            pe.wait_ge(ds_rc, 1)
            for h in range(H):
                last = nc.tensor.transpose(psX[:, 1, h * NSA:(h + 1) * NSA], orow[:, h * VD:(h + 1) * VD],
                                           ident[0:NSA, 0:NSA])
            last.then_inc(ds_rT, 1)

            pe.wait_ge(ds_o, 1)
            mem_attention(1, mq2)
            mem_sample(1)
            pe.wait_ge(mx_o, 2)
            for h in range(H):
                if h >= 4:
                    pe.wait_ge(turned, RT["sub"] + h - 3)
                square_sum(SQ["sub"] + h, (psX, psT, acc[0], acc[1])[h % 4], ones[:, :])
            pe.wait_ge(turned, RT["sub"] + H)
            out_section(1, "n3")
            pe.wait_ge(turned, RT["n3"] + 1)
            ffn(1, 3)
            ffn_tail(1)

        @block.scalar
        def _(act):
            own = [0]

            def split_hi(s, slot=None, loads=None):
                if slot is None:
                    if s >= STEPS:
                        return
                    slot, loads = s % 4, s // 4 + 1
                act.wait_ge(w_loaded[slot], loads * 16)
                if not isinstance(s, int) or s >= 2:
                    act.wait_ge(mm_done, s - 1)
                nc.scalar.activation(whi[:, slot % 2, :], wraw[:, slot, :], ACT.Copy).then_inc(w_hi_ready, 1)

            nsq = [0]

            def square(src, n=T):
                k = nsq[0]
                nsq[0] += 1
                if k >= 2:
                    act.wait_ge(sq_used, k - 1)
                nc.scalar.activation(sqt[:, k % 2, 0:n], src, ACT.Square).then_inc(sq_ready, 1)

            nrt = [0]

            def root(n):
                k = nrt[0]
                nrt[0] += 1
                w = n // 32
                act.wait_ge(var_ready, k + 1)
                nc.scalar.activation(small[:, 1, 0:w], small[:, 0, 0:w], ACT.Sqrt).then_inc(sd_ready, 1)

            def scaled_hi(dst, c, src, gain, s_):
                nc.scalar.activation(dst[:, c, :], src, ACT.Copy, scale=gain).then_inc(s_, 1)

            for r, k, src, done in put:
                if src is not None:
                    act.dma_start(rows[r % P:r % P + k, r // P, :], src[done:done + k, :]).then_inc(ld_rows, 16)
                    continue
            for name in ("mem_q", "mem_k"):
                r = col[name]
                assert r // P == (r + 1) // P
                for h in range(2):
                    act.dma_start(rows[r % P:r % P + 2, r // P, h * MHD:(h + 1) * MHD],
                                 a[name + "_norm"]).then_inc(ld_rows, 16)
            split_hi(0)
            split_hi(1)
            for c in range(KD):
                act.wait_ge(setup_drained, c + 3)
                square(xT[:, c, :])
                scaled_hi(xa_hi, c, xT[:, c, :], pcol("norm_mix", c), xg_hi)
            root(T)
            act.wait_ge(lam_sum, 1)
            nc.scalar.activation(lamt[:, 2:4], lamt[:, 0:2], ACT.Exp).then_inc(lam_exp, 1)

            def tile_sq(s):
                kind, t, nq = tiles[s]
                if kind != "v":
                    act.wait_ge(tile_ev, t + 1)
                    square(qf[:, t % 2, 0:cols_of(s)], cols_of(s))

            def tile_end(s):
                kind, t, nq = tiles[s]
                if kind != "v":
                    root(cols_of(s))
                    return
                act.wait_ge(tile_pe, sum(1 for v in tiles.values() if v[0] == "v" and v[1] <= t))
                if s < S_B:
                    l, c = (s - S_MEM) // 4, (s - S_MEM) % 2
                    src = acc[s % 2][:, 0, 0:MEM].rearrange("p (m n) -> p m n", n=P)
                    nc.scalar.activation(memv[:, l, :, c * P:(c + 1) * P], src, ACT.Copy).then_inc(acc_free, 1)
                    return
                h = (s - S_B) // 3
                if h >= 2:
                    act.wait_ge(st_v[h % 2], 16 * (h // 2))
                    act.wait_ge(at_pv, QB * (h - 1))
                nc.scalar.activation(vnew[:, h, :], acc[s % 2][0:NSA, 1, 0:P], ACT.Copy).then_inc(act_self, 1)
                own[0] += 1
                nc.scalar.activation(vnat[:, h % 2, :, :], acc[s % 2][:, 0, :].rearrange("p (i n) -> p i n", n=P),
                                     ACT.Copy).then_inc(acc_free, 1)

            for s in range(0, S_MEM):
                if s < 2 * CC and s % 2:
                    act.wait_ge(acc_free, s + 1)
                    nc.scalar.activation(stile[:, :], gtile[:, :], ACT.Sigmoid).then_inc(sig_ready, 1)
                if s in tiles:
                    tile_sq(s)
                split_hi(s + 2)
                if s in tiles:
                    tile_end(s)
                if s == 1:
                    for c in range(KD):
                        act.wait_ge(setup_drained, 10 + c // 2 + 1)
                        square(memT[:, c, :], MEM)
                    root(MEM)
                    for l in range(2):
                        for c in range(KD):
                            nc.scalar.activation(mg_hi[l][:, c, :], memT[:, c, :], ACT.Copy,
                                                 scale=pcol("norm_mem", 8 * l + c)).then_inc(mg_h, 1)
            def memory_keys_out(l):
                act.wait_ge(mk_T, l + 1)
                if l:
                    act.wait_ge(st_mk, 16)
                nc.scalar.activation(mkn[:, :, :].rearrange("p m n -> p (m n)"), psT[:, l, :], ACT.Copy).then_inc(mk_c, 1)

            for s in range(S_MEM, S_OUT[0]):
                tile_sq(s)
                split_hi(s + 2)
                tile_end(s)
                if s == S_MEM + 3:
                    act.wait_ge(ct_T, 1)
                    nc.scalar.activation(ctail[0:30, 0, 0:512], psX[0:30, 0, :], ACT.Copy).then_inc(ct_c, 1)
                    nc.scalar.activation(ctail[:, 1, 0:512], psT[0:NSA, 0, :], ACT.Copy).then_inc(ct_c, 1)
                    for g, n in ((0, 30), (1, NSA)):
                        ins = nc.scalar.activation(ctail[0:n, g, 512:CA], psX[0:n, 1, g * 256:(g + 1) * 256], ACT.Copy)
                    ins.then_inc(ct_c, 1)
                if s == S_MEM + 6:
                    memory_keys_out(0)

            memory_keys_out(1)

            def mem_attention(l):
                base = 8 * l

                def exps(m):
                    act.wait_ge(ma_nb, base + m + 1)
                    if m >= 2:
                        act.wait_ge(ma_T, base + m - 1)
                    for h in range(2):
                        last = nc.scalar.activation(et[:, m % 2, h * MEM:(h + 1) * MEM], ma_bank(m, h),
                                                    ACT.Exp, bias=stat[:, m % 2, 2 + h:3 + h], scale=ISQ,
                                                    accum_out=stat[:, m % 2, 4 + h:5 + h])
                    last.then_inc(ma_exp, 1)

                def copy(m):
                    act.wait_ge(ma_T, base + m + 1)
                    if m:
                        act.wait_ge(ma_pv, base + m)
                    nc.scalar.activation(pTt[:, :, :].rearrange("p m n -> p (m n)"), psT[:, 0, :], ACT.Copy).then_inc(ma_aT, 1)

                def copy_cached(b_):
                    act.wait_ge(ms_T, base + b_ + 1)
                    if b_ >= 2:
                        act.wait_ge(ms_S, base + b_ - 1)
                    nc.scalar.activation(kTb[:, b_ % 2, :, :].rearrange("p m n -> p (m n)"), ms_keys,
                                         ACT.Copy).then_inc(ms_kc, 1)

                exps(0)
                for m in range(8):
                    copy_cached(m)
                    if m < 7:
                        exps(m + 1)
                    copy(m)

            def mem_sample(l):
                act.wait_ge(mx_nb, l + 1)
                nc.scalar.activation(et[:, 0, 0:MEM], ms_scores, ACT.Exp, bias=stat[:, 0, 2:3], scale=ISQ,
                                     accum_out=stat[:, 0, 4:5]).then_inc(mx_exp, 1)
                act.wait_ge(mx_T, l + 1)
                nc.scalar.activation(pTt[:, 0:2, :].rearrange("p m n -> p (m n)"), psT[:, 0, 0:MEM], ACT.Copy
                                     ).then_inc(mx_aT, 1)

            def mix_hi(l, tile_):
                act.wait_ge(mx_o, l + 1)
                for c in range(MC):
                    nc.scalar.activation(xb_hi[:, CC + c, :], tile_[:, c, :], ACT.Copy).then_inc(cm_hi, 1)

            mem_attention(0)
            mem_sample(0)
            mix_hi(0, mT)

            act.wait_ge(ln_mean, 1)
            nc.scalar.activation(qf[:, 0, :].rearrange("p (c n) -> p c n", c=2), psX[:, :, 0:HT], ACT.Copy,
                                 scale=1.0 / CA).then_inc(ln_m, 1)
            for j in range(CC):
                act.wait_ge(ln_c, j + 1)
                square(convt[:, j, :])
            root(T)
            for j in range(CC):
                act.wait_ge(ln_n, j + 1)
                if j >= 1:
                    act.wait_ge(cm_lo, MC + j)
                nc.scalar.activation(qf[:, 1, :], convt[:, j, :], ACT.Silu, bias=pcol("ln_a_b", j),
                                     scale=pcol("ln_a_g", j)).then_inc(ln_y, 1)
                act.wait_ge(ln_y, j + 1)
                nc.scalar.activation(xb_hi[:, j, :], qf[:, 1, :], ACT.Copy).then_inc(cm_hi, 1)

            def out_section(l, gain):
                for m in range(KD):
                    s = S_OUT[l] + m
                    split_hi(s + 2)
                    act.wait_ge(acc_free, s + 1)
                    square(xT[:, m, :])
                    scaled_hi(xa_hi, m, xT[:, m, :], pcol(gain, 8 * l + m), xg_hi)
                root(T)

            def ffn(l):
                for g, (g0, n) in enumerate(GROUPS):
                    def up(i, s0=UP[l][g]):
                        for cc in range(2):
                            q = i * 2 + (l * FC + g0 + cc)
                            s = s0 + 2 * cc
                            split_hi(i * 4 + (s + 2), (s + 2) % 4, i + ((s + 2) // 4 + 1))
                            act.wait_ge(conv_ready, q + 1)
                            nc.scalar.activation(gel[:, :], gcv[:, :], ACT.Gelu_apprx_tanh,
                                                 bias=pcol_at("ffn_conv_b", q)).then_inc(gelu_ready, 1)
                            split_hi(i * 4 + (s + 3), (s + 3) % 4, i + ((s + 3) // 4 + 1))
                            act.wait_ge(u_ready, q + 1)
                            nc.scalar.activation(xb_hi[:, bass.ds(i * 2 + cc, 1), :].rearrange("p o n -> p (o n)"),
                                                 prod[:, :], ACT.Copy).then_inc(uhi_ready, 1)

                    with act.Fori(0, n // 2) as i:
                        up(i)
                    s0 = DOWN[l][g]
                    if g < 2:
                        with act.Fori(0, 2) as i:
                            for c in range(4):
                                s = s0 + c + 2
                                split_hi(i * 4 + s, s % 4, i + (s // 4 + 1))
                        continue
                    for m in range(KD):
                        s = s0 + m
                        split_hi(s + 2)
                        if l == 0:
                            act.wait_ge(acc_free, s + 1)
                            square(xT[:, m, :])
                            scaled_hi(xa_hi, m, xT[:, m, :], pcol("norm_kv", m), xg_hi)
                        elif m >= 1:
                            y_rows(m - 1)
                    if l:
                        y_rows(KD - 1)
                    else:
                        root(T)

            def y_rows(m):
                act.wait_ge(y_T, m + 1)
                if m >= 2:
                    act.wait_ge(st_y[m % 2], 16 * (m // 2))
                nc.scalar.activation(ynat[:, m % 2, :, :].rearrange("p i n -> p (i n)"), psT[:, m % 2, :], ACT.Copy
                                     ).then_inc(y_c, 1)
                if m == KD - 1:
                    for g in range(2):
                        nc.scalar.activation(ysam[:, g * 512:(g + 1) * 512], psX[0:NSA, g, :], ACT.Copy).then_inc(y_c, 1)

            def ffn_tail(l):
                act.wait_ge(ft_T, l + 1)
                if l:
                    act.wait_ge(st_ft, 32)
                nc.scalar.activation(fout[0:4 * FC, 0:4, :].rearrange("p i n -> p (i n)"), psT[0:4 * FC, 0, :],
                                     ACT.Copy).then_inc(act_self, 1)
                nc.scalar.activation(fout[0:2 * FC, 4, :], psT[0:2 * FC, 1, 0:P], ACT.Copy).then_inc(ft_c, 1)
                own[0] += 1

            act.wait_ge(st_cs, 32)
            act.wait_ge(st_mk, 32)
            out_section(0, "norm_ffn")
            ffn(0)
            ffn_tail(0)

            act.wait_ge(st_ft, 32)
            act.wait_ge(mm_done, S_B)
            for c in range(KD):
                scaled_hi(xb_hi, c, xT[:, c, :], pcol("norm_mix", 8 + c), xb_h)

            def attend(what, n):
                i = n % QB
                L = (i + 1) * P
                if what == "S":
                    act.wait_ge(at_nb, n + 1)
                    for c in range(2):
                        last = nc.scalar.activation(et[:, c, 0:L], psX[:, c, 0:L], ACT.Exp, bias=stat[:, n % 2, 2 + c:3 + c],
                                                    scale=ISQ, accum_out=stat[:, n % 2, 4 + c:5 + c])
                    last.then_inc(at_exp, 1)
                elif what == "T":
                    act.wait_ge(at_T, n + 1)
                    if n:
                        act.wait_ge(at_pv, n)
                    nc.scalar.activation(pTt[:, 0:i + 1, :].rearrange("p i n -> p (i n)"), psT[:, 0, 0:L], ACT.Copy
                                         ).then_inc(at_aT, 1)

            def react(b):
                for what, n in beat(b):
                    attend(what, n)

            for s in range(S_B, S_B + 20):
                b0 = 4 * (s + 1 - S_B)
                tile_sq(s)
                react(b0)
                split_hi(s + 2)
                react(b0 + 1)
                tile_end(s)
                react(b0 + 2)
                react(b0 + 3)
            for b_ in range(84, LAST_BEAT + 1):
                react(b_)
            for h in range(H):
                act.wait_ge(kn_T, h + 1)
                nc.scalar.activation(knat[:, :, h * P:(h + 1) * P], psT[:, h % 2, :].rearrange("p (i n) -> p i n", n=P),
                                     ACT.Copy).then_inc(kn_c, 1)
            nc.scalar.activation(knsam[:, 0:512], psX[0:NSA, 0, :], ACT.Copy).then_inc(act_self, 1)
            nc.scalar.activation(knsam[:, 512:CA], psX[0:NSA, 1, 0:256], ACT.Copy).then_inc(kn_c, 1)

            for g in range(DB // 2):
                for b2 in range(2):
                    b_ = 2 * g + b2
                    for q in range(3):
                        u = 3 * b_ + q
                        act.wait_ge(ds_T, u + 1)
                        if q == 0 and b_:
                            act.wait_ge(ds_S, b_)
                        nc.scalar.activation(kTs[:, 2 * q:2 * q + 2, 0:PAST],
                                             psT[:, u % 2, :].rearrange("p (h n) -> p h n", h=2), ACT.Copy).then_inc(ds_kc, 1)
                act.wait_ge(ds_nb, g + 1)
                if g:
                    act.wait_ge(ds_A, g)
                nc.scalar.activation(exps[:, :], psX[:, 0, 0:NKEY], ACT.Exp, bias=stat[:, 0, 2:3], scale=ISQ,
                                     accum_out=stat[:, 0, 4:5]).then_inc(ds_exp, 1)
            act.wait_ge(ds_row, 1)
            nc.scalar.activation(orow[:, 0:512], acc[0][0:NSA, 0, :], ACT.Copy).then_inc(act_self, 1)
            nc.scalar.activation(orow[:, 512:CA], acc[0][0:NSA, 1, 0:256], ACT.Copy).then_inc(ds_rc, 1)

            mem_attention(1)
            mem_sample(1)
            mix_hi(1, mT2)
            for h in range(H):
                square(od[:, h, :])
            root(H * T)
            for h in range(H):
                act.wait_ge(ln_n, CC + h + 1)
                nc.scalar.activation(xb_hi[:, h, :], qf[:, h % 2, :], ACT.Copy).then_inc(cm_hi, 1)
            out_section(1, "norm_ffn")
            ffn(1)
            ffn_tail(1)

        @block.vector
        def _(dve):
            own = [0]

            def link(ins):
                own[0] = own[0] + 1
                ins.then_inc(dve_self, 1)

            def settle():
                dve.wait_ge(dve_self, own[0])

            def split_lo(s, slot=None):
                if slot is None:
                    if s >= STEPS:
                        return
                    slot = s % 4
                dve.wait_ge(w_hi_ready, s + 1)
                nc.vector.tensor_tensor(wlo[:, slot % 2, :], wraw[:, slot, :], whi[:, slot % 2, :].bitcast(F32),
                                        ALU.subtract).then_inc(w_lo_ready, 1)

            nrt, nturn = [0], [0]

            def root(src, n, scale, eps_, out, read=None, beside=None):
                k = nrt[0]
                nrt[0] += 1
                w = n // 32
                if read is None:
                    nturn[0] += 1
                    read = (turned, nturn[0])
                nc.vector.transpose(t1[:, 0:n], src).then_inc(read[0], 1)
                dve.wait_ge(*read)
                nc.vector.tensor_scalar(small[:, 0, 0:w], t1[:, 0:n].rearrange("p (a b) -> p a b", b=32)[:, :, 0],
                                        scale, eps_, ALU.mult, ALU.add).then_inc(var_ready, 1)
                if beside:
                    beside()
                dve.wait_ge(sd_ready, k + 1)
                link(nc.vector.reciprocal(small[:, 2, 0:w], small[:, 1, 0:w]))
                settle()
                link(nc.vector.transpose(out, small[:, 2, 0:w].unsqueeze(2).broadcast_to((P, w, 32))))
                settle()

            def scaled_lo(lo, hi, c, src, gain, hi_sem, lo_sem, n):
                dve.wait_ge(hi_sem, n)
                nc.vector.scalar_tensor_tensor(out=lo[:, c, :], in0=src, scalar=gain, in1=hi[:, c, :].bitcast(F32),
                                               op0=ALU.mult, op1=ALU.subtract).then_inc(lo_sem, 1)

            dve.wait_ge(setup_filled, 1)
            nc.vector.tensor_copy(pT[:, 0:NROW], psT[:, 0, 0:NROW]).then_inc(setup_drained, 1)
            dve.wait_ge(setup_filled, 2)
            nc.vector.tensor_copy(xT[:, :, NPR:T], psT[:, 1, 0:KD * NSA].rearrange("p (c n) -> p c n", n=NSA)
                                  ).then_inc(setup_drained, 1)
            dve.wait_ge(setup_drained, 2)
            for c in range(KD):
                dve.wait_ge(setup_filled, 3 + c)
                nc.vector.tensor_copy(xT[:, c, 0:NPR], psT[:, c % 2, :]).then_inc(setup_drained, 1)
            split_lo(0)
            for c in range(KD):
                scaled_lo(xa_lo, xa_hi, c, xT[:, c, :], pcol("norm_mix", c), xg_hi, xg_lo, c + 1)
            split_lo(1)
            dve.wait_ge(sq_used, 8)
            root(psX[:, :, 0:HT], T, 1.0 / D, EPS, rstd[:, :])

            dve.wait_ge(ld_lam, 16)
            link(nc.vector.tensor_tensor(lamin[:, 0, :], lamin[:, 0, :], lamin[:, 1, :], ALU.mult))
            link(nc.vector.tensor_tensor(lamin[:, 2, :], lamin[:, 2, :], lamin[:, 3, :], ALU.mult))
            settle()
            link(nc.vector.tensor_reduce(lamt[:, 0:1], lamin[:, 0, :], AX.X, ALU.add))
            nc.vector.tensor_reduce(lamt[:, 1:2], lamin[:, 2, :], AX.X, ALU.add).then_inc(lam_sum, 1)

            def from_acc(s, out, gain=None):
                n = cols_of(s)
                r = rstd if n == T else rstdM
                return nc.vector.tensor_tensor(flat2(out, n), psum2(acc[s % 2], n), flat2(r[:, 0:n], n), ALU.mult)

            cursor_, chunks_in = [0], [0]
            n_conv = TAPS * CC

            def conv(count):
                while count and cursor_[0] < n_conv:
                    q = cursor_[0]
                    pair, x = divmod(q, 2 * TAPS)
                    tap, j = x // 2, 2 * pair + x % 2
                    if chunks_in[0] < 2 * pair + 2:
                        return
                    w = pcol("conv_a_w", tap * CC + j)
                    o, x = convt[:, j, 0:NPR], uext[:, j, tap:tap + NPR]
                    if tap:
                        dve.wait_ge(conv_step, q - 1)
                        ins = nc.vector.scalar_tensor_tensor(out=o, in0=x, scalar=w, in1=o, op0=ALU.mult, op1=ALU.add)
                    else:
                        ins = nc.vector.tensor_scalar(o, x, w, pcol("conv_a_b", j), ALU.mult, ALU.add)
                    ins.then_inc(conv_step, 1)
                    cursor_[0] += 1
                    count -= 1

            def conv_sample(j):
                x = uext[:, j, CEXT:].rearrange("p (b t) -> p b t", t=SEXT)
                w0_ = col["conv_a_w"]
                w = pT[:, w0_:w0_ + TAPS * CC].rearrange("p (k c) -> p c k", c=CC)[:, j, :]
                for t in range(DS):
                    link(nc.vector.tensor_tensor(sprod[:, :, t, :], x[:, :, t:t + TAPS],
                                                 w.unsqueeze(1).broadcast_to((P, DB, TAPS)), ALU.mult))
                settle()
                o = convt[:, j, NPR:T]
                link(nc.vector.tensor_reduce(o, sprod[:, :, :, :].rearrange("p b t k -> p (b t) k"), AX.X, ALU.add))
                settle()
                link(nc.vector.tensor_scalar(o, o, pcol("conv_a_b", j), None, ALU.add))
                settle()

            def tile_take(s):
                kind, t, nq = tiles[s]
                dve.wait_ge(mm_done, s + 1)
                from_acc(s, qf[:, t % 2, 0:cols_of(s)]).then_inc(tile_ev, 1)

            def tile_norm(s):
                kind, t, nq = tiles[s]
                if kind == "v":
                    return
                n = cols_of(s)
                dve.wait_ge(sq_used, sq_index(s) + 1)

                root(psum2(acc[s % 2], n), n, 1.0 / MHD, EPS, rr[:, 0:n], read=(acc_free, s + 1),
                     beside=(lambda: conv(3)) if s < S_OUT[0] else None)
                if s < S_MEM:
                    out, gain = mq[:, s - 2 * CC, :], pcol("mem_q", 0)
                elif s < S_OUT[0]:
                    l, c = divmod(s - S_MEM, 4)
                    out, gain = memk[:, l, c, :], pcol("mem_k", l)
                elif s < S_B + 18:
                    h = (s - S_B) // 3
                    out, gain = (kT[:, h, :], pcol("k_norm")) if kind == "k" else (qT[:, h % 2, :], pcol("q_norm"))
                    if kind == "q" and h >= 2:
                        dve.wait_ge(at_S, QB * (h - 1))
                else:
                    out, gain = mq2[:, s - S_B - 18, :], pcol("mem_q", 1)
                nc.vector.scalar_tensor_tensor(out=out, in0=qf[:, t % 2, 0:n], scalar=gain, in1=rr[:, 0:n],
                                               op0=ALU.mult, op1=ALU.mult).then_inc(qk_done, 1)
                if kind == "q" and S_B <= s < S_B + 18:
                    dve.wait_ge(qk_done, nq + 1)
                    link(nc.vector.tensor_copy(qnew[:, (s - S_B) // 3, :], qT[:, (s - S_B) // 3 % 2, NPR:T]))

            dve.wait_ge(zeroed, 2)
            for s in range(0, S_MEM):
                if s in tiles:
                    tile_take(s)
                    split_lo(s + 2)
                    conv(5)
                    tile_norm(s)
                    conv(5)
                    continue
                dve.wait_ge(mm_done, s + 1)
                if s % 2 == 0:
                    from_acc(s, atile[:, :]).then_inc(acc_free, 1)
                    split_lo(s + 2)
                    conv(9)
                    continue
                j = s // 2
                from_acc(s, gtile[:, :]).then_inc(acc_free, 1)
                split_lo(s + 2)
                conv(7)
                dve.wait_ge(acc_free, s)
                dve.wait_ge(sig_ready, j + 1)
                link(nc.vector.tensor_tensor(uext[:, j, TAPS - 1:CEXT], atile[:, 0:NPR], stile[:, 0:NPR], ALU.mult))
                link(nc.vector.tensor_tensor(unew[:, j, :], atile[:, NPR:T], stile[:, NPR:T], ALU.mult))
                settle()
                link(nc.vector.tensor_copy(uext[:, j, CEXT:].rearrange("p (b t) -> p b t", t=SEXT)[:, :, TAPS - 1:],
                                           unew[:, j, :].rearrange("p (b t) -> p b t", t=DS)))
                settle()
                if s > 1:
                    chunks_in[0] += 1
                    conv_sample(j)
                    continue
                for jj in range(4):
                    dve.wait_ge(setup_filled, 11 + jj)
                    nc.vector.tensor_copy(memT[:, 2 * jj:2 * jj + 2, :], psT[:, jj % 2, :].rearrange("p (c n) -> p c n", n=MEM)
                                          ).then_inc(setup_drained, 1)
                for jj in range(CC):
                    dve.wait_ge(setup_filled, 15 + jj)
                    nc.vector.tensor_copy(uext[:, jj, CEXT:].rearrange("p (b t) -> p b t", t=SEXT)[:, :, 0:TAPS - 1],
                                          psT[:, jj % 2, 0:240].rearrange("p (b t) -> p b t", t=TAPS - 1)
                                          ).then_inc(setup_drained, 1)
                for g in range(2):
                    dve.wait_ge(setup_filled, 21 + g)
                    for l in range(2):
                        ins = nc.vector.tensor_copy(
                            stT[:, l * FC + g * 11:l * FC + (g + 1) * 11, :],
                            psT[:, g, 0:352].rearrange("p (j r) -> p j r", r=32)[:, :, l * 16:(l + 1) * 16])
                        if l == 0:
                            link(ins)
                        else:
                            ins.then_inc(setup_drained, 1)
                dve.wait_ge(setup_drained, 22)
                settle()
                chunks_in[0] = 1
                conv_sample(0)
                dve.wait_ge(sq_used, SQ["mem"] + KD)
                root(psX[:, 0, 0:MEM], MEM, 1.0 / D, EPS, rstdM[:, :])
                for l in range(2):
                    for c in range(KD):
                        scaled_lo(mg_lo[l], mg_hi[l], c, memT[:, c, :], pcol("norm_mem", 8 * l + c), mg_h, mg_l, 8 * l + c + 1)
            for s in range(S_MEM, S_OUT[0]):
                tile_take(s)
                split_lo(s + 2)
                tile_norm(s)
                conv(5)

            def softmax_weights(n, out):
                link(nc.vector.reciprocal(out, n))
                settle()

            def mem_attention(l, out):
                base = 8 * l

                def maxes(m):
                    dve.wait_ge(ma_S, base + m + 1)
                    for h in range(2):
                        link(nc.vector.tensor_reduce(stat[:, m % 2, h:h + 1], ma_bank(m, h), AX.X, ALU.max))
                    settle()
                    nc.vector.tensor_scalar(stat[:, m % 2, 2:4], stat[:, m % 2, 0:2], -ISQ, None, ALU.mult).then_inc(ma_nb, 1)

                def probs(m):
                    dve.wait_ge(ma_exp, base + m + 1)
                    softmax_weights(stat[:, m % 2, 4:6], stat[:, m % 2, 6:8])
                    for h in range(2):
                        e_ = et[:, m % 2, h * MEM:(h + 1) * MEM]
                        ins = nc.vector.tensor_scalar(e_, e_, stat[:, m % 2, 6 + h:7 + h], None, ALU.mult)
                        if h == 0:
                            link(ins)
                    ins.then_inc(ma_p, 1)

                def take(m):
                    c, tb = divmod(m, QB)
                    dve.wait_ge(ma_pv, base + m + 1)
                    for h in range(2):
                        r = slice(h * MHD, (h + 1) * MHD)
                        ins = nc.vector.tensor_copy(out[r, c, tb * P:(tb + 1) * P], psT[r, 1, h * P:(h + 1) * P])
                        if h == 0:
                            link(ins)
                    ins.then_inc(ma_o, 1)

                maxes(0)
                for m in range(8):
                    probs(m)
                    if m < 7:
                        maxes(m + 1)
                    if m:
                        take(m - 1)
                    if l == 0:
                        conv(4)
                take(7)

            def mem_sample(l, q, out):
                dve.wait_ge(qm_zero, l + 1)
                dve.wait_ge(qk_done, 2 if l == 0 else 20)
                for c in range(MC):
                    for h in range(2):
                        r = slice(h * MHD, (h + 1) * MHD)
                        x = (2 * c + h) * DS
                        ins = nc.vector.tensor_copy(qm[r, c, :].rearrange("p (b n) -> p b n", n=144)[:, :, x:x + DS],
                                                    q[r, c, NPR:T].rearrange("p (b t) -> p b t", t=DS))
                        if c + h < 2:
                            link(ins)
                ins.then_inc(qm_ready, 1)
                return

            def mem_sample_rest(l, out):
                dve.wait_ge(ms_S, 8 * l + DB)
                link(nc.vector.tensor_reduce(stat[:, 0, 0:1], ms_scores, AX.X, ALU.max))
                settle()
                nc.vector.tensor_scalar(stat[:, 0, 2:3], stat[:, 0, 0:1], -ISQ, None, ALU.mult).then_inc(mx_nb, 1)
                dve.wait_ge(mx_exp, l + 1)
                softmax_weights(stat[:, 0, 4:5], stat[:, 0, 6:7])
                nc.vector.tensor_scalar(et[:, 0, 0:MEM], et[:, 0, 0:MEM], stat[:, 0, 6:7], None, ALU.mult).then_inc(mx_p, 1)
                dve.wait_ge(mx_pv, l + 1)
                src = psX[:, 1, 0:DB * MC * 16].rearrange("p (b c x) -> p b c x", c=MC, x=16)
                for c in range(MC):
                    for h in range(2):
                        r = slice(h * MHD, (h + 1) * MHD)
                        x = (2 * c + h) * DS
                        ins = nc.vector.tensor_copy(out[r, c, NPR:T].rearrange("p (b t) -> p b t", t=DS),
                                                    src[r, :, c, x:x + DS])
                        if c + h < 2:
                            link(ins)
                ins.then_inc(mx_o, 1)

            def mix_lo(l, tile_):
                for c in range(MC):
                    dve.wait_ge(cm_hi, 8 * l + c + 1)
                    nc.vector.tensor_tensor(xb_lo[:, CC + c, :], tile_[:, c, :], xb_hi[:, CC + c, :].bitcast(F32),
                                            ALU.subtract).then_inc(cm_lo, 1)

            mem_sample(0, mq, mT)
            mem_attention(0, mT)
            conv(12)
            mem_sample_rest(0, mT)
            mix_lo(0, mT)
            conv(n_conv)

            dve.wait_ge(ln_m, 1)
            for j in range(CC):
                nc.vector.tensor_tensor(convt[:, j, :], convt[:, j, :], qf[:, 0, :], ALU.subtract).then_inc(ln_c, 1)
            dve.wait_ge(sq_used, SQ["ln"] + CC)
            dve.wait_ge(ln_c, CC)
            root(psX[:, :, 0:HT], T, 1.0 / CA, LN_EPS, rr[:, :])
            for j in range(CC):
                nc.vector.tensor_tensor(convt[:, j, :], convt[:, j, :], rr[:, :], ALU.mult).then_inc(ln_n, 1)
            for j in range(CC):
                dve.wait_ge(cm_hi, MC + j + 1)
                nc.vector.tensor_tensor(xb_lo[:, j, :], qf[:, 1, :], xb_hi[:, j, :].bitcast(F32), ALU.subtract
                                        ).then_inc(cm_lo, 1)

            def residual(s, m, slot=None):
                dve.wait_ge(mm_done, s + 1)
                b_ = s % 2 if slot is None else slot
                x = xT[:, bass.ds(m, 1), :].rearrange("p o (c n) -> p (o c) n", c=2)
                nc.vector.tensor_tensor(x, acc[b_][:, :, 0:HT], x, ALU.add).then_inc(acc_free, 1)

            def out_section(l, n, nth):
                link(nc.vector.memset(gext[:, :, 0:FTAPS - 1], 0.0))
                for m in range(KD):
                    s = S_OUT[l] + m
                    residual(s, m)
                    split_lo(s + 2)
                    scaled_lo(xa_lo, xa_hi, m, xT[:, m, :], pcol("norm_ffn", 8 * l + m), xg_hi, xg_lo, 8 * nth + m + 1)
                dve.wait_ge(sq_used, SQ[n] + KD)
                root(psX[:, :, 0:HT], T, 1.0 / D, EPS, rstd[:, :])

            def ffn(l):
                for g, (g0, n) in enumerate(GROUPS):
                    def up(i, s0=UP[l][g]):
                        for cc in range(2):
                            q = i * 2 + (l * FC + g0 + cc)
                            j = i * 2 + (g0 + cc)
                            s = i * 4 + (s0 + 2 * cc)
                            sc = s0 + 2 * cc
                            ext = gext[:, cc, :]
                            smp = ext[:, GEXT:].rearrange("p (b t) -> p b t", t=GS)
                            A = acc[sc % 2]
                            dve.wait_ge(mm_done, s + 1)
                            st = stT[:, bass.ds(q, 1), :].rearrange("p o (b r) -> p (o b) r", r=2)
                            link(nc.vector.tensor_copy(smp[:, :, 0:2], st))
                            link(nc.vector.tensor_tensor(ext[:, 2:2 + HT], A[:, 0, 0:HT], rstd[:, 0:HT], ALU.mult))
                            link(nc.vector.tensor_tensor(ext[:, 2 + HT:GEXT], A[:, 1, 0:NPR - HT], rstd[:, HT:NPR], ALU.mult))
                            nc.vector.tensor_tensor(smp[:, :, 2:GS], A[:, 1, NPR - HT:HT].rearrange("p (b t) -> p b t", t=DS),
                                                    rstd[:, NPR:T].rearrange("p (b t) -> p b t", t=DS), ALU.mult
                                                    ).then_inc(acc_free, 1)
                            split_lo(s + 2, (sc + 2) % 4)
                            dve.wait_ge(acc_free, s + 1)
                            settle()
                            o2 = gcv[:, NPR:T].rearrange("p (b t) -> p b t", t=DS)
                            for tap in range(FTAPS):
                                w = pcol_at("ffn_conv_w", i * 2 + ((l * FTAPS + tap) * FC + g0 + cc))
                                parts = ((gcv[:, 0:NPR], ext[:, tap:tap + NPR]), (o2, smp[:, :, tap:tap + DS]))
                                for k, (o, x) in enumerate(parts):
                                    if tap == 0:
                                        ins = nc.vector.tensor_scalar(o, x, w, None, ALU.mult)
                                    else:
                                        dve.wait_ge(dve_self, own[0] - 1)
                                        ins = nc.vector.scalar_tensor_tensor(out=o, in0=x, scalar=w, in1=o,
                                                                             op0=ALU.mult, op1=ALU.add)
                                    if tap == FTAPS - 1 and k == 1:
                                        ins.then_inc(conv_ready, 1)
                                    else:
                                        link(ins)
                            tail = gcol[:, :, bass.ds(j, 1)]
                            link(nc.vector.tensor_copy(tail[:, 0:16, :].rearrange("p (b r) o -> p b (r o)", r=2), smp[:, :, DS:GS]))
                            link(nc.vector.tensor_copy(tail[:, 16:18, :].rearrange("p r o -> p (r o)"), ext[:, NPR:GEXT]))
                            dve.wait_ge(mm_done, s + 2)
                            nc.vector.tensor_tensor(val[:, :].rearrange("p (c n) -> p c n", c=2), acc[(sc + 1) % 2][:, :, 0:HT],
                                                    rstd[:, :].rearrange("p (c n) -> p c n", c=2), ALU.mult
                                                    ).then_inc(acc_free, 1)
                            split_lo(s + 3, (sc + 3) % 4)
                            dve.wait_ge(acc_free, s + 2)
                            dve.wait_ge(gelu_ready, q + 1)
                            nc.vector.tensor_tensor(prod[:, :], val[:, :], gel[:, :], ALU.mult).then_inc(u_ready, 1)
                            dve.wait_ge(uhi_ready, q + 1)
                            hi, lo = (x[:, bass.ds(i * 2 + cc, 1), :].rearrange("p o n -> p (o n)") for x in (xb_hi, xb_lo))
                            nc.vector.tensor_tensor(lo, prod[:, :], hi.bitcast(F32), ALU.subtract).then_inc(ulo_ready, 1)
                        return

                    start = own[0]
                    up(0)
                    per = own[0] - start
                    with dve.Fori(1, n // 2) as i:
                        own[0] = i * per + start
                        up(i)
                    own[0] = start + per * (n // 2)
                    s0 = DOWN[l][g]
                    if g < 2:
                        with dve.Fori(0, 2) as i:
                            for c in range(4):
                                residual(i * 4 + (s0 + c), i * 4 + c, (s0 + c) % 2)
                                split_lo(i * 4 + (s0 + c + 2), (s0 + c + 2) % 4)
                        continue
                    for m in range(KD):
                        s = s0 + m
                        residual(s, m)
                        split_lo(s + 2)
                        if l == 0:
                            scaled_lo(xa_lo, xa_hi, m, xT[:, m, :], pcol("norm_kv", m), xg_hi, xg_lo, 16 + m + 1)
                    if l == 0:
                        dve.wait_ge(sq_used, SQ["n2"] + KD)
                        root(psX[:, :, 0:HT], T, 1.0 / D, EPS, rstd[:, :])

            out_section(0, "n1", 1)
            ffn(0)

            dve.wait_ge(st_ft, 32)
            dve.wait_ge(lam_exp, 1)
            link(nc.vector.tensor_tensor(lamt[:, 4:5], lamt[:, 3:4], lamt[:, 2:3], ALU.subtract))
            settle()
            link(nc.vector.tensor_scalar(lamt[:, 7:8], lamt[:, 4:5], -LAM_INIT, None, ALU.add))
            settle()
            link(nc.vector.memset(lamt[:, 6:7], 1.0))
            settle()
            link(nc.vector.tensor_copy(lamt[MHD:P, 6:7], lamt[MHD:P, 7:8]))
            for c in range(KD):
                scaled_lo(xb_lo, xb_hi, c, xT[:, c, :], pcol("norm_mix", 8 + c), xb_h, xb_l, c + 1)

            def attend(what, n):
                h, i = divmod(n, QB)
                L = (i + 1) * P
                if what == "S":
                    dve.wait_ge(at_S, n + 1)
                    mask = cst[:, C_MASK:C_MASK + P].unsqueeze(1).broadcast_to((P, 2, P))
                    link(nc.vector.tensor_tensor(psX[:, :, i * P:L], psX[:, :, i * P:L], mask, ALU.add))
                    settle()
                    link(nc.vector.tensor_reduce(stat[:, n % 2, 0:2], psX[:, :, 0:L], AX.X, ALU.max))
                    settle()
                    nc.vector.tensor_scalar(stat[:, n % 2, 2:4], stat[:, n % 2, 0:2], -ISQ, None, ALU.mult).then_inc(at_nb, 1)
                elif what == "N":
                    dve.wait_ge(at_exp, n + 1)
                    if n:
                        dve.wait_ge(at_T, n)
                    softmax_weights(stat[:, n % 2, 4:6], stat[:, n % 2, 6:8])
                    link(nc.vector.tensor_tensor(stat[:, n % 2, 7:8], stat[:, n % 2, 7:8], lamt[:, 7:8], ALU.mult))
                    link(nc.vector.tensor_scalar(prb[:, 0:L], et[:, 0, 0:L], stat[:, n % 2, 6:7], None, ALU.mult))
                    settle()
                    nc.vector.scalar_tensor_tensor(out=prb[:, 0:L], in0=et[:, 1, 0:L], scalar=stat[:, n % 2, 7:8],
                                                   in1=prb[:, 0:L], op0=ALU.mult, op1=ALU.add).then_inc(at_p, 1)
                elif what == "O":
                    dve.wait_ge(at_pv, n + 1)
                    nc.vector.tensor_copy(od[:, h, i * P:L], psT[:, 1, 0:P]).then_inc(at_O, 1)

            def react(b):
                for what, n in beat(b):
                    attend(what, n)
                for what, n in beat(b - 1):
                    if what == "S":
                        attend("N", n)

            for s in range(S_B, S_B + 20):
                b0 = 4 * (s + 1 - S_B)
                tile_take(s)
                react(b0)
                split_lo(s + 2)
                react(b0 + 1)
                tile_norm(s)
                react(b0 + 2)
                react(b0 + 3)
            for b_ in range(84, LAST_BEAT + 1):
                react(b_)

            dve.wait_ge(qk_done, 6 + 12)
            settle()
            nc.vector.tensor_copy(kTs[:, :, PAST:NKEY], kT[:, :, NPR:T]).then_inc(kn_ready, 1)
            dve.wait_ge(qp_zero, 1)
            for g in range(DB // 2):
                if g:
                    dve.wait_ge(ds_S, 2 * g)
                for c in range(2):
                    for b2 in range(2):
                        r = slice(c * MHD, (c + 1) * MHD)
                        x = c * 64 + b2 * DS
                        ins = nc.vector.tensor_copy(qpad[r, b2, :].rearrange("p (h n) -> p h n", n=136)[:, :, x:x + DS],
                                                    qnew[r, :, (2 * g + b2) * DS:(2 * g + b2 + 1) * DS])
                        if c + b2 < 2:
                            link(ins)
                ins.then_inc(qp_ready, 1)
                dve.wait_ge(ds_S, 2 * g + 2)
                new = psX[:, 0, PAST:NKEY]
                link(nc.vector.tensor_tensor(new, new, cst[:, C_NEW + g * NSA:C_NEW + (g + 1) * NSA], ALU.add))
                settle()
                link(nc.vector.tensor_reduce(stat[:, 0, 0:1], psX[:, 0, 0:NKEY], AX.X, ALU.max))
                settle()
                nc.vector.tensor_scalar(stat[:, 0, 2:3], stat[:, 0, 0:1], -ISQ, None, ALU.mult).then_inc(ds_nb, 1)
                dve.wait_ge(ds_exp, g + 1)
                softmax_weights(stat[:, 0, 4:5], stat[:, 0, 6:7])
                nc.vector.tensor_scalar(cs[:, :], cst[:, C_FOLD:C_FOLD + 48], stat[:, 0, 6:7], lamt[:, 6:7],
                                        ALU.mult, ALU.mult).then_inc(ds_p, 1)
                dve.wait_ge(ds_A, g + 1)
                if g:
                    dve.wait_ge(ds_pv, g)
                link(nc.vector.memset(apad[:, :, :, :, :], 0.0))
                settle()
                folded = psX[:, 1, 0:96].rearrange("p (k h b t) -> p k h b t", k=PAGES, h=H, t=DS)
                for b2 in range(2):
                    x = (2 * g + b2) * DS
                    link(nc.vector.tensor_copy(apad[:, b2, :, :, x:x + DS], folded[:, :, :, b2, :]))
                nc.vector.tensor_copy(anew[:, :, 2 * g * DS:2 * (g + 1) * DS],
                                      psX[0:NSA, 1, 96:144].rearrange("p (h n) -> p h n", h=H)).then_inc(ds_a, 1)
            dve.wait_ge(ds_rT, 1)
            nc.vector.tensor_copy(od[:, :, NPR:T], psX[:, 1, 0:H * NSA].rearrange("p (h n) -> p h n", h=H)).then_inc(ds_o, 1)

            mem_sample(1, mq2, mT2)
            mem_attention(1, mT2)
            mem_sample_rest(1, mT2)
            mix_lo(1, mT2)
            w = T // 32
            for h in range(H):
                dve.wait_ge(sq_used, SQ["sub"] + h + 1)
                t_ = (t1, rr)[h % 2]
                if h >= 2:
                    settle()
                nc.vector.transpose(t_[:, :], (psX, psT, acc[0], acc[1])[h % 4][:, :, 0:HT]).then_inc(turned, 1)
                nturn[0] += 1
                dve.wait_ge(turned, nturn[0])
                ins = nc.vector.tensor_scalar(small[:, 0, h * w:(h + 1) * w], t_[:, :].rearrange("p (a b) -> p a b", b=32)[:, :, 0],
                                              1.0 / VD, EPS, ALU.mult, ALU.add)
                if h < H - 1:
                    link(ins)
            ins.then_inc(var_ready, 1)
            nrt[0] += 1
            dve.wait_ge(sd_ready, nrt[0])
            link(nc.vector.reciprocal(small[:, 2, :], small[:, 1, :]))
            settle()
            link(nc.vector.tensor_scalar(small[:, 2, :], small[:, 2, :], 1.0 - LAM_INIT, None, ALU.mult))
            settle()
            for h in range(H):
                r_ = (t1, rr)[h % 2]
                link(nc.vector.transpose(r_[:, :], small[:, 2, h * w:(h + 1) * w].unsqueeze(2).broadcast_to((P, w, 32))))
                settle()
                nc.vector.scalar_tensor_tensor(out=qf[:, h % 2, :], in0=od[:, h, :], scalar=pcol("subln"), in1=r_[:, :],
                                               op0=ALU.mult, op1=ALU.mult).then_inc(ln_n, 1)
                dve.wait_ge(cm_hi, 8 + MC + h + 1)
                nc.vector.tensor_tensor(xb_lo[:, h, :], qf[:, h % 2, :], xb_hi[:, h, :].bitcast(F32), ALU.subtract
                                        ).then_inc(cm_lo, 1)
            out_section(1, "n3", 3)
            ffn(1)

        @block.gpsimd
        def _(pool):
            pool.memset(ones[:, :], 1.0).then_inc(zeroed, 1)
            pool.memset(uext[:, :, 0:TAPS - 1], 0.0).then_inc(zeroed, 1)
            pool.dma_start(ptab[:, :], a["page_table"].rearrange("(o b) p -> o (b p)", o=1)).then_inc(ld_pt, 16)
            pool.dma_start(a["s_conv_a"][0][:, 0:TAPS - 1 - DS, :], a["state_conv_a"][0][:, DS:, :]).then_inc(st_misc, 16)

            def cache_rows(which, l, b_):
                src = a[which][l][b_].rearrange("(m p) h d -> p m (h d)", p=P)
                return mcache[:, b_, :].rearrange("p (m n) -> p m n", n=MW), src

            def mem_cache_k(l):
                for b_ in range(DB):
                    pool.dma_start(*cache_rows("cache_mem_k", l, b_)).then_inc(mc_k, 16)

            def mem_cache_v(l):
                for b_ in range(DB):
                    pool.wait_ge(ms_T, DB * l + b_ + 1)
                    pool.dma_start(*cache_rows("cache_mem_v", l, b_)).then_inc(mc_v, 16)

            pool.wait_ge(mm_done, S_MEM)
            pool.memset(qm[:, :, :], 0.0).then_inc(qm_zero, 1)
            mem_cache_k(0)
            for l in range(2):
                pool.wait_ge(acc_free, S_MEM + 4 * l + 4)
                pool.dma_start(a["p_mem_v"][l][0].rearrange("(m p) h d -> p m (h d)", p=P), memv[:, l, :, :]).then_inc(st_mv, 16)
            for l in range(2):
                pool.wait_ge(mk_c, l + 1)
                pool.dma_start(a["p_mem_k"][l][0].rearrange("(m p) h d -> p m (h d)", p=P), mkn[:, :, :]).then_inc(st_mk, 16)
            mem_cache_v(0)
            pool.wait_ge(ct_c, 3)
            pool.dma_start(a["p_conv_a"][0][0], ctail[0:TAPS - 1, 0, :]).then_inc(st_cs, 16)
            pool.dma_start(a["s_conv_a"][0][:, TAPS - 1 - DS:, :], ctail[:, 1, :]).then_inc(st_cs, 16)

            def ffn_tail(l):
                pool.wait_ge(ft_c, l + 1)
                pool.dma_start(a["s_ffn_conv"][l].rearrange("b r (j n) -> (b r j) n", n=P).rearrange("(g p) n -> p g n", g=4),
                               fout[0:4 * FC, 0:4, :]).then_inc(st_ft, 16)
                pool.dma_start(a["p_ffn_conv"][l][0].rearrange("r (j n) -> (r j) n", n=P), fout[0:2 * FC, 4, :]).then_inc(st_ft, 16)

            ffn_tail(0)
            for h in range(H):
                pool.wait_ge(acc_free, S_B + 3 * h + 2)
                pool.dma_start(a["p_v"][0].rearrange("(i p) h d -> p i h d", p=P)[:, :, h, :], vnat[:, h % 2, :, :]
                               ).then_inc(st_v[h % 2], 16)
            pool.dma_start(a["s_v"].rearrange("b t h d -> (b t) (h d)"), vnew[:, :, :].rearrange("p h d -> p (h d)")
                           ).then_inc(st_misc, 16)
            pool.wait_ge(mm_done, S_B + 20)
            pool.memset(qpad[:, :, :], 0.0).then_inc(qp_zero, 1)
            pool.memset(qm[:, :, :], 0.0).then_inc(qm_zero, 1)
            pool.wait_ge(ld_pt, 16)

            def pages(dst, cache, b_, done):
                for pg in range(PAGES):
                    page = pool.value_load(ptab[0:1, b_ * PAGES + pg:b_ * PAGES + pg + 1], min_val=0,
                                           max_val=a[cache].shape[0] - 1)
                    pool.dma_start(dst[:, b_ % 2, pg, :],
                                   a[cache][bass.ds(page, 1)].rearrange("o p h d -> (o p) (h d)")).then_inc(done[b_ % 2], 16)

            for b_ in range(2):
                pages(kpg, "cache_k", b_, kp_ld)
                pages(vpg, "cache_v", b_, vp_ld)
            pool.wait_ge(kn_c, H + 1)
            pool.dma_start(a["p_k"][0].rearrange("(i p) h d -> p i (h d)", p=P), knat[:, :, :]).then_inc(st_kn, 16)
            pool.dma_start(a["s_k"].rearrange("b t h d -> (b t) (h d)"), knsam[:, :]).then_inc(st_kn, 16)
            for b_ in range(2, DB):
                pool.wait_ge(ds_T, 3 * (b_ - 2) + 3)
                pages(kpg, "cache_k", b_, kp_ld)
                if b_ == 2:
                    pool.wait_ge(st_kn, 32)
                    mem_cache_k(1)
                if b_ % 2:
                    pool.wait_ge(ds_pv, b_ // 2)
                    for b2 in (b_ - 1, b_):
                        pages(vpg, "cache_v", b2, vp_ld)
            mem_cache_v(1)
            for m in range(KD):
                pool.wait_ge(y_c, m + 1)
                pool.dma_start(a["y_prompt"][0].rearrange("(i p) n -> p i n", p=P)[:, :, m * P:(m + 1) * P],
                               ynat[:, m % 2, :, :]).then_inc(st_y[m % 2], 16)
            pool.wait_ge(y_c, KD + 2)
            pool.dma_start(a["y_sample"].rearrange("b t n -> (b t) n"), ysam[:, :]).then_inc(st_misc, 16)
            ffn_tail(1)
            for s_, n in ((st_mk, 32), (st_mv, 32), (st_misc, 48), (st_y[0], 8 * KD), (st_y[1], 8 * KD), (st_kn, 32), (st_ft, 64),
                          (st_cs, 32), (st_v[0], 48), (st_v[1], 48)):
                pool.wait_ge(s_, n)


_OUTS = {
    "y_prompt": (1, NPR, D), "y_sample": (DB, DS, D), "p_mem_k": (2, 1, MEM, MH, MHD), "p_mem_v": (2, 1, MEM, MH, MHD),
    "p_conv_a": (1, 1, TAPS - 1, CA), "p_ffn_conv": (2, 1, FTAPS - 1, FF), "p_k": (1, NPR, H, VD), "p_v": (1, NPR, H, VD),
    "s_conv_a": (1, DB, TAPS - 1, CA), "s_ffn_conv": (2, DB, FTAPS - 1, FF), "s_k": (DB, DS, H, VD), "s_v": (DB, DS, H, VD),
}


def constants():
    import numpy as np

    c = np.zeros((P, C_ALL), np.float32)
    r = np.arange(P)
    c[:, C_ID:C_ID + P] = r[:, None] == r[None, :]
    c[:, C_BLK:C_BLK + P] = r[:, None] // MHD == r[None, :] // MHD
    c[:, C_MASK:C_MASK + P] = np.where(r[None, :] <= r[:, None], 0.0, -1e30)
    for g in range(DB // 2):
        for row in range(P):
            j = row % 64
            if j < 48:
                b_, t = 2 * g + j // DS % 2, j % DS
                for col in range(NSA):
                    if col // DS != b_ or col % DS > t:
                        c[row, C_NEW + g * NSA + col] = -1e30
    for j in range(48):
        c[j, C_FOLD + j] = c[64 + j, C_FOLD + j] = 1.0
    return c


def kernel(**inputs):
    import numpy as np
    import concourse.bacc as bacc
    from concourse.bass_utils import run_bass_kernel_spmd

    nc = bacc.Bacc("TRN2", target_bir_lowering=False, num_devices=1)
    arrays, aps = {}, {}
    for name, x in list(inputs.items()) + [("consts", constants())]:
        x = np.ascontiguousarray(x)
        arrays[f"in_{name}"] = x
        aps[name] = nc.dram_tensor(f"in_{name}", x.shape, mybir.dt.from_np(x.dtype), kind="ExternalInput").ap()
    for name, shape in _OUTS.items():
        aps[name] = nc.dram_tensor(f"out_{name}", shape, F32, kind="ExternalOutput").ap()
    build(nc, aps)
    r = run_bass_kernel_spmd(nc, [arrays], core_ids=[0])
    return tuple(r.results[0][f"out_{name}"] for name in _OUTS)
```

```python
import math
from contextlib import ExitStack

import concourse.bass as bass
from concourse import mybir

F32 = mybir.dt.float32
F32R = mybir.dt.float32r
I32 = mybir.dt.int32
ALU = mybir.AluOpType
ACT = mybir.ActivationFunctionType
AX = mybir.AxisListType

P = 128
D = 1024
KD = D // P
NPR = 512
DB, DS = 8, 4
NSA = DB * DS
T = NPR + NSA
HT = T // 2
QB = NPR // P
MEM = 256
MB = MEM // P
MH, MHD = 4, 64
MW = MH * MHD
MC = MW // P
CA = D - MW
CC = CA // P
TAPS = 31
PE_TAPS = range(0, 30, 3)
NPT = len(PE_TAPS)
CEXT = TAPS - 1 + NPR
SEXT = TAPS - 1 + DS
H = 6
VD = 128
PAST = 256
PAGES = PAST // P
NKEY = PAST + NSA
FF = 2816
FC = FF // P
FTAPS = 3
GEXT = FTAPS - 1 + NPR
GS = FTAPS - 1 + DS
GROUPS = ((0, 8), (8, 8), (16, 6))
EPS, LN_EPS = 1e-6, 1e-5
LAM_INIT = 0.8 - 0.6 * math.exp(-0.3)
ISQ = MHD ** -0.5

S_IN = 0
S_MEM = S_IN + 2 * CC + MC
S_OUT = (S_MEM + 8, S_MEM + 8 + 8 + 68 + 20)
S_FFN = (S_OUT[0] + 8, S_OUT[1] + 8)
S_B = S_FFN[0] + 68
STEPS = S_FFN[1] + 68
UP = tuple(tuple(f + o for o in (0, 24, 48)) for f in S_FFN)
DOWN = tuple(tuple(f + o for o in (16, 40, 60)) for f in S_FFN)

C_ID, C_BLK, C_MASK, C_NEW, C_FOLD = 0, P, 2 * P, 3 * P, 4 * P
C_ALL = C_FOLD + 48


def build(nc, a):
    ctx = ExitStack()
    with ctx:
        def sem(name):
            return ctx.enter_context(nc.semaphore(name))

        cursor = [nc.sbuf_base + 31 & ~31]

        def place(name, shape, dt=F32, at=None):
            size = 4
            for n in shape[1:]:
                size *= n
            size = size + 31 & ~31
            if at is None:
                at = cursor[0]
                cursor[0] += size
            assert at + size <= nc.sbuf_usable_end, (name, at + size)
            h = nc.alloc_sbuf_tensor_at(name, shape, dt, offset=at)
            return h, at + size

        xT, _ = place("x_resid", [P, KD, T])
        regA = cursor[0]
        xa_hi, e = place("xa_hi", [P, KD, T], F32R)
        xa_lo, e = place("xa_lo", [P, KD, T], F32R)
        regB = cursor[0]
        xb_hi, _ = place("xb_hi", [P, KD, T], F32R)
        xb_lo, endB = place("xb_lo", [P, KD, T], F32R)
        wraw, _ = place("w_raw", [P, 4, KD * P])
        whi, _ = place("w_hi", [P, 2, KD * P], F32R)
        wlo, _ = place("w_lo", [P, 2, KD * P], F32R)
        pT, _ = place("params", [P, 512])
        cst, _ = place("consts", [P, C_ALL])
        ones, _ = place("ones", [P, P])
        stT, _ = place("ffn_state", [P, 2 * FC, 2 * DB])
        gcol, _ = place("gate_tail", [P, 2 * DB + 2, FC])
        unew, e = place("glu_new", [P, CC, NSA], at=cursor[0] - (4 * (2 * DB + 2) * FC + 31 & ~31))
        tap_lo, e = place("tap_lo", [P, TAPS * CC], at=e)
        assert e <= cursor[0]
        rstd, _ = place("rstd", [P, T])
        tap_hi, _ = place("tap_hi", [P, TAPS * CC], F32R, at=cursor[0])
        rstdM, _ = place("rstd_mem", [P, MEM])
        apad, _ = place("fold_padded", [P, 2, PAGES, H, NSA], at=cursor[0])
        sqt, _ = place("squares", [P, 2, T])
        qf, _ = place("tile_raw", [P, 2, T])
        t1, _ = place("turned", [P, T])
        total, _ = place("square_total", [P, T], at=cursor[0])
        rr, _ = place("root_row", [P, T])
        small, _ = place("small", [P, 3, H * T // 32])
        lamt, _ = place("lam", [P, 8])
        stat, _ = place("softmax_stats", [P, 2, 8])
        ptab, _ = place("page_table_sb", [1, 16], I32)
        w0 = cursor[0]
        gext, _ = place("gate_ext", [P, 2, GEXT + DB * GS])
        gcv, _ = place("gate_conv", [P, T])
        gel, _ = place("gelu", [P, T])
        val, _ = place("value", [P, T])
        prod, endW = place("product", [P, T])
        et, e = place("exps", [P, 2, 512], at=w0)
        anew, _ = place("fold_new", [NSA, H, NSA], at=e + 4 * 384)
        exps, _ = place("sample_exps", [P, NKEY], at=e)
        kTb, _ = place("mem_k_cache_t", [P, 2, MC, MEM], at=e)
        prb, e = place("probs", [P, 2, 512], at=e)
        pTt, e = place("probs_t", [P, 4, P], at=e)
        assert e <= endW
        memk, _ = place("mem_k", [P, 2, MC, MEM])
        memv, _ = place("mem_v", [P, 2, MB, MW])
        regC = cursor[0]
        uext, e = place("glu_ext", [P, CC, CEXT + DB * SEXT], at=regC)
        atile, _ = place("glu_a", [P, T], at=w0)
        gtile, _ = place("glu_g", [P, T], at=w0 + 4 * T)
        stile, _ = place("glu_s", [P, T], at=w0 + 8 * T)
        convt, eC = place("conv_out", [P, CC, T], at=e)
        rows, e1 = place("param_rows", [P, 4, P], at=e)
        frow, e1 = place("ffn_state_rows", [2 * 2 * DB, FF], at=e1)
        sprod, e2 = place("sample_tap_products", [P, DB, DS, TAPS], at=w0 + 12 * T)
        diag, e2 = place("tap_diagonals", [P, 2, 2, P], F32R, at=e2)
        assert e2 <= endW
        crow, e2 = place("conv_state_rows", [4 * (TAPS - 1), 2, CA], at=w0 + 12 * T)
        assert e2 <= endW
        e1 = max(e1, eC)
        memT, _ = place("mem_t", [P, KD, MEM], at=e1)
        cu_hi, e2 = place("glu_hi", [P, CEXT], F32R, at=e1)
        cu_lo, e2 = place("glu_lo", [P, CEXT], F32R, at=e2)
        mT, e3 = place("mem_mix", [P, MC, T], at=e1)
        e2 = max(e2, e3)
        mq, e2 = place("mem_q", [P, MC, T], at=e2)
        qT, e = place("diff_q", [P, 2, T], at=regC)
        mT2, _ = place("mem_mix_b", [P, MC, T], at=regC)
        qnew, e = place("diff_q_new", [P, H, NSA], at=e)
        kT, e = place("diff_k", [P, H, T], at=e)
        od, e = place("diff_o", [P, H, T], at=e)
        orow, _ = place("diff_o_rows", [NSA, CA], at=e)
        vnat, e = place("diff_v", [P, 2, QB, VD], at=e)
        vnew, e = place("diff_v_new", [NSA, H, VD], at=e)
        mq2, e = place("mem_q_b", [P, MC, T], at=e)
        cs, e = place("fold_scaled", [P, 48], at=e)
        mcache, e = place("mem_cache", [P, DB, MB * MW], at=regA)
        qm, e = place("mem_q_padded", [P, MC, DB * 144], at=e)
        ctail, _ = place("conv_tail", [NSA, 2, CA], at=e)
        qpad, e = place("diff_q_padded", [P, 2, 136 * H], at=e)
        mkn, e = place("mem_k_rows", [P, MB, MW], at=e)
        assert e <= regB
        knat, e = place("k_rows_out", [P, QB, CA], at=regA)
        knsam, e = place("k_rows_sample_out", [NSA, CA], at=e)
        assert e <= regA + 4 * DB * MB * MW
        xnat, e = place("x_rows", [P, 5, D], at=regB)
        mnat, e = place("mem_rows", [P, MB, D], at=e)
        assert e <= endB
        lamin, _ = place("lambdas_in", [P, 4, MHD], at=e)
        mg_hi, mg_lo = [], []
        at = regB
        for l in range(2):
            for part, lst in (("hi", mg_hi), ("lo", mg_lo)):
                h_, at = place(f"mem_g{l}_{part}", [P, KD, MEM], F32R, at=at)
                lst.append(h_)
        kpg, e = place("k_pages", [P, 2, PAGES, CA], at=regB)
        vpg, e = place("v_pages", [P, 2, PAGES, CA], at=e)
        kTs, e = place("k_pages_t", [P, H, NKEY], at=e)
        assert e <= endB
        fout, e = place("ffn_state_out", [P, 5, P], at=regC)
        ynat, e = place("y_rows_out", [P, 2, QB, P], at=e)
        ysam, _ = place("y_sample_out", [NSA, D], at=e)

        acc = [ctx.enter_context(nc.psum_tensor(f"acc{i}", [P, 2, 512], F32)) for i in range(2)]
        psX = ctx.enter_context(nc.psum_tensor("psX", [P, 2, 512], F32))
        psT = ctx.enter_context(nc.psum_tensor("psT", [P, 2, 512], F32))

        ld_const, ld_rows, ld_state, ld_mem = (sem(n) for n in ("ld_const", "ld_rows", "ld_state", "ld_mem"))
        ld_x = [sem(f"ld_x{i}") for i in range(2)]
        w_loaded = [sem(f"w_loaded{i}") for i in range(4)]
        w_hi_ready, w_lo_ready = sem("w_hi_ready"), sem("w_lo_ready")
        mm_done = sem("mm_done")
        acc_free = sem("acc_free")
        setup_filled, setup_drained = sem("setup_filled"), sem("setup_drained")
        zeroed = sem("zeroed")
        sq_ready, sq_used = sem("sq_ready"), sem("sq_used")
        turned, var_ready, sd_ready = sem("turned"), sem("var_ready"), sem("sd_ready")
        xg_hi, xg_lo, xb_h, xb_l = sem("xg_hi"), sem("xg_lo"), sem("xb_h"), sem("xb_l")
        mg_h, mg_l = sem("mg_h"), sem("mg_l")
        tile_ev, tile_pe, qk_done = sem("tile_ev"), sem("tile_pe"), sem("qk_done")
        sig_ready, conv_step = sem("sig_ready"), sem("conv_step")
        taps_hi, taps_lo, glu_ready, cu_h, cu_l, diag_ready, diag_used, taps_summed = (sem(n) for n in (
            "taps_hi", "taps_lo", "glu_ready", "glu_hi_ready", "glu_lo_ready", "diag_ready", "diag_used", "taps_summed"))
        conv_total = sem("conv_total")
        ln_mean, ln_m, ln_c, ln_n, ln_y = (sem(n) for n in ("ln_mean", "ln_m", "ln_c", "ln_n", "ln_y"))
        cm_hi, cm_lo = sem("cm_hi"), sem("cm_lo")
        ma_S, ma_nb, ma_exp, ma_p, ma_T, ma_aT, ma_pv, ma_o = (sem("ma_" + n) for n in (
            "scores", "max", "exp", "probs", "turned", "copied", "pv", "out"))
        mc_k, mc_v, qm_zero, qm_ready = sem("mc_k"), sem("mc_v"), sem("qm_zero"), sem("qm_ready")
        ms_T, ms_kc, ms_S = sem("ms_turned"), sem("ms_copied"), sem("ms_scores")
        mx_nb, mx_exp, mx_p, mx_T, mx_aT, mx_pv, mx_o = (sem("mx_" + n) for n in (
            "max", "exp", "probs", "turned", "copied", "pv", "out"))
        at_S, at_nb, at_exp, at_p, at_T, at_aT, at_pv, at_O = (sem("at_" + n) for n in (
            "scores", "max", "exp", "probs", "turned", "copied", "pv", "out"))
        kp_ld = [sem(f"kp_ld{i}") for i in range(2)]
        vp_ld = [sem(f"vp_ld{i}") for i in range(2)]
        ld_pt = sem("ld_pt")
        qp_zero, qp_ready, kn_ready = sem("qp_zero"), sem("qp_ready"), sem("kn_ready")
        ds_T, ds_kc, ds_S, ds_nb, ds_exp, ds_p, ds_A, ds_a, ds_pv, ds_row, ds_rc, ds_rT, ds_o = (sem("ds_" + n) for n in (
            "turned", "copied", "scores", "max", "exp", "probs", "folded", "fold_copied", "pv", "rows", "rows_copied",
            "rows_turned", "out"))
        sb_sq, sb_sum, sb_read = sem("sb_squared"), sem("sb_summed"), sem("sb_read")
        kn_T, kn_c = sem("kn_turned"), sem("kn_copied")
        mk_T, mk_c = sem("mk_turned"), sem("mk_copied")
        ct_T, ct_c = sem("ct_turned"), sem("ct_copied")
        conv_ready, gelu_ready, u_ready, uhi_ready, ulo_ready = (sem(n) for n in (
            "gate_conv_ready", "gelu_ready", "u_ready", "uhi_ready", "ulo_ready"))
        ft_T, ft_c = sem("ft_turned"), sem("ft_copied")
        y_T, y_c = sem("y_turned"), sem("y_copied")
        ld_lam, lam_sum, lam_exp = sem("ld_lam"), sem("lam_sum"), sem("lam_exp")
        dve_self, act_self = sem("dve_self"), sem("act_self")
        st_mk, st_mv, st_misc, st_kn, st_ft, st_cs = (sem(n) for n in (
            "st_mk", "st_mv", "st_misc", "st_kn", "st_ft", "st_cs"))
        st_ys = sem("st_y_last")
        st_y = [sem(f"st_y{i}") for i in range(2)]
        st_v = [sem(f"st_v{i}") for i in range(2)]

        ident = cst[:, C_ID:C_ID + P]
        blk = cst[:, C_BLK:C_BLK + P]

        col, put, nrow = {}, [], [0]

        def param(name, src, n):
            col[name] = nrow[0]
            done = 0
            while done < n:
                r = nrow[0] + done
                k = min(n - done, P - r % P)
                put.append((r, k, src, done))
                done += k
            nrow[0] += n

        param("norm_mix", a["norm_mix"].rearrange("l (c p) -> (l c) p", p=P), 16)
        param("norm_ffn", a["norm_ffn"].rearrange("l (c p) -> (l c) p", p=P), 16)
        param("norm_mem", a["norm_mem"].rearrange("l (c p) -> (l c) p", p=P), 16)
        param("norm_kv", a["norm_kv"].rearrange("(c p) -> c p", p=P), 8)
        param("conv_a_b", a["conv_a_b"].rearrange("l (c p) -> (l c) p", p=P), CC)
        param("ln_a_g", a["ln_a_g"].rearrange("l (c p) -> (l c) p", p=P), CC)
        param("ln_a_b", a["ln_a_b"].rearrange("l (c p) -> (l c) p", p=P), CC)
        param("conv_a_w", a["conv_a_w"].rearrange("l t (c p) -> (l t c) p", p=P), TAPS * CC)
        param("ffn_conv_w", a["ffn_conv_w"].rearrange("l t (c p) -> (l t c) p", p=P), 2 * FTAPS * FC)
        param("ffn_conv_b", a["ffn_conv_b"].rearrange("l (c p) -> (l c) p", p=P), 2 * FC)
        param("k_norm", a["k_norm"].rearrange("(o c) d -> o (c d)", o=1), 1)
        param("q_norm", a["q_norm"].rearrange("o c d -> o (c d)"), 1)
        param("subln", a["subln_g"], 1)
        param("mem_q", None, 2)
        param("mem_k", None, 2)
        NROW = nrow[0]

        def pcol(name, i=0, rows_=slice(0, P)):
            return pT[rows_, col[name] + i:col[name] + i + 1]

        def pcol_at(name, i):
            return pT[:, bass.ds(i + col[name], 1)]

        SQ = dict(n0=0, mem=8, tA=16, ln=22, n1=28, n2=36, tB=44, n3=58)
        RT = dict(n0=0, mem=1, ln=2, n1=3, n2=4, n3=5)

        PARAMS_AT = KD // 2

        tiles = {}
        for s in [S_MEM - 2, S_MEM - 1] + list(range(S_MEM, S_MEM + 8)) + list(range(S_B, S_B + 20)):
            if s < S_MEM:
                kind = "q"
            elif s < S_MEM + 8:
                kind = "k" if (s - S_MEM) % 4 < 2 else "v"
            else:
                kind = "kvq"[(s - S_B) % 3] if s < S_B + 18 else "q"
            nq = sum(1 for v in tiles.values() if v[0] != "v")
            tiles[s] = (kind, len(tiles), nq if kind != "v" else None)

        def sq_index(s):
            nq = tiles[s][2]
            return SQ["tA"] + nq if s < S_B else SQ["tB"] + nq - 6

        def cols_of(s):
            return MEM if S_MEM <= s < S_MEM + 8 else T

        def psum2(t, n):
            return t[:, :, 0:HT] if n == T else t[:, 0, 0:n]

        def ma_bank(m, h):
            return (psX[:, m % 2, 0:MEM], acc[m % 2][:, 0, 0:MEM])[h]

        ms_keys, ms_scores = acc[0][:, 1, :], acc[1][:, 1, 0:MEM]

        def flat2(ap, n):
            return ap.rearrange("p (c n) -> p c n", c=2) if n == T else ap

        def side_units(s):
            j, half = divmod(s - 4, 2)
            n = NPT // 2
            return [(j, i) for i in (range(n, NPT) if half else range(n))] if 0 <= j < CC else []

        conv_final = {}

        def tap_sum(j):
            return (psT, psX)[j % 2][:, :, 0:NPR // 2]

        block = ctx.enter_context(nc.Block())

        def beat(b):
            out = []
            for what, lag in (("S", 18), ("T", 22), ("O", 24)):
                n, r = divmod(b - lag, 3)
                if r == 0 and 0 <= n < H * QB:
                    out.append((what, n))
            return out

        SUB_HEADS = ((0, 1), (2, 3), (4,), (5,))
        KEY_ROWS_BEAT = 84

        def key_rows_sample(i):
            return acc[1 - i][0:NSA, 1, :]

        LAST_BEAT = 18 + 3 * (H * QB - 1) + 6

        @block.sync
        def _(sp):
            sp.dma_start(cst[:, :], a["consts"]).then_inc(ld_const, 16)
            x_rows = a["x_prompt"].rearrange("o (i p) n -> (o p) i n", p=P)
            sp.dma_start(xnat[0:NSA, QB, :], a["x_sample"].rearrange("b t n -> (b t) n")).then_inc(ld_x[0], 16)
            sp.dma_start(xnat[:, 0:QB, 0:512], x_rows[:, :, 0:512]).then_inc(ld_x[0], 16)
            for r, k, src, done in put:
                if src is not None:
                    sp.dma_start(rows[r % P:r % P + k, r // P, :], src[done:done + k, :]).then_inc(ld_rows, 16)
                    continue
            for name in ("mem_q", "mem_k"):
                r = col[name]
                assert r // P == (r + 1) // P
                for h in range(2):
                    sp.dma_start(rows[r % P:r % P + 2, r // P, h * MHD:(h + 1) * MHD],
                                 a[name + "_norm"]).then_inc(ld_rows, 16)
            sp.dma_start(xnat[:, 0:QB, 512:D], x_rows[:, :, 512:D]).then_inc(ld_x[1], 16)

            def load(s, src, kb=KD):
                if not isinstance(s, int) or s >= 4:
                    sp.wait_ge(w_lo_ready, s - 3)
                slot = s % 4 if isinstance(s, int) else slot_of[0]
                sp.dma_start(wraw[:, slot, 0:kb * P].rearrange("p (k n) -> p k n", n=P), src).then_inc(w_loaded[slot], 16)

            slot_of = [0]

            def block_cols(w, m, k0=0, kb=KD):
                return w[k0 * P:(k0 + kb) * P, m * P:(m + 1) * P].rearrange("(k p) n -> p k n", p=P)

            win, wmem = a["w_in_a"][0], a["w_mem_kv"]
            for s in range(S_IN, S_MEM):
                m = s // 2 + CC * (s % 2) if s < 2 * CC else s
                load(s, block_cols(win, m))
                if s == 1:
                    sp.dma_start(crow[0:120, :, :], a["state_conv_a"][0].rearrange("(g b) t n -> (b t) g n", g=2)
                                 ).then_inc(ld_state, 16)
                    sp.dma_start(frow[:, :], a["state_ffn_conv"].rearrange("l b r n -> (l b r) n")).then_inc(ld_state, 16)
                    sp.dma_start(lamin[:, :, :].rearrange("p c n -> p (c n)"),
                                 a["lambdas"].rearrange("o c n -> o (c n)").partition_broadcast(P)).then_inc(ld_lam, 16)
                    sp.dma_start(mnat[:, :, :], a["mem_prompt"].rearrange("o (i p) n -> (o p) i n", p=P)
                                 ).then_inc(ld_mem, 16)
            for s in range(S_MEM, S_OUT[0]):
                l, m = divmod(s - S_MEM, 4)
                load(s, block_cols(wmem[l], m))
            for l in range(2):
                wo = a["w_out_a"][0] if l == 0 else a["w_out_b"][0]
                for m in range(KD):
                    load(S_OUT[l] + m, block_cols(wo, m))
                for g, (g0, n) in enumerate(GROUPS):
                    with sp.Fori(0, n // 2) as i:
                        for c in range(4):
                            s = UP[l][g] + c
                            slot_of[0] = s % 4
                            first = g0 + c // 2 + FC * (c % 2)
                            src = a["w_up"][l][:, bass.ds(i * (2 * P) + first * P, P)].rearrange("(k p) n -> p k n", p=P)
                            load(i * 4 + s, src)
                    with sp.Fori(0, 2) as i:
                        for c in range(4):
                            s = DOWN[l][g] + c
                            slot_of[0] = s % 4
                            src = a["w_down"][l][g0 * P:(g0 + n) * P, bass.ds(i * (4 * P) + c * P, P)
                                                 ].rearrange("(k p) n -> p k n", p=P)
                            load(i * 4 + s, src, kb=n)
                if l == 0:
                    for h in range(H):
                        load(S_B + 3 * h, block_cols(a["w_kv"], h))
                        load(S_B + 3 * h + 1, block_cols(a["w_kv"], H + h))
                        load(S_B + 3 * h + 2, block_cols(a["w_in_b"][0], h))
                    for c in range(MC):
                        load(S_B + 18 + c, block_cols(a["w_in_b"][0], H + c))

            for m in range(KD - 2, KD):
                sp.wait_ge(y_c, m + 1)
                sp.dma_start(a["y_prompt"][0].rearrange("(i p) n -> p i n", p=P)[:, :, m * P:(m + 1) * P],
                             ynat[:, m % 2, :, :]).then_inc(st_ys, 16)
            sp.wait_ge(y_c, KD + 2)
            sp.dma_start(a["y_sample"].rearrange("b t n -> (b t) n"), ysam[:, :]).then_inc(st_ys, 16)

        @block.tensor
        def _(pe):
            def mm_step(s, slot, hi, lo, kb=KD, cols=T, ready=None, hooks=None):
                pe.wait_ge(w_lo_ready, s + 1)
                if not isinstance(s, int) or s >= 2:
                    pe.wait_ge(acc_free, s - 1)
                n, parts = (HT, 2) if cols == T else (cols, 1)
                for k in range(kb):
                    if ready:
                        ready(k)
                    wh, wl = whi[:, slot, k * P:(k + 1) * P], wlo[:, slot, k * P:(k + 1) * P]
                    for q, (w, x) in enumerate(((wh, hi), (wh, lo), (wl, hi))):
                        for c in range(parts):
                            last = nc.tensor.matmul(acc[slot][:, c, 0:n], w, x[:, k, c * n:(c + 1) * n],
                                                    start=(k == 0 and q == 0), stop=(k == kb - 1 and q == 2))
                    if k == kb - 1:
                        last.then_inc(mm_done, 1)
                    if hooks:
                        hooks(k)

            def square_sum(k, out, w, cols=T, first=True, final=True):
                pe.wait_ge(sq_ready, k + 1)
                n, parts = (HT, 2) if cols == T else (cols, 1)
                for c in range(parts):
                    last = nc.tensor.matmul(out[:, c, 0:n], w, sqt[:, k % 2, c * n:(c + 1) * n],
                                            start=first, stop=final)
                last.then_inc(sq_used, 1)

            def model_square_sum(norm, out=psX, chunks=KD):
                last = SQ[norm] + chunks - 1
                pe.wait_ge(sq_used, last)
                for c in range(2):
                    nc.tensor.matmul(out[:, c, 0:HT], ones[:, :], total[:, c * HT:(c + 1) * HT], start=True, stop=False)
                square_sum(last, out, ones[:, :], first=False)

            def tile_hook(s):
                kind, t, nq = tiles[s]
                if kind != "v":
                    square_sum(sq_index(s), acc[s % 2], blk, cols_of(s))
                    return
                pe.wait_ge(tile_ev, t + 1)
                src = qf[:, t % 2, :]
                if s < S_B:
                    for i in range(MB):
                        last = nc.tensor.transpose(acc[s % 2][:, 0, i * P:(i + 1) * P], src[:, i * P:(i + 1) * P], ident)
                else:
                    for i in range(QB):
                        nc.tensor.transpose(acc[s % 2][:, 0, i * P:(i + 1) * P], src[:, i * P:(i + 1) * P], ident)
                    last = nc.tensor.transpose(acc[s % 2][0:NSA, 1, 0:P], src[:, NPR:T], ident)
                last.then_inc(tile_pe, 1)

            pe.wait_ge(ld_const, 16)
            pe.wait_ge(zeroed, 1)

            def setup_bank(q):
                if q >= 2:
                    pe.wait_ge(setup_drained, q - 1)
                return psT[:, q % 2, :]

            pe.wait_ge(ld_x[0], 32)
            b = setup_bank(0)
            for c in range(KD):
                last = nc.tensor.transpose(b[:, c * NSA:(c + 1) * NSA], xnat[0:NSA, QB, c * P:(c + 1) * P],
                                           ident[0:NSA, 0:NSA])
            last.then_inc(setup_filled, 1)
            for c in range(KD):
                if c == PARAMS_AT:
                    pe.wait_ge(ld_rows, 16 * (sum(1 for x in put if x[2] is not None) + 4))
                    b = setup_bank(1 + c)
                    for i in range(4):
                        n = min(P, NROW - i * P)
                        last = nc.tensor.transpose(b[:, i * P:i * P + n], rows[0:n, i, :], ident[0:n, 0:n])
                    last.then_inc(setup_filled, 1)
                    pe.wait_ge(ld_x[1], 16)
                b = setup_bank(1 + c + (c >= PARAMS_AT))
                for i in range(QB):
                    last = nc.tensor.transpose(b[:, i * P:(i + 1) * P], xnat[:, i, c * P:(c + 1) * P], ident)
                last.then_inc(setup_filled, 1)
            def xa_ready(n):
                return lambda k: pe.wait_ge(xg_lo, 8 * n + k + 1)

            mm_step(0, 0, xa_hi, xa_lo, ready=xa_ready(0))
            model_square_sum("n0")
            mm_step(1, 1, xa_hi, xa_lo)
            pe.wait_ge(ld_mem, 16)
            for j in range(4):
                b = setup_bank(10 + j)
                for cc in range(2):
                    for m in range(MB):
                        last = nc.tensor.transpose(b[:, (cc * MB + m) * P:(cc * MB + m + 1) * P],
                                                   mnat[:, m, (2 * j + cc) * P:(2 * j + cc + 1) * P], ident)
                last.then_inc(setup_filled, 1)
            pe.wait_ge(ld_state, 32)
            for j in range(CC):
                b = setup_bank(14 + j)
                for g in range(2):
                    last = nc.tensor.transpose(b[:, g * 120:(g + 1) * 120], crow[0:120, g, j * P:(j + 1) * P],
                                               ident[0:120, 0:120])
                last.then_inc(setup_filled, 1)
            for g in range(2):
                b = setup_bank(20 + g)
                for j in range(11):
                    c = g * 11 + j
                    last = nc.tensor.transpose(b[:, j * 32:(j + 1) * 32], frow[:, c * P:(c + 1) * P], ident[0:32, 0:32])
                last.then_inc(setup_filled, 1)
            pe.wait_ge(turned, RT["n0"] + 1)
            for c in range(KD):
                square_sum(SQ["mem"] + c, psX, ones[:, :], MEM, first=(c == 0), final=(c == KD - 1))

            def conv_tail():
                pe.wait_ge(setup_drained, 22)
                for g in range(2):
                    for j in range(CC):
                        dst = ((psX, psT)[g][:, 0, j * P:(j + 1) * P] if j < 4 else
                               psX[:, 1, (2 * g + j - 4) * P:(2 * g + j - 3) * P])
                        dst, src = (dst[0:30, :], uext[:, j, NPR:CEXT]) if g == 0 else (dst[0:NSA, :], unew[:, j, :])
                        last = nc.tensor.transpose(dst, src, ident)
                last.then_inc(ct_T, 1)

            def memory_keys_out(l):
                pe.wait_ge(qk_done, 2 + 2 * (l + 1))
                for c in range(MC):
                    for m in range(MB):
                        last = nc.tensor.transpose(psT[:, l, m * MW + c * P:m * MW + (c + 1) * P],
                                                   memk[:, l, c, m * P:(m + 1) * P], ident)
                last.then_inc(mk_T, 1)

            def conv_unit(j, i):
                u = j * NPT + i
                if i == 0:
                    pe.wait_ge(cu_l, j + 1)
                    if j >= 2:
                        pe.wait_ge(taps_summed, j - 1)
                    else:
                        pe.wait_ge(setup_drained, 22)
                        pe.wait_ge(turned, RT["mem"] + 1)
                pe.wait_ge(diag_ready, u + 1)
                for q, (d, x) in enumerate(((0, cu_hi), (0, cu_lo), (1, cu_hi))):
                    for c in range(2):
                        at = PE_TAPS[i] + c * (NPR // 2)
                        last = nc.tensor.matmul(tap_sum(j)[:, c, :], diag[:, u % 2, d, :], x[:, at:at + NPR // 2],
                                                start=(i + q == 0), stop=(i == NPT - 1 and q == 2))
                last.then_inc(diag_used, 1)

            def beside(s, k):
                if k == 3 and s - 1 in tiles:
                    tile_hook(s - 1)
                todo = side_units(s)
                for j, i in (todo[k - 4:k - 3] if k < 7 else todo[3:]) if k >= 4 else ():
                    conv_unit(j, i)
                if (s, k) == (S_MEM + 3, 5):
                    pe.wait_ge(taps_summed, CC)
                    conv_tail()
                if (s, k) == (S_MEM + 4, 6):
                    pe.wait_ge(ct_c, 3)
                    memory_keys_out(0)
                if (s, k) == (S_MEM + 7, 6):
                    memory_keys_out(1)

            for s in range(2, S_MEM):
                mm_step(s, s % 2, xa_hi, xa_lo, hooks=lambda k, s=s: beside(s, k))
            for s in range(S_MEM, S_OUT[0]):
                l = (s - S_MEM) // 4
                mm_step(s, s % 2, mg_hi[l], mg_lo[l], cols=MEM,
                        ready=(lambda k, l=l: pe.wait_ge(mg_l, 8 * l + k + 1)) if (s - S_MEM) % 4 == 0 else None,
                        hooks=lambda k, s=s: beside(s, k))
            out_order = ([CC, CC + 1] + list(range(CC)), list(range(KD)))
            OUT_EARLY = (MC, CC)

            def out_part(l, m, parts):
                s = S_OUT[l] + m
                if parts[0] == 0:
                    pe.wait_ge(w_lo_ready, s + 1)
                    pe.wait_ge(acc_free, s - 1)
                for i in parts:
                    k = out_order[l][i]
                    if m == 0:
                        pe.wait_ge(cm_lo, 8 * l + i + 1)
                    wh, wl = whi[:, s % 2, k * P:(k + 1) * P], wlo[:, s % 2, k * P:(k + 1) * P]
                    for q, (w, x) in enumerate(((wh, xb_hi), (wh, xb_lo), (wl, xb_hi))):
                        for c in range(2):
                            last = nc.tensor.matmul(acc[s % 2][:, c, 0:HT], w, x[:, k, c * HT:(c + 1) * HT],
                                                    start=(i == 0 and q == 0), stop=(i == KD - 1 and q == 2))
                if parts[-1] == KD - 1:
                    last.then_inc(mm_done, 1)

            def mem_attention(l, q):
                base = 8 * l

                def scores(m):
                    c, tb = divmod(m, QB)
                    if m >= 2:
                        pe.wait_ge(ma_exp, base + m - 1)
                    for h in range(2):
                        r = slice(h * MHD, (h + 1) * MHD)
                        last = nc.tensor.matmul(ma_bank(m, h), q[r, c, tb * P:(tb + 1) * P],
                                                memk[r, l, c, :], start=True, stop=True)
                    last.then_inc(ma_S, 1)

                def turn(m):
                    pe.wait_ge(ma_p, base + m + 1)
                    if l == 0 and m == 0:
                        pe.wait_ge(mk_c, 2)
                    if m:
                        pe.wait_ge(ma_aT, base + m)
                    for x in range(4):
                        last = nc.tensor.transpose(psT[:, 0, x * P:(x + 1) * P], et[:, m % 2, x * P:(x + 1) * P], ident)
                    last.then_inc(ma_T, 1)

                def pv(m):
                    c = m // QB
                    pe.wait_ge(ma_aT, base + m + 1)
                    if m:
                        pe.wait_ge(ma_o, base + m)
                    for mb in range(MB):
                        last = nc.tensor.matmul(psT[:, 1, 0:2 * P], memv[:, l, mb, c * P:(c + 1) * P],
                                                pTt[:, mb:4:2, :], start=(mb == 0), stop=(mb == MB - 1))
                    last.then_inc(ma_pv, 1)

                def turn_cached(b_):
                    if b_ == 0:
                        pe.wait_ge(mc_k, 16 * DB * (l + 1))
                    else:
                        pe.wait_ge(ms_kc, base + b_)
                    for c in range(MC):
                        for m in range(MB):
                            last = nc.tensor.transpose(ms_keys[:, c * MEM + m * P:c * MEM + (m + 1) * P],
                                                       mcache[:, b_, m * MW + c * P:m * MW + (c + 1) * P], ident)
                    last.then_inc(ms_T, 1)

                def scores_cached(b_):
                    if b_ == 0:
                        pe.wait_ge(qm_ready, l + 1)
                    pe.wait_ge(ms_kc, base + b_ + 1)
                    for c in range(MC):
                        last = nc.tensor.matmul(ms_scores, qm[:, c, b_ * P:(b_ + 1) * P], kTb[:, b_ % 2, c, :],
                                                start=(b_ == 0 and c == 0), stop=(b_ == DB - 1 and c == MC - 1))
                    last.then_inc(ms_S, 1)

                pe.wait_ge(acc_free, S_OUT[l] - 1)
                scores(0)
                if l == 0:
                    tile_hook(S_OUT[0] - 1)
                pe.wait_ge(acc_free, S_OUT[l])
                for m in range(8):
                    if m < 7:
                        scores(m + 1)
                    turn_cached(m)
                    if m:
                        pv(m - 1)
                        scores_cached(m - 1)
                    turn(m)
                pv(7)
                scores_cached(DB - 1)
                pe.wait_ge(ma_o, base + 8)

            def mem_sample(l):
                if l:
                    out_part(1, 0, range(OUT_EARLY[1]))
                pe.wait_ge(mx_p, l + 1)
                for m in range(MB):
                    last = nc.tensor.transpose(psT[:, 0, m * P:(m + 1) * P], et[:, 0, m * P:(m + 1) * P], ident)
                last.then_inc(mx_T, 1)
                pe.wait_ge(mx_aT, l + 1)
                pe.wait_ge(mc_v, 16 * DB * (l + 1))
                for b_ in range(DB):
                    for c in range(MC):
                        for m in range(MB):
                            x = (b_ * MC + c) * 16
                            last = nc.tensor.matmul(psX[:, 1, x:x + 16], mcache[:, b_, m * MW + c * P:m * MW + (c + 1) * P],
                                                    pTt[:, m, b_ * 16:(b_ + 1) * 16], start=(m == 0), stop=(m == MB - 1))
                last.then_inc(mx_pv, 1)

            mem_attention(0, mq)
            pe.wait_ge(conv_total, CC - 1)
            for c in range(2):
                last = nc.tensor.matmul(acc[0][:, c, 0:HT], ones[:, :], total[:, c * HT:(c + 1) * HT], start=True, stop=True)
            last.then_inc(ln_mean, 1)
            mem_sample(0)

            pe.wait_ge(ln_m, 1)
            model_square_sum("ln", acc[0], CC)
            def out_section(l):
                n = OUT_EARLY[l]
                for m in range(KD):
                    out_part(l, m, range(n if m < 2 else 0, KD))

            def ffn(l, norm):
                def beside_down(m, k):
                    if (m, k) == (1, 1):
                        ffn_tail(l)
                    if k == 3 and m:
                        after_chunk(l, m - 1)

                for g, (g0, n) in enumerate(GROUPS):
                    s0 = UP[l][g]
                    for c in range(4):
                        mm_step(s0 + c, (s0 + c) % 2, xa_hi, xa_lo,
                                ready=xa_ready(norm) if g == 0 and c == 0 else None,
                                hooks=(lambda k: model_square_sum("n%d" % norm) if k == 3 else None) if g == 0 and c == 0 else None)
                    with pe.Fori(1, n // 2) as i:
                        for c in range(4):
                            mm_step(i * 4 + (s0 + c), (s0 + c) % 2, xa_hi, xa_lo)
                    s0 = DOWN[l][g]
                    if g < 2:
                        for c in range(4):
                            mm_step(s0 + c, (s0 + c) % 2, xb_hi, xb_lo, kb=n,
                                    ready=(lambda k: pe.wait_ge(ulo_ready, l * FC + g0 + k + 1)) if c == 0 else None)
                        with pe.Fori(1, 2) as i:
                            for c in range(4):
                                mm_step(i * 4 + (s0 + c), (s0 + c) % 2, xb_hi, xb_lo, kb=n)
                        continue
                    for m in range(KD):
                        mm_step(s0 + m, (s0 + m) % 2, xb_hi, xb_lo, kb=n,
                                ready=(lambda k: pe.wait_ge(ulo_ready, l * FC + g0 + k + 1)) if m == 0 else None,
                                hooks=lambda k, m=m: beside_down(m, k))
                    after_chunk(l, KD - 1)

            def after_chunk(l, m):
                if l == 0:
                    return
                pe.wait_ge(acc_free, DOWN[1][2] + m + 1)
                if m >= 2:
                    pe.wait_ge(y_c, m - 1)
                else:
                    pe.wait_ge(ft_c, 2)
                for i in range(QB):
                    nc.tensor.transpose(psT[:, m % 2, i * P:(i + 1) * P], xT[:, m, i * P:(i + 1) * P], ident)
                last = nc.tensor.transpose(psX[0:NSA, m // 4, (m % 4) * P:(m % 4 + 1) * P], xT[:, m, NPR:T], ident)
                last.then_inc(y_T, 1)

            def ffn_tail(l):
                for r in range(5):
                    n = 4 * FC if r < 4 else 2 * FC
                    last = nc.tensor.transpose(psT[0:n, r // 4, (r % 4) * P:(r % 4 + 1) * P],
                                               gcol[:, 4 * r:4 * r + n // FC, :], ident)
                last.then_inc(ft_T, 1)

            pe.wait_ge(turned, RT["ln"] + 1)
            for m in range(2):
                out_part(0, m, range(OUT_EARLY[0]))
            out_section(0)
            ffn(0, 1)

            def attend(what, n):
                h, i = divmod(n, QB)
                L = (i + 1) * P
                if what == "S":
                    if i == 0:
                        pe.wait_ge(qk_done, 6 + 2 * h + 2)
                    if n:
                        pe.wait_ge(at_exp, n)
                    else:
                        pe.wait_ge(turned, RT["n2"] + 1)
                    for c in range(2):
                        r = slice(c * MHD, (c + 1) * MHD)
                        last = nc.tensor.matmul(psX[:, c, 0:L], qT[r, h % 2, i * P:(i + 1) * P], kT[r, h, 0:L],
                                                start=True, stop=True)
                    last.then_inc(at_S, 1)
                elif what == "T":
                    pe.wait_ge(at_p, n + 1)
                    if n:
                        pe.wait_ge(at_aT, n)
                    for j in range(i + 1):
                        last = nc.tensor.transpose(psT[:, 0, j * P:(j + 1) * P], prb[:, n % 2, j * P:(j + 1) * P], ident)
                    last.then_inc(at_T, 1)
                else:
                    pe.wait_ge(at_aT, n + 1)
                    if n:
                        pe.wait_ge(at_O, n)
                    if i == 0:
                        pe.wait_ge(acc_free, S_B + 3 * h + 2)
                    for j in range(i + 1):
                        last = nc.tensor.matmul(psT[:, 1, 0:P], vnat[:, h % 2, j, :], pTt[:, j, :],
                                                start=(j == 0), stop=(j == i))
                    last.then_inc(at_pv, 1)

            pe.wait_ge(ft_c, 1)
            for s in range(S_B, S_B + 20):
                def hooks(k, s=s):
                    if k % 2 == 0:
                        for what, n in beat(4 * (s - S_B) + k // 2):
                            attend(what, n)
                    if k == 4 and s > S_B:
                        tile_hook(s - 1)
                    if k == 3 and s == S_B:
                        model_square_sum("n2")
                q_step = (s - S_B) % 3 == 2 or s >= S_B + 18
                hi, lo = (xb_hi, xb_lo) if q_step else (xa_hi, xa_lo)
                ready = xa_ready(2) if s == S_B else (lambda k: pe.wait_ge(xb_l, k + 1)) if s == S_B + 2 else None
                mm_step(s, s % 2, hi, lo, ready=ready, hooks=hooks)
            for b_ in range(80, LAST_BEAT + 1):
                if b_ == 82:
                    tile_hook(S_B + 19)
                for what, n in beat(b_):
                    attend(what, n)
                h = b_ - KEY_ROWS_BEAT
                if 0 <= h < H:
                    if h == 0:
                        pe.wait_ge(acc_free, S_OUT[1])
                    if h >= 2:
                        pe.wait_ge(kn_c, h - 1)
                    for i in range(QB):
                        nc.tensor.transpose(acc[h % 2][:, 0, i * P:(i + 1) * P], kT[:, h, i * P:(i + 1) * P], ident)
                    last = nc.tensor.transpose(key_rows_sample(h // 4)[:, (h % 4) * P:(h % 4 + 1) * P], kT[:, h, NPR:T], ident)
                    last.then_inc(kn_T, 1)

            def o_rows(h):
                return acc[0][0:NSA, h // 4, (h % 4) * VD:(h % 4 + 1) * VD]

            pe.wait_ge(acc_free, S_OUT[1])
            pe.wait_ge(kn_c, H + 1)
            pe.wait_ge(kn_ready, 1)
            def turn_pages(b_, q):
                if b_ >= DB:
                    return
                if q == 0:
                    pe.wait_ge(kp_ld[b_ % 2], 32 * (b_ // 2 + 1))
                u = 3 * b_ + q
                if u >= 2:
                    pe.wait_ge(ds_kc, u - 1)
                for hh in range(2):
                    for pg in range(PAGES):
                        last = nc.tensor.transpose(psT[:, u % 2, (hh * PAGES + pg) * P:(hh * PAGES + pg + 1) * P],
                                                   kpg[:, b_ % 2, pg, (2 * q + hh) * VD:(2 * q + hh + 1) * VD], ident)
                last.then_inc(ds_T, 1)

            def output_norm(i):
                pe.wait_ge(sb_sq, i + 1)
                if i >= 2:
                    pe.wait_ge(sb_read, i - 1)
                n = NPR if i < H else H * NSA
                nc.tensor.matmul(acc[1][:, i % 2, 0:n], ones[:, :], qf[:, i % 2, 0:n], start=True, stop=True
                                 ).then_inc(sb_sum, 1)

            for q in range(3):
                turn_pages(0, q)
            for g in range(DB // 2):
                for b2 in range(2):
                    b_ = 2 * g + b2
                    if b2:
                        turn_pages(b_, 1)
                        turn_pages(b_, 2)
                    else:
                        turn_pages(b_ + 1, 0)
                    pe.wait_ge(ds_kc, 3 * b_ + 3)
                    if b2 == 0:
                        pe.wait_ge(qp_ready, g + 1)
                        if g:
                            pe.wait_ge(ds_exp, g)
                    for h in range(H):
                        last = nc.tensor.matmul(psX[:, 0, 0:NKEY], qpad[:, b2, h * P:(h + 1) * P], kTs[:, h, :],
                                                start=(b2 == 0 and h == 0), stop=(b2 == 1 and h == H - 1))
                    last.then_inc(ds_S, 1)
                turn_pages(2 * g + 2, 0)
                turn_pages(2 * g + 2, 1)
                pe.wait_ge(ds_p, g + 1)
                for kb in range(PAGES):
                    nc.tensor.matmul(psX[:, 1, kb * 48:(kb + 1) * 48], exps[:, kb * P:(kb + 1) * P], cs[:, :],
                                     start=True, stop=True)
                last = nc.tensor.matmul(psX[0:NSA, 1, 96:144], exps[:, PAST:NKEY], cs[:, :], start=True, stop=True)
                last.then_inc(ds_A, 1)
                turn_pages(2 * g + 2, 2)
                pe.wait_ge(ds_a, g + 1)
                for b2 in range(2):
                    pe.wait_ge(vp_ld[b2], 32 * (g + 1))
                    for h in range(H):
                        for pg in range(PAGES):
                            last = nc.tensor.matmul(o_rows(h), apad[:, b2, pg, h, :], vpg[:, b2, pg, h * VD:(h + 1) * VD],
                                                    start=(g + b2 + pg == 0 and h % 4 == 0), stop=False)
                last.then_inc(ds_pv, 1)
                for i in SUB_HEADS[g]:
                    output_norm(i)
            for h in range(H):
                last = nc.tensor.matmul(o_rows(h), anew[:, h, :], vnew[:, h, :], start=False, stop=h in (3, H - 1))
            last.then_inc(ds_row, 1)
            pe.wait_ge(ds_rc, 1)
            for h in range(H):
                last = nc.tensor.transpose(psX[:, 1, h * NSA:(h + 1) * NSA], orow[:, h * VD:(h + 1) * VD],
                                           ident[0:NSA, 0:NSA])
            last.then_inc(ds_rT, 1)

            output_norm(H)
            pe.wait_ge(sb_read, H + 1)
            mem_attention(1, mq2)
            mem_sample(1)
            out_part(1, 1, range(OUT_EARLY[1]))
            out_section(1)
            ffn(1, 3)

        @block.scalar
        def _(act):
            own = [0]

            def split_hi(s, slot=None, loads=None):
                if slot is None:
                    if s >= STEPS:
                        return
                    slot, loads = s % 4, s // 4 + 1
                act.wait_ge(w_loaded[slot], loads * 16)
                if not isinstance(s, int) or s >= 2:
                    act.wait_ge(mm_done, s - 1)
                nc.scalar.activation(whi[:, slot % 2, :], wraw[:, slot, :], ACT.Copy).then_inc(w_hi_ready, 1)

            nsq = [0]

            def square(src, n=T):
                k = nsq[0]
                nsq[0] += 1
                if k >= 2:
                    act.wait_ge(sq_used, k - 1)
                nc.scalar.activation(sqt[:, k % 2, 0:n], src, ACT.Square).then_inc(sq_ready, 1)

            nrt = [0]

            def root(n):
                k = nrt[0]
                nrt[0] += 1
                w = n // 32
                act.wait_ge(var_ready, k + 1)
                nc.scalar.activation(small[:, 1, 0:w], small[:, 0, 0:w], ACT.Sqrt).then_inc(sd_ready, 1)

            def scaled_hi(dst, c, src, gain, s_):
                nc.scalar.activation(dst[:, c, :], src, ACT.Copy, scale=gain).then_inc(s_, 1)

            split_hi(0)
            split_hi(1)
            for c in range(KD):
                act.wait_ge(setup_drained, c + 2 + (c >= PARAMS_AT))
                square(xT[:, c, :])
                for cc in range(0 if c == PARAMS_AT else c, c + 1) if c >= PARAMS_AT else ():
                    scaled_hi(xa_hi, cc, xT[:, cc, :], pcol("norm_mix", cc), xg_hi)
            root(T)
            act.wait_ge(lam_sum, 1)
            nc.scalar.activation(lamt[:, 2:4], lamt[:, 0:2], ACT.Exp).then_inc(lam_exp, 1)

            def tile_sq(s):
                kind, t, nq = tiles[s]
                if kind != "v":
                    act.wait_ge(tile_ev, t + 1)
                    square(qf[:, t % 2, 0:cols_of(s)], cols_of(s))

            def tile_end(s):
                kind, t, nq = tiles[s]
                if kind != "v":
                    root(cols_of(s))
                    return
                act.wait_ge(tile_pe, sum(1 for v in tiles.values() if v[0] == "v" and v[1] <= t))
                if s < S_B:
                    l, c = (s - S_MEM) // 4, (s - S_MEM) % 2
                    src = acc[s % 2][:, 0, 0:MEM].rearrange("p (m n) -> p m n", n=P)
                    nc.scalar.activation(memv[:, l, :, c * P:(c + 1) * P], src, ACT.Copy).then_inc(acc_free, 1)
                    return
                h = (s - S_B) // 3
                if h >= 2:
                    act.wait_ge(st_v[h % 2], 16 * (h // 2))
                    act.wait_ge(at_pv, QB * (h - 1))
                nc.scalar.activation(vnew[:, h, :], acc[s % 2][0:NSA, 1, 0:P], ACT.Copy).then_inc(act_self, 1)
                own[0] += 1
                nc.scalar.activation(vnat[:, h % 2, :, :], acc[s % 2][:, 0, :].rearrange("p (i n) -> p i n", n=P),
                                     ACT.Copy).then_inc(acc_free, 1)

            def conv_parts(s):
                todo = side_units(s + 1)
                if todo and todo[0][1] == 0:
                    j = todo[0][0]
                    act.wait_ge(glu_ready, j + 1)
                    if j:
                        act.wait_ge(diag_used, NPT * j)
                    nc.scalar.activation(cu_hi[:, :], uext[:, j, 0:CEXT], ACT.Copy).then_inc(cu_h, 1)
                    if j == 0:
                        act.wait_ge(setup_drained, 20)
                        act.wait_ge(taps_lo, 1)
                return todo

            def diagonals(todo):
                for j, i in todo:
                    u = j * NPT + i
                    if u >= 2:
                        act.wait_ge(diag_used, u - 1)
                    c = PE_TAPS[i] * CC + j
                    nc.scalar.activation(diag[:, u % 2, 0, :], ident, ACT.Copy, scale=pcol("conv_a_w", c))
                    nc.scalar.activation(diag[:, u % 2, 1, :], ident, ACT.Copy, scale=tap_lo[:, c:c + 1]
                                         ).then_inc(diag_ready, 1)

            w0_ = col["conv_a_w"]
            nc.scalar.activation(tap_hi[:, :], pT[:, w0_:w0_ + TAPS * CC], ACT.Copy).then_inc(taps_hi, 1)
            for s in range(0, S_MEM):
                if s < 2 * CC and s % 2:
                    act.wait_ge(acc_free, s + 1)
                    nc.scalar.activation(stile[:, :], gtile[:, :], ACT.Sigmoid).then_inc(sig_ready, 1)
                if s in tiles:
                    tile_sq(s)
                split_hi(s + 2)
                todo = conv_parts(s)
                if s in tiles:
                    tile_end(s)
                diagonals(todo)
                if s == 1:
                    for c in range(KD):
                        act.wait_ge(setup_drained, 10 + c // 2 + 1)
                        square(memT[:, c, :], MEM)
                    root(MEM)
                    for l in range(2):
                        for c in range(KD):
                            nc.scalar.activation(mg_hi[l][:, c, :], memT[:, c, :], ACT.Copy,
                                                 scale=pcol("norm_mem", 8 * l + c)).then_inc(mg_h, 1)
            def memory_keys_out(l):
                act.wait_ge(mk_T, l + 1)
                if l:
                    act.wait_ge(st_mk, 16)
                nc.scalar.activation(mkn[:, :, :].rearrange("p m n -> p (m n)"), psT[:, l, :], ACT.Copy).then_inc(mk_c, 1)

            for s in range(S_MEM, S_OUT[0]):
                tile_sq(s)
                split_hi(s + 2)
                todo = conv_parts(s)
                tile_end(s)
                diagonals(todo)
                if s == S_MEM + 3:
                    act.wait_ge(ct_T, 1)
                    nc.scalar.activation(ctail[0:30, 0, 0:512], psX[0:30, 0, :], ACT.Copy).then_inc(ct_c, 1)
                    nc.scalar.activation(ctail[:, 1, 0:512], psT[0:NSA, 0, :], ACT.Copy).then_inc(ct_c, 1)
                    for g, n in ((0, 30), (1, NSA)):
                        ins = nc.scalar.activation(ctail[0:n, g, 512:CA], psX[0:n, 1, g * 256:(g + 1) * 256], ACT.Copy)
                    ins.then_inc(ct_c, 1)
                if s == S_MEM + 4:
                    memory_keys_out(0)

            memory_keys_out(1)

            def mem_attention(l):
                base = 8 * l

                def exps(m):
                    act.wait_ge(ma_nb, base + m + 1)
                    if m >= 2:
                        act.wait_ge(ma_T, base + m - 1)
                    for h in range(2):
                        last = nc.scalar.activation(et[:, m % 2, h * MEM:(h + 1) * MEM], ma_bank(m, h),
                                                    ACT.Exp, bias=stat[:, m % 2, 2 + h:3 + h], scale=ISQ,
                                                    accum_out=stat[:, m % 2, 4 + h:5 + h])
                    last.then_inc(ma_exp, 1)

                def copy(m):
                    act.wait_ge(ma_T, base + m + 1)
                    if m:
                        act.wait_ge(ma_pv, base + m)
                    nc.scalar.activation(pTt[:, :, :].rearrange("p m n -> p (m n)"), psT[:, 0, :], ACT.Copy).then_inc(ma_aT, 1)

                def copy_cached(b_):
                    act.wait_ge(ms_T, base + b_ + 1)
                    if b_ >= 2:
                        act.wait_ge(ms_S, base + b_ - 1)
                    nc.scalar.activation(kTb[:, b_ % 2, :, :].rearrange("p m n -> p (m n)"), ms_keys,
                                         ACT.Copy).then_inc(ms_kc, 1)

                exps(0)
                for m in range(8):
                    copy_cached(m)
                    if m < 7:
                        exps(m + 1)
                    copy(m)
                    if l and m < H:
                        act.wait_ge(ln_n, CC + m + 1)
                        nc.scalar.activation(xb_hi[:, m, :], qf[:, m % 2, :], ACT.Copy).then_inc(cm_hi, 1)

            def mem_sample(l):
                act.wait_ge(mx_nb, l + 1)
                nc.scalar.activation(et[:, 0, 0:MEM], ms_scores, ACT.Exp, bias=stat[:, 0, 2:3], scale=ISQ,
                                     accum_out=stat[:, 0, 4:5]).then_inc(mx_exp, 1)
                if l == 0:
                    act.wait_ge(ln_mean, 1)
                    nc.scalar.activation(qf[:, 0, :].rearrange("p (c n) -> p c n", c=2), acc[0][:, :, 0:HT], ACT.Copy,
                                         scale=1.0 / CA).then_inc(ln_m, 1)
                act.wait_ge(mx_T, l + 1)
                nc.scalar.activation(pTt[:, 0:2, :].rearrange("p m n -> p (m n)"), psT[:, 0, 0:MEM], ACT.Copy
                                     ).then_inc(mx_aT, 1)

            def mix_hi(l, tile_):
                act.wait_ge(mx_o, l + 1)
                for c in range(MC):
                    nc.scalar.activation(xb_hi[:, CC + c, :], tile_[:, c, :], ACT.Copy).then_inc(cm_hi, 1)

            mem_attention(0)
            mem_sample(0)
            for j in range(CC):
                act.wait_ge(ln_c, j + 1)
                square(convt[:, j, :])
            mix_hi(0, mT)
            root(T)
            for j in range(CC):
                act.wait_ge(ln_n, j + 1)
                if j >= 1:
                    act.wait_ge(cm_lo, MC + j)
                nc.scalar.activation(qf[:, 1, :], convt[:, j, :], ACT.Silu, bias=pcol("ln_a_b", j),
                                     scale=pcol("ln_a_g", j)).then_inc(ln_y, 1)
                act.wait_ge(ln_y, j + 1)
                nc.scalar.activation(xb_hi[:, j, :], qf[:, 1, :], ACT.Copy).then_inc(cm_hi, 1)

            def out_section(l, gain):
                for m in range(KD):
                    s = S_OUT[l] + m
                    split_hi(s + 2)
                    act.wait_ge(acc_free, s + 1)
                    square(xT[:, m, :])
                    scaled_hi(xa_hi, m, xT[:, m, :], pcol(gain, 8 * l + m), xg_hi)
                root(T)

            def ffn(l):
                for g, (g0, n) in enumerate(GROUPS):
                    def up(i, s0=UP[l][g]):
                        for cc in range(2):
                            q = i * 2 + (l * FC + g0 + cc)
                            s = s0 + 2 * cc
                            split_hi(i * 4 + (s + 2), (s + 2) % 4, i + ((s + 2) // 4 + 1))
                            act.wait_ge(conv_ready, q + 1)
                            nc.scalar.activation(gel[:, :], gcv[:, :], ACT.Gelu_apprx_tanh,
                                                 bias=pcol_at("ffn_conv_b", q)).then_inc(gelu_ready, 1)
                            split_hi(i * 4 + (s + 3), (s + 3) % 4, i + ((s + 3) // 4 + 1))
                            act.wait_ge(u_ready, q + 1)
                            nc.scalar.activation(xb_hi[:, bass.ds(i * 2 + cc, 1), :].rearrange("p o n -> p (o n)"),
                                                 prod[:, :], ACT.Copy).then_inc(uhi_ready, 1)

                    with act.Fori(0, n // 2) as i:
                        up(i)
                    s0 = DOWN[l][g]
                    if g < 2:
                        with act.Fori(0, 2) as i:
                            for c in range(4):
                                s = s0 + c + 2
                                split_hi(i * 4 + s, s % 4, i + (s // 4 + 1))
                        continue
                    for m in range(KD):
                        s = s0 + m
                        if m == 1:
                            ffn_tail(l)
                        split_hi(s + 2)
                        if l == 0:
                            act.wait_ge(acc_free, s + 1)
                            square(xT[:, m, :])
                            scaled_hi(xa_hi, m, xT[:, m, :], pcol("norm_kv", m), xg_hi)
                        if l and m >= 1:
                            y_rows(m - 1)
                    if l:
                        y_rows(KD - 1)
                    else:
                        root(T)

            def y_rows(m):
                act.wait_ge(y_T, m + 1)
                if m >= 2:
                    act.wait_ge(st_y[m % 2], 16 * (m // 2))
                nc.scalar.activation(ynat[:, m % 2, :, :].rearrange("p i n -> p (i n)"), psT[:, m % 2, :], ACT.Copy
                                     ).then_inc(y_c, 1)
                if m == KD - 1:
                    for g in range(2):
                        nc.scalar.activation(ysam[:, g * 512:(g + 1) * 512], psX[0:NSA, g, :], ACT.Copy).then_inc(y_c, 1)

            def ffn_tail(l):
                act.wait_ge(ft_T, l + 1)
                if l:
                    act.wait_ge(st_ft, 32)
                nc.scalar.activation(fout[0:4 * FC, 0:4, :].rearrange("p i n -> p (i n)"), psT[0:4 * FC, 0, :],
                                     ACT.Copy).then_inc(act_self, 1)
                nc.scalar.activation(fout[0:2 * FC, 4, :], psT[0:2 * FC, 1, 0:P], ACT.Copy).then_inc(ft_c, 1)
                own[0] += 1

            act.wait_ge(st_cs, 32)
            act.wait_ge(st_mk, 32)
            out_section(0, "norm_ffn")
            ffn(0)

            act.wait_ge(st_ft, 32)
            act.wait_ge(mm_done, S_B)
            for c in range(KD):
                scaled_hi(xb_hi, c, xT[:, c, :], pcol("norm_mix", 8 + c), xb_h)

            def attend(what, n):
                i = n % QB
                L = (i + 1) * P
                if what == "S":
                    act.wait_ge(at_nb, n + 1)
                    for c in range(2):
                        last = nc.scalar.activation(et[:, c, 0:L], psX[:, c, 0:L], ACT.Exp, bias=stat[:, n % 2, 2 + c:3 + c],
                                                    scale=ISQ, accum_out=stat[:, n % 2, 4 + c:5 + c])
                    last.then_inc(at_exp, 1)
                elif what == "T":
                    act.wait_ge(at_T, n + 1)
                    if n:
                        act.wait_ge(at_pv, n)
                    nc.scalar.activation(pTt[:, 0:i + 1, :].rearrange("p i n -> p (i n)"), psT[:, 0, 0:L], ACT.Copy
                                         ).then_inc(at_aT, 1)

            def react(b):
                for what, n in beat(b):
                    attend(what, n)

            for s in range(S_B, S_B + 20):
                b0 = 4 * (s + 1 - S_B)
                tile_sq(s)
                react(b0)
                split_hi(s + 2)
                react(b0 + 1)
                tile_end(s)
                react(b0 + 2)
                react(b0 + 3)
            for b_ in range(84, LAST_BEAT + 1):
                react(b_)
                h = b_ - KEY_ROWS_BEAT
                if 0 <= h < H:
                    act.wait_ge(kn_T, h + 1)
                    nc.scalar.activation(knat[:, :, h * P:(h + 1) * P], acc[h % 2][:, 0, :].rearrange("p (i n) -> p i n", n=P),
                                         ACT.Copy).then_inc(kn_c, 1)
            nc.scalar.activation(knsam[:, 0:512], key_rows_sample(0), ACT.Copy).then_inc(act_self, 1)
            nc.scalar.activation(knsam[:, 512:CA], key_rows_sample(1)[:, 0:256], ACT.Copy).then_inc(kn_c, 1)

            def output_square(i):
                if i >= 2:
                    act.wait_ge(sb_sum, i - 1)
                if i < H:
                    dst, src = qf[:, i % 2, 0:NPR], od[:, i, 0:NPR]
                    if i == 0:
                        act.wait_ge(at_O, H * QB)
                else:
                    act.wait_ge(ds_o, 1)
                    dst, src = qf[:, i % 2, 0:H * NSA].rearrange("p (h n) -> p h n", h=H), od[:, :, NPR:T]
                nc.scalar.activation(dst, src, ACT.Square).then_inc(sb_sq, 1)

            for g in range(DB // 2):
                for b2 in range(2):
                    b_ = 2 * g + b2
                    for q in range(3):
                        u = 3 * b_ + q
                        act.wait_ge(ds_T, u + 1)
                        if q == 0 and b_:
                            act.wait_ge(ds_S, b_)
                        nc.scalar.activation(kTs[:, 2 * q:2 * q + 2, 0:PAST],
                                             psT[:, u % 2, :].rearrange("p (h n) -> p h n", h=2), ACT.Copy).then_inc(ds_kc, 1)
                for h in SUB_HEADS[g]:
                    output_square(h)
                act.wait_ge(ds_nb, g + 1)
                if g:
                    act.wait_ge(ds_A, g)
                nc.scalar.activation(exps[:, :], psX[:, 0, 0:NKEY], ACT.Exp, bias=stat[:, 0, 2:3], scale=ISQ,
                                     accum_out=stat[:, 0, 4:5]).then_inc(ds_exp, 1)
            act.wait_ge(ds_row, 1)
            act.wait_ge(at_pv, H * QB)
            for i in range(2):
                act.wait_ge(st_v[i], 48)
            nc.scalar.activation(orow[:, 0:512], acc[0][0:NSA, 0, :], ACT.Copy).then_inc(act_self, 1)
            nc.scalar.activation(orow[:, 512:CA], acc[0][0:NSA, 1, 0:256], ACT.Copy).then_inc(ds_rc, 1)

            output_square(H)
            root(H * T)
            mem_attention(1)
            mem_sample(1)
            mix_hi(1, mT2)
            out_section(1, "norm_ffn")
            ffn(1)

        @block.vector
        def _(dve):
            own = [0]

            def link(ins):
                own[0] = own[0] + 1
                ins.then_inc(dve_self, 1)

            def settle():
                dve.wait_ge(dve_self, own[0])

            def split_lo(s, slot=None):
                if slot is None:
                    if s >= STEPS:
                        return
                    slot = s % 4
                dve.wait_ge(w_hi_ready, s + 1)
                nc.vector.tensor_tensor(wlo[:, slot % 2, :], wraw[:, slot, :], whi[:, slot % 2, :].bitcast(F32),
                                        ALU.subtract).then_inc(w_lo_ready, 1)

            nrt, nturn = [0], [0]

            def root(src, n, scale, eps_, out, read=None, beside=None):
                k = nrt[0]
                nrt[0] += 1
                w = n // 32
                if read is None:
                    nturn[0] += 1
                    read = (turned, nturn[0])
                nc.vector.transpose(t1[:, 0:n], src).then_inc(read[0], 1)
                dve.wait_ge(*read)
                nc.vector.tensor_scalar(small[:, 0, 0:w], t1[:, 0:n].rearrange("p (a b) -> p a b", b=32)[:, :, 0],
                                        scale, eps_, ALU.mult, ALU.add).then_inc(var_ready, 1)
                if beside:
                    beside()
                dve.wait_ge(sd_ready, k + 1)
                link(nc.vector.reciprocal(small[:, 2, 0:w], small[:, 1, 0:w]))
                settle()
                link(nc.vector.transpose(out, small[:, 2, 0:w].unsqueeze(2).broadcast_to((P, w, 32))))
                settle()

            def scaled_lo(lo, hi, c, src, gain, hi_sem, lo_sem, n):
                dve.wait_ge(hi_sem, n)
                nc.vector.scalar_tensor_tensor(out=lo[:, c, :], in0=src, scalar=gain, in1=hi[:, c, :].bitcast(F32),
                                               op0=ALU.mult, op1=ALU.subtract).then_inc(lo_sem, 1)

            dve.wait_ge(setup_filled, 1)
            nc.vector.tensor_copy(xT[:, :, NPR:T], psT[:, 0, 0:KD * NSA].rearrange("p (c n) -> p c n", n=NSA)
                                  ).then_inc(setup_drained, 1)
            for c in range(KD):
                if c == PARAMS_AT:
                    dve.wait_ge(setup_filled, 2 + c)
                    nc.vector.tensor_copy(pT[:, 0:NROW], psT[:, (1 + c) % 2, 0:NROW]).then_inc(setup_drained, 1)
                i = 1 + c + (c >= PARAMS_AT)
                dve.wait_ge(setup_filled, i + 1)
                nc.vector.tensor_copy(xT[:, c, 0:NPR], psT[:, i % 2, :]).then_inc(setup_drained, 1)
            dve.wait_ge(setup_drained, KD + 2)
            split_lo(0)
            for c in range(KD):
                scaled_lo(xa_lo, xa_hi, c, xT[:, c, :], pcol("norm_mix", c), xg_hi, xg_lo, c + 1)
            split_lo(1)
            dve.wait_ge(sq_used, 8)
            root(psX[:, :, 0:HT], T, 1.0 / D, EPS, rstd[:, :])

            dve.wait_ge(ld_lam, 16)
            link(nc.vector.tensor_tensor(lamin[:, 0, :], lamin[:, 0, :], lamin[:, 1, :], ALU.mult))
            link(nc.vector.tensor_tensor(lamin[:, 2, :], lamin[:, 2, :], lamin[:, 3, :], ALU.mult))
            settle()
            link(nc.vector.tensor_reduce(lamt[:, 0:1], lamin[:, 0, :], AX.X, ALU.add))
            nc.vector.tensor_reduce(lamt[:, 1:2], lamin[:, 2, :], AX.X, ALU.add).then_inc(lam_sum, 1)

            def from_acc(s, out, gain=None):
                n = cols_of(s)
                r = rstd if n == T else rstdM
                return nc.vector.tensor_tensor(flat2(out, n), psum2(acc[s % 2], n), flat2(r[:, 0:n], n), ALU.mult)

            cursor_, chunks_in = [0], [0]
            steps_, after = [0], [0] * CC
            begun, done_ = [False] * CC, [0] * CC
            mine = [t for t in range(TAPS) if t not in PE_TAPS]
            n_conv = len(mine) * CC

            def conv_op(j, ins):
                steps_[0] += 1
                after[j] = steps_[0]
                ins.then_inc(conv_step, 1)

            def conv(count):
                while count and cursor_[0] < n_conv:
                    open_ = [j for j in range(chunks_in[0]) if done_[j] < len(mine)][:2]
                    if not open_:
                        return
                    j = next((j for j in open_ if after[j] != steps_[0]), open_[0])
                    tap = mine[done_[j]]
                    done_[j] += 1
                    conv_final[j] = steps_[0] + 1
                    w = pcol("conv_a_w", tap * CC + j)
                    o, src = convt[:, j, 0:NPR], uext[:, j, tap:tap + NPR]
                    if begun[j]:
                        if after[j]:
                            dve.wait_ge(conv_step, after[j])
                        ins = nc.vector.scalar_tensor_tensor(out=o, in0=src, scalar=w, in1=o, op0=ALU.mult, op1=ALU.add)
                    else:
                        ins = nc.vector.tensor_scalar(o, src, w, pcol("conv_a_b", j), ALU.mult, ALU.add)
                        begun[j] = True
                    conv_op(j, ins)
                    cursor_[0] += 1
                    count -= 1

            def side_conv(s):
                todo = side_units(s + 1)
                if todo and todo[0][1] == 0:
                    j = todo[0][0]
                    dve.wait_ge(cu_h, j + 1)
                    nc.vector.tensor_tensor(cu_lo[:, :], uext[:, j, 0:CEXT], cu_hi[:, :].bitcast(F32), ALU.subtract
                                            ).then_inc(cu_l, 1)
                done = side_units(s - 1)
                if done and done[0][1]:
                    j = done[0][0]
                    dve.wait_ge(diag_used, NPT * (j + 1))
                    o = convt[:, j, 0:NPR].rearrange("p (c n) -> p c n", c=2)
                    if begun[j]:
                        dve.wait_ge(conv_step, after[j])
                        ins = nc.vector.tensor_tensor(o, tap_sum(j), o, ALU.add)
                    else:
                        ins = nc.vector.tensor_scalar(o, tap_sum(j), pcol("conv_a_b", j), None, ALU.add)
                        begun[j] = True
                    ins.then_inc(taps_summed, 1)
                    dve.wait_ge(taps_summed, j + 1)

            def conv_sample(j):
                x = uext[:, j, CEXT:].rearrange("p (b t) -> p b t", t=SEXT)
                w0_ = col["conv_a_w"]
                w = pT[:, w0_:w0_ + TAPS * CC].rearrange("p (k c) -> p c k", c=CC)[:, j, :]
                for t in range(DS):
                    link(nc.vector.tensor_tensor(sprod[:, :, t, :], x[:, :, t:t + TAPS],
                                                 w.unsqueeze(1).broadcast_to((P, DB, TAPS)), ALU.mult))
                settle()
                o = convt[:, j, NPR:T]
                link(nc.vector.tensor_reduce(o, sprod[:, :, :, :].rearrange("p b t k -> p (b t) k"), AX.X, ALU.add))
                settle()
                link(nc.vector.tensor_scalar(o, o, pcol("conv_a_b", j), None, ALU.add))
                settle()

            def tile_take(s):
                kind, t, nq = tiles[s]
                dve.wait_ge(mm_done, s + 1)
                from_acc(s, qf[:, t % 2, 0:cols_of(s)]).then_inc(tile_ev, 1)

            def tile_norm(s):
                kind, t, nq = tiles[s]
                if kind == "v":
                    return
                n = cols_of(s)
                dve.wait_ge(sq_used, sq_index(s) + 1)

                root(psum2(acc[s % 2], n), n, 1.0 / MHD, EPS, rr[:, 0:n], read=(acc_free, s + 1),
                     beside=(lambda: conv(3)) if s < S_OUT[0] else None)
                if s < S_MEM:
                    out, gain = mq[:, s - 2 * CC, :], pcol("mem_q", 0)
                elif s < S_OUT[0]:
                    l, c = divmod(s - S_MEM, 4)
                    out, gain = memk[:, l, c, :], pcol("mem_k", l)
                elif s < S_B + 18:
                    h = (s - S_B) // 3
                    out, gain = (kT[:, h, :], pcol("k_norm")) if kind == "k" else (qT[:, h % 2, :], pcol("q_norm"))
                    if kind == "q" and h >= 2:
                        dve.wait_ge(at_S, QB * (h - 1))
                else:
                    out, gain = mq2[:, s - S_B - 18, :], pcol("mem_q", 1)
                nc.vector.scalar_tensor_tensor(out=out, in0=qf[:, t % 2, 0:n], scalar=gain, in1=rr[:, 0:n],
                                               op0=ALU.mult, op1=ALU.mult).then_inc(qk_done, 1)
                if kind == "q" and S_B <= s < S_B + 18:
                    dve.wait_ge(qk_done, nq + 1)
                    link(nc.vector.tensor_copy(qnew[:, (s - S_B) // 3, :], qT[:, (s - S_B) // 3 % 2, NPR:T]))

            dve.wait_ge(taps_hi, 1)
            w0_ = col["conv_a_w"]
            nc.vector.tensor_tensor(tap_lo[:, :], pT[:, w0_:w0_ + TAPS * CC], tap_hi[:, :].bitcast(F32), ALU.subtract
                                    ).then_inc(taps_lo, 1)
            dve.wait_ge(zeroed, 2)
            for s in range(0, S_MEM):
                if s in tiles:
                    tile_take(s)
                    split_lo(s + 2)
                    conv(1)
                    side_conv(s)
                    tile_norm(s)
                    conv(5)
                    continue
                dve.wait_ge(mm_done, s + 1)
                if s % 2 == 0:
                    from_acc(s, atile[:, :]).then_inc(acc_free, 1)
                    split_lo(s + 2)
                    side_conv(s)
                    conv(8 if s > 2 else 3)
                    continue
                j = s // 2
                from_acc(s, gtile[:, :]).then_inc(acc_free, 1)
                split_lo(s + 2)
                conv(2 if s > 3 else 0)
                side_conv(s)
                conv(4 if s > 3 else 3)
                dve.wait_ge(acc_free, s)
                dve.wait_ge(sig_ready, j + 1)
                link(nc.vector.tensor_tensor(uext[:, j, TAPS - 1:CEXT], atile[:, 0:NPR], stile[:, 0:NPR], ALU.mult))
                link(nc.vector.tensor_tensor(unew[:, j, :], atile[:, NPR:T], stile[:, NPR:T], ALU.mult))
                settle()
                nc.vector.tensor_copy(uext[:, j, CEXT:].rearrange("p (b t) -> p b t", t=SEXT)[:, :, TAPS - 1:],
                                      unew[:, j, :].rearrange("p (b t) -> p b t", t=DS)).then_inc(glu_ready, 1)
                dve.wait_ge(glu_ready, j + 1)
                if s > 1:
                    chunks_in[0] += 1
                    conv_sample(j)
                    continue
                for jj in range(4):
                    dve.wait_ge(setup_filled, 11 + jj)
                    nc.vector.tensor_copy(memT[:, 2 * jj:2 * jj + 2, :], psT[:, jj % 2, :].rearrange("p (c n) -> p c n", n=MEM)
                                          ).then_inc(setup_drained, 1)
                for jj in range(CC):
                    dve.wait_ge(setup_filled, 15 + jj)
                    nc.vector.tensor_copy(uext[:, jj, CEXT:].rearrange("p (b t) -> p b t", t=SEXT)[:, :, 0:TAPS - 1],
                                          psT[:, jj % 2, 0:240].rearrange("p (b t) -> p b t", t=TAPS - 1)
                                          ).then_inc(setup_drained, 1)
                for g in range(2):
                    dve.wait_ge(setup_filled, 21 + g)
                    for l in range(2):
                        ins = nc.vector.tensor_copy(
                            stT[:, l * FC + g * 11:l * FC + (g + 1) * 11, :],
                            psT[:, g, 0:352].rearrange("p (j r) -> p j r", r=32)[:, :, l * 16:(l + 1) * 16])
                        if l == 0:
                            link(ins)
                        else:
                            ins.then_inc(setup_drained, 1)
                dve.wait_ge(setup_drained, 22)
                settle()
                chunks_in[0] = 1
                conv_sample(0)
                dve.wait_ge(sq_used, SQ["mem"] + KD)
                root(psX[:, 0, 0:MEM], MEM, 1.0 / D, EPS, rstdM[:, :])
                for l in range(2):
                    for c in range(KD):
                        scaled_lo(mg_lo[l], mg_hi[l], c, memT[:, c, :], pcol("norm_mem", 8 * l + c), mg_h, mg_l, 8 * l + c + 1)
            for s in range(S_MEM, S_OUT[0]):
                tile_take(s)
                split_lo(s + 2)
                side_conv(s)
                tile_norm(s)
                if s < S_OUT[0] - 1:
                    conv(4)

            def softmax_weights(sums, out):
                link(nc.vector.reciprocal(out, sums))
                settle()

            def mem_attention(l, out):
                base = 8 * l

                def maxes(m):
                    dve.wait_ge(ma_S, base + m + 1)
                    for h in range(2):
                        link(nc.vector.tensor_reduce(stat[:, m % 2, h:h + 1], ma_bank(m, h), AX.X, ALU.max))
                    settle()
                    nc.vector.tensor_scalar(stat[:, m % 2, 2:4], stat[:, m % 2, 0:2], -ISQ, None, ALU.mult).then_inc(ma_nb, 1)

                def probs(m):
                    dve.wait_ge(ma_exp, base + m + 1)
                    softmax_weights(stat[:, m % 2, 4:6], stat[:, m % 2, 6:8])
                    for h in range(2):
                        e_ = et[:, m % 2, h * MEM:(h + 1) * MEM]
                        ins = nc.vector.tensor_scalar(e_, e_, stat[:, m % 2, 6 + h:7 + h], None, ALU.mult)
                        if h == 0:
                            link(ins)
                    ins.then_inc(ma_p, 1)

                def take(m):
                    c, tb = divmod(m, QB)
                    dve.wait_ge(ma_pv, base + m + 1)
                    for h in range(2):
                        r = slice(h * MHD, (h + 1) * MHD)
                        ins = nc.vector.tensor_copy(out[r, c, tb * P:(tb + 1) * P], psT[r, 1, h * P:(h + 1) * P])
                        if h == 0:
                            link(ins)
                    ins.then_inc(ma_o, 1)

                maxes(0)
                for m in range(8):
                    probs(m)
                    if m < 7:
                        maxes(m + 1)
                    if m:
                        take(m - 1)
                    if l == 0:
                        conv(5)
                    else:
                        if 0 < m <= H:
                            output_lo(m - 1)
                        if m < H:
                            output_normed(m)
                take(7)

            def pad_queries(l, q):
                dve.wait_ge(qm_zero, l + 1)
                dve.wait_ge(qk_done, 2 if l == 0 else 20)
                for c in range(MC):
                    for h in range(2):
                        r = slice(h * MHD, (h + 1) * MHD)
                        x = (2 * c + h) * DS
                        ins = nc.vector.tensor_copy(qm[r, c, :].rearrange("p (b n) -> p b n", n=144)[:, :, x:x + DS],
                                                    q[r, c, NPR:T].rearrange("p (b t) -> p b t", t=DS))
                        if c + h < 2:
                            link(ins)
                ins.then_inc(qm_ready, 1)

            def mem_sample(l, out):
                dve.wait_ge(ms_S, 8 * l + DB)
                link(nc.vector.tensor_reduce(stat[:, 0, 0:1], ms_scores, AX.X, ALU.max))
                settle()
                nc.vector.tensor_scalar(stat[:, 0, 2:3], stat[:, 0, 0:1], -ISQ, None, ALU.mult).then_inc(mx_nb, 1)
                dve.wait_ge(mx_exp, l + 1)
                softmax_weights(stat[:, 0, 4:5], stat[:, 0, 6:7])
                nc.vector.tensor_scalar(et[:, 0, 0:MEM], et[:, 0, 0:MEM], stat[:, 0, 6:7], None, ALU.mult).then_inc(mx_p, 1)
                if l == 0:
                    dve.wait_ge(ln_m, 1)
                    for j in range(CC):
                        nc.vector.tensor_tensor(convt[:, j, :], convt[:, j, :], qf[:, 0, :], ALU.subtract).then_inc(ln_c, 1)
                dve.wait_ge(mx_pv, l + 1)
                src = psX[:, 1, 0:DB * MC * 16].rearrange("p (b c x) -> p b c x", c=MC, x=16)
                for c in range(MC):
                    for h in range(2):
                        r = slice(h * MHD, (h + 1) * MHD)
                        x = (2 * c + h) * DS
                        ins = nc.vector.tensor_copy(out[r, c, NPR:T].rearrange("p (b t) -> p b t", t=DS),
                                                    src[r, :, c, x:x + DS])
                        if c + h < 2:
                            link(ins)
                ins.then_inc(mx_o, 1)

            def mix_lo(l, tile_):
                for c in range(MC):
                    dve.wait_ge(cm_hi, 8 * l + (H if l else 0) + c + 1)
                    nc.vector.tensor_tensor(xb_lo[:, CC + c, :], tile_[:, c, :], xb_hi[:, CC + c, :].bitcast(F32),
                                            ALU.subtract).then_inc(cm_lo, 1)

            pad_queries(0, mq)
            mem_attention(0, mT)
            conv(n_conv)
            mem_sample(0, mT)
            mix_lo(0, mT)

            dve.wait_ge(sq_used, SQ["ln"] + CC)
            dve.wait_ge(ln_c, CC)
            root(acc[0][:, :, 0:HT], T, 1.0 / CA, LN_EPS, rr[:, :])
            for j in range(CC):
                nc.vector.tensor_tensor(convt[:, j, :], convt[:, j, :], rr[:, :], ALU.mult).then_inc(ln_n, 1)
            for j in range(CC):
                dve.wait_ge(cm_hi, MC + j + 1)
                nc.vector.tensor_tensor(xb_lo[:, j, :], qf[:, 1, :], xb_hi[:, j, :].bitcast(F32), ALU.subtract
                                        ).then_inc(cm_lo, 1)

            def residual(s, m, slot=None):
                dve.wait_ge(mm_done, s + 1)
                b_ = s % 2 if slot is None else slot
                x = xT[:, bass.ds(m, 1), :].rearrange("p o (c n) -> p (o c) n", c=2)
                nc.vector.tensor_tensor(x, acc[b_][:, :, 0:HT], x, ALU.add).then_inc(acc_free, 1)

            def out_section(l, n, nth):
                link(nc.vector.memset(gext[:, :, 0:FTAPS - 1], 0.0))
                for m in range(KD):
                    s = S_OUT[l] + m
                    residual(s, m)
                    split_lo(s + 2)
                    scaled_lo(xa_lo, xa_hi, m, xT[:, m, :], pcol("norm_ffn", 8 * l + m), xg_hi, xg_lo, 8 * nth + m + 1)
                dve.wait_ge(sq_used, SQ[n] + KD)
                root(psX[:, :, 0:HT], T, 1.0 / D, EPS, rstd[:, :])

            def ffn(l):
                for g, (g0, n) in enumerate(GROUPS):
                    def up(i, s0=UP[l][g]):
                        for cc in range(2):
                            q = i * 2 + (l * FC + g0 + cc)
                            j = i * 2 + (g0 + cc)
                            s = i * 4 + (s0 + 2 * cc)
                            sc = s0 + 2 * cc
                            ext = gext[:, cc, :]
                            smp = ext[:, GEXT:].rearrange("p (b t) -> p b t", t=GS)
                            A = acc[sc % 2]
                            dve.wait_ge(mm_done, s + 1)
                            st = stT[:, bass.ds(q, 1), :].rearrange("p o (b r) -> p (o b) r", r=2)
                            link(nc.vector.tensor_copy(smp[:, :, 0:2], st))
                            link(nc.vector.tensor_tensor(ext[:, 2:2 + HT], A[:, 0, 0:HT], rstd[:, 0:HT], ALU.mult))
                            link(nc.vector.tensor_tensor(ext[:, 2 + HT:GEXT], A[:, 1, 0:NPR - HT], rstd[:, HT:NPR], ALU.mult))
                            nc.vector.tensor_tensor(smp[:, :, 2:GS], A[:, 1, NPR - HT:HT].rearrange("p (b t) -> p b t", t=DS),
                                                    rstd[:, NPR:T].rearrange("p (b t) -> p b t", t=DS), ALU.mult
                                                    ).then_inc(acc_free, 1)
                            split_lo(s + 2, (sc + 2) % 4)
                            dve.wait_ge(acc_free, s + 1)
                            settle()
                            o2 = gcv[:, NPR:T].rearrange("p (b t) -> p b t", t=DS)
                            for tap in range(FTAPS):
                                w = pcol_at("ffn_conv_w", i * 2 + ((l * FTAPS + tap) * FC + g0 + cc))
                                parts = ((gcv[:, 0:NPR], ext[:, tap:tap + NPR]), (o2, smp[:, :, tap:tap + DS]))
                                for k, (o, x) in enumerate(parts):
                                    if tap == 0:
                                        ins = nc.vector.tensor_scalar(o, x, w, None, ALU.mult)
                                    else:
                                        dve.wait_ge(dve_self, own[0] - 1)
                                        ins = nc.vector.scalar_tensor_tensor(out=o, in0=x, scalar=w, in1=o,
                                                                             op0=ALU.mult, op1=ALU.add)
                                    if tap == FTAPS - 1 and k == 1:
                                        ins.then_inc(conv_ready, 1)
                                    else:
                                        link(ins)
                            tail = gcol[:, :, bass.ds(j, 1)]
                            link(nc.vector.tensor_copy(tail[:, 0:16, :].rearrange("p (b r) o -> p b (r o)", r=2), smp[:, :, DS:GS]))
                            link(nc.vector.tensor_copy(tail[:, 16:18, :].rearrange("p r o -> p (r o)"), ext[:, NPR:GEXT]))
                            dve.wait_ge(mm_done, s + 2)
                            nc.vector.tensor_tensor(val[:, :].rearrange("p (c n) -> p c n", c=2), acc[(sc + 1) % 2][:, :, 0:HT],
                                                    rstd[:, :].rearrange("p (c n) -> p c n", c=2), ALU.mult
                                                    ).then_inc(acc_free, 1)
                            split_lo(s + 3, (sc + 3) % 4)
                            dve.wait_ge(acc_free, s + 2)
                            dve.wait_ge(gelu_ready, q + 1)
                            nc.vector.tensor_tensor(prod[:, :], val[:, :], gel[:, :], ALU.mult).then_inc(u_ready, 1)
                            dve.wait_ge(uhi_ready, q + 1)
                            hi, lo = (x[:, bass.ds(i * 2 + cc, 1), :].rearrange("p o n -> p (o n)") for x in (xb_hi, xb_lo))
                            nc.vector.tensor_tensor(lo, prod[:, :], hi.bitcast(F32), ALU.subtract).then_inc(ulo_ready, 1)
                        return

                    start = own[0]
                    up(0)
                    per = own[0] - start
                    with dve.Fori(1, n // 2) as i:
                        own[0] = i * per + start
                        up(i)
                    own[0] = start + per * (n // 2)
                    s0 = DOWN[l][g]
                    if g < 2:
                        with dve.Fori(0, 2) as i:
                            for c in range(4):
                                residual(i * 4 + (s0 + c), i * 4 + c, (s0 + c) % 2)
                                split_lo(i * 4 + (s0 + c + 2), (s0 + c + 2) % 4)
                        continue
                    for m in range(KD):
                        s = s0 + m
                        residual(s, m)
                        split_lo(s + 2)
                        if l == 0:
                            scaled_lo(xa_lo, xa_hi, m, xT[:, m, :], pcol("norm_kv", m), xg_hi, xg_lo, 16 + m + 1)
                    if l == 0:
                        dve.wait_ge(sq_used, SQ["n2"] + KD)
                        root(psX[:, :, 0:HT], T, 1.0 / D, EPS, rstd[:, :])

            out_section(0, "n1", 1)
            ffn(0)

            dve.wait_ge(st_ft, 32)
            dve.wait_ge(lam_exp, 1)
            link(nc.vector.tensor_tensor(lamt[:, 4:5], lamt[:, 3:4], lamt[:, 2:3], ALU.subtract))
            settle()
            link(nc.vector.tensor_scalar(lamt[:, 7:8], lamt[:, 4:5], -LAM_INIT, None, ALU.add))
            settle()
            link(nc.vector.memset(lamt[:, 6:7], 1.0))
            settle()
            link(nc.vector.tensor_copy(lamt[MHD:P, 6:7], lamt[MHD:P, 7:8]))
            for c in range(KD):
                scaled_lo(xb_lo, xb_hi, c, xT[:, c, :], pcol("norm_mix", 8 + c), xb_h, xb_l, c + 1)

            def attend(what, n):
                h, i = divmod(n, QB)
                L = (i + 1) * P
                if what == "S":
                    dve.wait_ge(at_S, n + 1)
                    mask = cst[:, C_MASK:C_MASK + P].unsqueeze(1).broadcast_to((P, 2, P))
                    link(nc.vector.tensor_tensor(psX[:, :, i * P:L], psX[:, :, i * P:L], mask, ALU.add))
                    settle()
                    link(nc.vector.tensor_reduce(stat[:, n % 2, 0:2], psX[:, :, 0:L], AX.X, ALU.max))
                    settle()
                    nc.vector.tensor_scalar(stat[:, n % 2, 2:4], stat[:, n % 2, 0:2], -ISQ, None, ALU.mult).then_inc(at_nb, 1)
                elif what == "N":
                    dve.wait_ge(at_exp, n + 1)
                    if n >= 2:
                        dve.wait_ge(at_T, n - 1)
                    softmax_weights(stat[:, n % 2, 4:6], stat[:, n % 2, 6:8])
                    link(nc.vector.tensor_tensor(stat[:, n % 2, 7:8], stat[:, n % 2, 7:8], lamt[:, 7:8], ALU.mult))
                    link(nc.vector.tensor_scalar(prb[:, n % 2, 0:L], et[:, 0, 0:L], stat[:, n % 2, 6:7], None, ALU.mult))
                    settle()
                    nc.vector.scalar_tensor_tensor(out=prb[:, n % 2, 0:L], in0=et[:, 1, 0:L], scalar=stat[:, n % 2, 7:8],
                                                   in1=prb[:, n % 2, 0:L], op0=ALU.mult, op1=ALU.add).then_inc(at_p, 1)
                elif what == "O":
                    dve.wait_ge(at_pv, n + 1)
                    nc.vector.tensor_copy(od[:, h, i * P:L], psT[:, 1, 0:P]).then_inc(at_O, 1)

            def react(b):
                for what, n in beat(b):
                    attend(what, n)
                for what, n in beat(b - 1):
                    if what == "S":
                        attend("N", n)

            for s in range(S_B, S_B + 20):
                b0 = 4 * (s + 1 - S_B)
                tile_take(s)
                react(b0)
                split_lo(s + 2)
                react(b0 + 1)
                tile_norm(s)
                react(b0 + 2)
                react(b0 + 3)
            for b_ in range(84, LAST_BEAT + 1):
                react(b_)

            w = T // 32

            def output_var(i):
                n = NPR if i < H else H * NSA
                settle()
                dve.wait_ge(sb_sum, i + 1)
                nc.vector.transpose(t1[:, 0:n], acc[1][:, i % 2, 0:n]).then_inc(sb_read, 1)
                dve.wait_ge(sb_read, i + 1)
                vars_ = small[:, 0, :].rearrange("p (h x) -> p h x", x=w)
                dst = vars_[:, i, 0:w - 1] if i < H else vars_[:, :, w - 1]
                ins = nc.vector.tensor_scalar(dst, t1[:, 0:n].rearrange("p (a b) -> p a b", b=32)[:, :, 0],
                                              1.0 / VD, EPS, ALU.mult, ALU.add)
                if i < H:
                    link(ins)
                else:
                    ins.then_inc(var_ready, 1)

            dve.wait_ge(qk_done, 6 + 12)
            settle()
            nc.vector.tensor_copy(kTs[:, :, PAST:NKEY], kT[:, :, NPR:T]).then_inc(kn_ready, 1)
            dve.wait_ge(qp_zero, 1)
            for g in range(DB // 2):
                if g:
                    dve.wait_ge(ds_S, 2 * g)
                for c in range(2):
                    for b2 in range(2):
                        r = slice(c * MHD, (c + 1) * MHD)
                        x = c * 64 + b2 * DS
                        ins = nc.vector.tensor_copy(qpad[r, b2, :].rearrange("p (h n) -> p h n", n=136)[:, :, x:x + DS],
                                                    qnew[r, :, (2 * g + b2) * DS:(2 * g + b2 + 1) * DS])
                        if c + b2 < 2:
                            link(ins)
                ins.then_inc(qp_ready, 1)
                for i in SUB_HEADS[g - 1] if g else ():
                    output_var(i)
                if g:
                    dve.wait_ge(ds_pv, g)
                link(nc.vector.memset(apad[:, :, :, :, :], 0.0))
                settle()
                dve.wait_ge(ds_S, 2 * g + 2)
                new = psX[:, 0, PAST:NKEY]
                link(nc.vector.tensor_tensor(new, new, cst[:, C_NEW + g * NSA:C_NEW + (g + 1) * NSA], ALU.add))
                settle()
                link(nc.vector.tensor_reduce(stat[:, 0, 0:1], psX[:, 0, 0:NKEY], AX.X, ALU.max))
                settle()
                nc.vector.tensor_scalar(stat[:, 0, 2:3], stat[:, 0, 0:1], -ISQ, None, ALU.mult).then_inc(ds_nb, 1)
                dve.wait_ge(ds_exp, g + 1)
                softmax_weights(stat[:, 0, 4:5], stat[:, 0, 6:7])
                nc.vector.tensor_scalar(cs[:, :], cst[:, C_FOLD:C_FOLD + 48], stat[:, 0, 6:7], lamt[:, 6:7],
                                        ALU.mult, ALU.mult).then_inc(ds_p, 1)
                dve.wait_ge(ds_A, g + 1)
                folded = psX[:, 1, 0:96].rearrange("p (k h b t) -> p k h b t", k=PAGES, h=H, t=DS)
                for b2 in range(2):
                    x = (2 * g + b2) * DS
                    link(nc.vector.tensor_copy(apad[:, b2, :, :, x:x + DS], folded[:, :, :, b2, :]))
                nc.vector.tensor_copy(anew[:, :, 2 * g * DS:2 * (g + 1) * DS],
                                      psX[0:NSA, 1, 96:144].rearrange("p (h n) -> p h n", h=H)).then_inc(ds_a, 1)
            dve.wait_ge(ds_rT, 1)
            nc.vector.tensor_copy(od[:, :, NPR:T], psX[:, 1, 0:H * NSA].rearrange("p (h n) -> p h n", h=H)).then_inc(ds_o, 1)
            output_var(H - 1)
            output_var(H)
            nrt[0] += 1
            dve.wait_ge(sd_ready, nrt[0])
            link(nc.vector.reciprocal(small[:, 2, :], small[:, 1, :]))
            settle()
            link(nc.vector.tensor_scalar(small[:, 2, :], small[:, 2, :], 1.0 - LAM_INIT, None, ALU.mult))
            settle()

            def output_normed(h):
                r_ = (t1, rr)[h % 2]
                if h >= 2:
                    dve.wait_ge(cm_lo, 8 + h - 1)
                link(nc.vector.transpose(r_[:, :], small[:, 2, h * w:(h + 1) * w].unsqueeze(2).broadcast_to((P, w, 32))))
                settle()
                nc.vector.scalar_tensor_tensor(out=qf[:, h % 2, :], in0=od[:, h, :], scalar=pcol("subln"), in1=r_[:, :],
                                               op0=ALU.mult, op1=ALU.mult).then_inc(ln_n, 1)

            def output_lo(h):
                dve.wait_ge(cm_hi, 8 + h + 1)
                nc.vector.tensor_tensor(xb_lo[:, h, :], qf[:, h % 2, :], xb_hi[:, h, :].bitcast(F32), ALU.subtract
                                        ).then_inc(cm_lo, 1)

            pad_queries(1, mq2)
            mem_attention(1, mT2)
            mem_sample(1, mT2)
            mix_lo(1, mT2)
            out_section(1, "n3", 3)
            ffn(1)

        @block.gpsimd
        def _(pool):
            pool.memset(ones[:, :], 1.0).then_inc(zeroed, 1)
            pool.memset(uext[:, :, 0:TAPS - 1], 0.0).then_inc(zeroed, 1)
            pool.dma_start(ptab[:, :], a["page_table"].rearrange("(o b) p -> o (b p)", o=1)).then_inc(ld_pt, 16)
            pool.dma_start(a["s_conv_a"][0][:, 0:TAPS - 1 - DS, :], a["state_conv_a"][0][:, DS:, :]).then_inc(st_misc, 16)

            def add_squares(norm, chunks=KD):
                k = SQ[norm]
                if k:
                    pool.wait_ge(sq_used, k)
                pool.wait_ge(sq_ready, k + 2)
                nc.gpsimd.tensor_tensor(total[:, :], sqt[:, 0, :], sqt[:, 1, :], ALU.add).then_inc(sq_used, 2)
                for c in range(2, chunks - 1):
                    pool.wait_ge(sq_ready, k + c + 1)
                    pool.wait_ge(sq_used, k + c)
                    ins = nc.gpsimd.tensor_tensor(total[:, :], total[:, :], sqt[:, c % 2, :], ALU.add)
                    ins.then_inc(sq_used, 1)

            def cache_rows(which, l, b_):
                src = a[which][l][b_].rearrange("(m p) h d -> p m (h d)", p=P)
                return mcache[:, b_, :].rearrange("p (m n) -> p m n", n=MW), src

            def mem_cache_k(l):
                for b_ in range(DB):
                    pool.dma_start(*cache_rows("cache_mem_k", l, b_)).then_inc(mc_k, 16)

            def mem_cache_v(l):
                for b_ in range(DB):
                    pool.wait_ge(ms_T, DB * l + b_ + 1)
                    pool.dma_start(*cache_rows("cache_mem_v", l, b_)).then_inc(mc_v, 16)

            add_squares("n0")
            pool.wait_ge(mm_done, S_MEM)
            pool.memset(qm[:, :, :], 0.0).then_inc(qm_zero, 1)
            mem_cache_k(0)

            def memory_values_out(l):
                pool.wait_ge(acc_free, S_MEM + 4 * l + 4)
                pool.dma_start(a["p_mem_v"][l][0].rearrange("(m p) h d -> p m (h d)", p=P), memv[:, l, :, :]).then_inc(st_mv, 16)

            def memory_keys_out(l):
                pool.wait_ge(mk_c, l + 1)
                pool.dma_start(a["p_mem_k"][l][0].rearrange("(m p) h d -> p m (h d)", p=P), mkn[:, :, :]).then_inc(st_mk, 16)

            memory_values_out(0)
            memory_keys_out(0)
            pool.wait_ge(qk_done, 6)
            for j in range(1, CC):
                pool.wait_ge(conv_step, max(conv_final[j], conv_final[0]))
                pool.wait_ge(taps_summed, j + 1)
                if j > 1:
                    pool.wait_ge(conv_total, j - 1)
                nc.gpsimd.tensor_tensor(total[:, :], convt[:, 0, :] if j == 1 else total[:, :], convt[:, j, :], ALU.add
                                        ).then_inc(conv_total, 1)
            memory_values_out(1)
            memory_keys_out(1)
            mem_cache_v(0)
            pool.wait_ge(ln_mean, 1)
            add_squares("ln", CC)
            pool.wait_ge(ct_c, 3)
            pool.dma_start(a["p_conv_a"][0][0], ctail[0:TAPS - 1, 0, :]).then_inc(st_cs, 16)
            pool.dma_start(a["s_conv_a"][0][:, TAPS - 1 - DS:, :], ctail[:, 1, :]).then_inc(st_cs, 16)

            add_squares("n1")

            def ffn_tail(l):
                pool.wait_ge(ft_c, l + 1)
                pool.dma_start(a["s_ffn_conv"][l].rearrange("b r (j n) -> (b r j) n", n=P).rearrange("(g p) n -> p g n", g=4),
                               fout[0:4 * FC, 0:4, :]).then_inc(st_ft, 16)
                pool.dma_start(a["p_ffn_conv"][l][0].rearrange("r (j n) -> (r j) n", n=P), fout[0:2 * FC, 4, :]).then_inc(st_ft, 16)

            add_squares("n2")
            ffn_tail(0)
            for h in range(H):
                pool.wait_ge(acc_free, S_B + 3 * h + 2)
                pool.dma_start(a["p_v"][0].rearrange("(i p) h d -> p i h d", p=P)[:, :, h, :], vnat[:, h % 2, :, :]
                               ).then_inc(st_v[h % 2], 16)
            pool.dma_start(a["s_v"].rearrange("b t h d -> (b t) (h d)"), vnew[:, :, :].rearrange("p h d -> p (h d)")
                           ).then_inc(st_misc, 16)
            pool.wait_ge(mm_done, S_B + 20)
            pool.memset(qpad[:, :, :], 0.0).then_inc(qp_zero, 1)
            pool.memset(qm[:, :, :], 0.0).then_inc(qm_zero, 1)
            pool.wait_ge(ld_pt, 16)

            def pages(dst, cache, b_, done):
                for pg in range(PAGES):
                    page = pool.value_load(ptab[0:1, b_ * PAGES + pg:b_ * PAGES + pg + 1], min_val=0,
                                           max_val=a[cache].shape[0] - 1)
                    pool.dma_start(dst[:, b_ % 2, pg, :],
                                   a[cache][bass.ds(page, 1)].rearrange("o p h d -> (o p) (h d)")).then_inc(done[b_ % 2], 16)

            for b_ in range(2):
                pages(kpg, "cache_k", b_, kp_ld)
                pages(vpg, "cache_v", b_, vp_ld)
            pool.wait_ge(kn_c, H + 1)
            pool.dma_start(a["p_k"][0].rearrange("(i p) h d -> p i (h d)", p=P), knat[:, :, :]).then_inc(st_kn, 16)
            pool.dma_start(a["s_k"].rearrange("b t h d -> (b t) (h d)"), knsam[:, :]).then_inc(st_kn, 16)
            for b_ in range(2, DB):
                pool.wait_ge(ds_T, 3 * (b_ - 2) + 3)
                pages(kpg, "cache_k", b_, kp_ld)
                if b_ == 2:
                    pool.wait_ge(st_kn, 32)
                    mem_cache_k(1)
                if b_ % 2:
                    pool.wait_ge(ds_pv, b_ // 2)
                    for b2 in (b_ - 1, b_):
                        pages(vpg, "cache_v", b2, vp_ld)
            mem_cache_v(1)
            add_squares("n3")
            ffn_tail(1)
            for m in range(KD - 2):
                pool.wait_ge(y_c, m + 1)
                pool.dma_start(a["y_prompt"][0].rearrange("(i p) n -> p i n", p=P)[:, :, m * P:(m + 1) * P],
                               ynat[:, m % 2, :, :]).then_inc(st_y[m % 2], 16)
            for s_, n in ((st_mk, 32), (st_mv, 32), (st_misc, 32), (st_ys, 48), (st_y[0], 48), (st_y[1], 48), (st_kn, 32), (st_ft, 64),
                          (st_cs, 32), (st_v[0], 48), (st_v[1], 48)):
                pool.wait_ge(s_, n)


_OUTS = {
    "y_prompt": (1, NPR, D), "y_sample": (DB, DS, D), "p_mem_k": (2, 1, MEM, MH, MHD), "p_mem_v": (2, 1, MEM, MH, MHD),
    "p_conv_a": (1, 1, TAPS - 1, CA), "p_ffn_conv": (2, 1, FTAPS - 1, FF), "p_k": (1, NPR, H, VD), "p_v": (1, NPR, H, VD),
    "s_conv_a": (1, DB, TAPS - 1, CA), "s_ffn_conv": (2, DB, FTAPS - 1, FF), "s_k": (DB, DS, H, VD), "s_v": (DB, DS, H, VD),
}


def constants():
    import numpy as np

    c = np.zeros((P, C_ALL), np.float32)
    r = np.arange(P)
    c[:, C_ID:C_ID + P] = r[:, None] == r[None, :]
    c[:, C_BLK:C_BLK + P] = r[:, None] // MHD == r[None, :] // MHD
    c[:, C_MASK:C_MASK + P] = np.where(r[None, :] <= r[:, None], 0.0, -1e30)
    for g in range(DB // 2):
        for row in range(P):
            j = row % 64
            if j < 48:
                b_, t = 2 * g + j // DS % 2, j % DS
                for col in range(NSA):
                    if col // DS != b_ or col % DS > t:
                        c[row, C_NEW + g * NSA + col] = -1e30
    for j in range(48):
        c[j, C_FOLD + j] = c[64 + j, C_FOLD + j] = 1.0
    return c


def kernel(**inputs):
    import numpy as np
    import concourse.bacc as bacc
    from concourse.bass_utils import run_bass_kernel_spmd

    nc = bacc.Bacc("TRN2", target_bir_lowering=False, num_devices=1)
    arrays, aps = {}, {}
    for name, x in list(inputs.items()) + [("consts", constants())]:
        x = np.ascontiguousarray(x)
        arrays[f"in_{name}"] = x
        aps[name] = nc.dram_tensor(f"in_{name}", x.shape, mybir.dt.from_np(x.dtype), kind="ExternalInput").ap()
    for name, shape in _OUTS.items():
        aps[name] = nc.dram_tensor(f"out_{name}", shape, F32, kind="ExternalOutput").ap()
    build(nc, aps)
    r = run_bass_kernel_spmd(nc, [arrays], core_ids=[0])
    return tuple(r.results[0][f"out_{name}"] for name in _OUTS)
```
